# Optimizing a Trainium2 kernel written in Bass

```python
import math
import jax, jax.numpy as jnp
from jax import lax
import numpy as np

D_MODEL = 1024
BATCH = 1
SEQ = 256
DEPTH = 2

N_A = DEPTH // 2
N_B = DEPTH - N_A
FOX_HEADS = 16
FOX_HEAD_DIM = D_MODEL // FOX_HEADS
DIFF_HEADS = 8
DIFF_HEAD_DIM = D_MODEL // (2 * DIFF_HEADS)
DIFF_V_DIM = 2 * DIFF_HEAD_DIM
N_EXPERTS = 16
N_GROUPS = 4
EXPERTS_PER_GROUP = N_EXPERTS // N_GROUPS
TOP_K = 2
D_EXPERT = 512
Q_BLOCK = 128
DEEPNORM_ALPHA = (2 * DEPTH) ** 0.25
DEEPNORM_BETA = (8 * DEPTH) ** -0.25
LN_EPS = 1e-5
NEG_INF = -1e30

kernel_name = "yoco_fox_diffattn_grouped_moe_deepnorm_adaln"

def layer_norm(x, g, b):
    xf = x.astype(jnp.float32)
    mu = jnp.mean(xf, axis=-1, keepdims=True)
    var = jnp.mean(jnp.square(xf - mu), axis=-1, keepdims=True)
    y = (xf - mu) * lax.rsqrt(var + LN_EPS)
    return (y * g.astype(jnp.float32) + b.astype(jnp.float32)).astype(x.dtype)

def ada_params(c, w, b):
    return jax.nn.silu(c) @ w + b

def modulate(x, shift, scale):
    return x * (1.0 + scale[:, None, :]) + shift[:, None, :]

def post_norm_residual(x, y, gate, g, b):
    return layer_norm(DEEPNORM_ALPHA * x + (1.0 + gate[:, None, :]) * y, g, b)

def fox_attention(q, k, v, logf):
    B, H, S, Dh = q.shape
    nblk = S // Q_BLOCK
    f32 = jnp.float32
    cum = jnp.cumsum(logf.astype(f32), axis=-1)
    kf = k.astype(f32)
    vf = v.astype(f32)
    qb = (q.astype(f32) * (Dh ** -0.5)).reshape(B, H, nblk, Q_BLOCK, Dh).transpose(2, 0, 1, 3, 4)
    cb = cum.reshape(B, H, nblk, Q_BLOCK).transpose(2, 0, 1, 3)
    k_pos = jnp.arange(S)

    def one_block(args):
        i, q_i, c_i = args
        q_pos = i * Q_BLOCK + jnp.arange(Q_BLOCK)
        logits = jnp.einsum('bhqd,bhkd->bhqk', q_i, kf) + c_i[..., :, None] - cum[..., None, :]
        logits = jnp.where(k_pos[None, :] <= q_pos[:, None], logits, NEG_INF)
        p = jax.nn.softmax(logits, axis=-1)
        return jnp.einsum('bhqk,bhkd->bhqd', p, vf)

    out = lax.map(one_block, (jnp.arange(nblk), qb, cb))
    return out.transpose(1, 2, 0, 3, 4).reshape(B, H, S, Dh).astype(q.dtype)

def diff_attention(q1, q2, k1, k2, v, lam):
    B, H, S, d = q1.shape
    nblk = S // Q_BLOCK
    f32 = jnp.float32
    slopes = jnp.exp2(-8.0 * jnp.arange(1, H + 1, dtype=f32) / H)
    scale = d ** -0.5
    k1f, k2f, vf = k1.astype(f32), k2.astype(f32), v.astype(f32)
    q1b = (q1.astype(f32) * scale).reshape(B, H, nblk, Q_BLOCK, d).transpose(2, 0, 1, 3, 4)
    q2b = (q2.astype(f32) * scale).reshape(B, H, nblk, Q_BLOCK, d).transpose(2, 0, 1, 3, 4)
    k_pos = jnp.arange(S)

    def one_block(args):
        i, q1_i, q2_i = args
        q_pos = i * Q_BLOCK + jnp.arange(Q_BLOCK)
        dist = (q_pos[:, None] - k_pos[None, :]).astype(f32)
        bias = jnp.where(dist >= 0, -slopes[:, None, None] * dist, NEG_INF)
        p1 = jax.nn.softmax(jnp.einsum('bhqd,bhkd->bhqk', q1_i, k1f) + bias, axis=-1)
        p2 = jax.nn.softmax(jnp.einsum('bhqd,bhkd->bhqk', q2_i, k2f) + bias, axis=-1)
        return jnp.einsum('bhqk,bhkd->bhqd', p1 - lam * p2, vf)

    out = lax.map(one_block, (jnp.arange(nblk), q1b, q2b))
    return out.transpose(1, 2, 0, 3, 4).reshape(B, H, S, 2 * d)

def grouped_moe(h, router_w, router_b, w_gate, w_up, w_down):
    B, S, D = h.shape
    t = h.reshape(-1, D)
    T = t.shape[0]
    probs = jax.nn.softmax((t @ router_w).astype(jnp.float32), axis=-1)
    sel = probs + router_b.astype(jnp.float32)[None, :]
    grp = sel.reshape(T, N_GROUPS, EXPERTS_PER_GROUP)
    grp_score = jnp.sum(lax.top_k(grp, TOP_K)[0], axis=-1)
    g_idx = jnp.argmax(grp_score, axis=-1)
    in_grp = jnp.take_along_axis(grp, g_idx[:, None, None], axis=1)[:, 0]
    _, local = lax.top_k(in_grp, TOP_K)
    expert_idx = g_idx[:, None] * EXPERTS_PER_GROUP + local
    w = jnp.take_along_axis(probs, expert_idx, axis=-1)
    w = w / jnp.sum(w, axis=-1, keepdims=True)
    gates = jnp.sum(jax.nn.one_hot(expert_idx, N_EXPERTS, dtype=jnp.float32) * w[..., None], axis=1)
    gates = gates.astype(t.dtype)
    out = jnp.zeros_like(t)
    for e in range(N_EXPERTS):
        a = jax.nn.silu(t @ w_gate[e]) * (t @ w_up[e])
        out = out + gates[:, e:e + 1] * (a @ w_down[e])
    return out.reshape(B, S, D)

def setup_inputs(seed: int = 0) -> dict:
    key = jax.random.key(seed)
    keys = jax.random.split(key, 32)
    f32 = jnp.float32
    D = D_MODEL
    kd = DIFF_HEADS * DIFF_HEAD_DIM

    def normal(i, shape, scale):
        return scale * jax.random.normal(keys[i], shape, f32)

    x = normal(0, (BATCH, SEQ, D), 1.0)
    c = normal(1, (BATCH, D), 1.0)
    ada_w = normal(2, (DEPTH, D, 6 * D), 0.5 * D ** -0.5)
    ada_b = normal(3, (DEPTH, 6 * D), 0.02)
    ln_attn_g = 1.0 + normal(4, (DEPTH, D), 0.02)
    ln_attn_b = normal(5, (DEPTH, D), 0.02)
    ln_ffn_g = 1.0 + normal(6, (DEPTH, D), 0.02)
    ln_ffn_b = normal(7, (DEPTH, D), 0.02)
    fox_w_in = jnp.concatenate([
        normal(8, (N_A, D, 2 * D), D ** -0.5),
        normal(9, (N_A, D, D), DEEPNORM_BETA * D ** -0.5),
        normal(10, (N_A, D, FOX_HEADS), D ** -0.5),
    ], axis=-1)
    fox_b_f = 3.0 + normal(11, (N_A, FOX_HEADS), 1.0)
    fox_w_o = normal(12, (N_A, D, D), DEEPNORM_BETA * D ** -0.5)
    kv_ada_w = normal(13, (D, 2 * D), 0.5 * D ** -0.5)
    kv_ada_b = normal(14, (2 * D,), 0.02)
    kv_w = jnp.concatenate([
        normal(15, (D, 2 * kd), D ** -0.5),
        normal(16, (D, DIFF_HEADS * DIFF_V_DIM), DEEPNORM_BETA * D ** -0.5),
    ], axis=-1)
    diff_w_q = normal(17, (N_B, D, 2 * kd), D ** -0.5)
    diff_lambda = normal(18, (N_B, 4, DIFF_HEAD_DIM), 0.1)
    diff_norm_g = 1.0 + normal(19, (N_B, DIFF_V_DIM), 0.02)
    diff_w_o = normal(20, (N_B, DIFF_HEADS * DIFF_V_DIM, D), DEEPNORM_BETA * D ** -0.5)
    router_w = normal(21, (D, N_EXPERTS), D ** -0.5)
    router_b = normal(22, (N_EXPERTS,), 0.01)
    moe_w_gate = normal(23, (DEPTH, N_EXPERTS, D, D_EXPERT), D ** -0.5)
    moe_w_up = normal(24, (DEPTH, N_EXPERTS, D, D_EXPERT), D ** -0.5)
    moe_w_down = normal(25, (DEPTH, N_EXPERTS, D_EXPERT, D), DEEPNORM_BETA * D_EXPERT ** -0.5)
    return {"x": x, "c": c, "ada_w": ada_w, "ada_b": ada_b,
            "ln_attn_g": ln_attn_g, "ln_attn_b": ln_attn_b, "ln_ffn_g": ln_ffn_g, "ln_ffn_b": ln_ffn_b,
            "fox_w_in": fox_w_in, "fox_b_f": fox_b_f, "fox_w_o": fox_w_o,
            "kv_ada_w": kv_ada_w, "kv_ada_b": kv_ada_b, "kv_w": kv_w,
            "diff_w_q": diff_w_q, "diff_lambda": diff_lambda, "diff_norm_g": diff_norm_g, "diff_w_o": diff_w_o,
            "router_w": router_w, "router_b": router_b,
            "moe_w_gate": moe_w_gate, "moe_w_up": moe_w_up, "moe_w_down": moe_w_down}

def reference(x, c, ada_w, ada_b, ln_attn_g, ln_attn_b, ln_ffn_g, ln_ffn_b,
              fox_w_in, fox_b_f, fox_w_o, kv_ada_w, kv_ada_b, kv_w,
              diff_w_q, diff_lambda, diff_norm_g, diff_w_o,
              router_w, router_b, moe_w_gate, moe_w_up, moe_w_down):
    B, S, D = x.shape
    f32 = jnp.float32
    H_A, dh = FOX_HEADS, FOX_HEAD_DIM
    H_B, d = DIFF_HEADS, DIFF_HEAD_DIM
    kd = H_B * d

    def to_heads(t, h):
        return t.reshape(B, S, h, -1).transpose(0, 2, 1, 3)

    def from_heads(t):
        return t.transpose(0, 2, 1, 3).reshape(B, S, -1)

    k1 = k2 = v_sh = None
    for l in range(DEPTH):
        mod = ada_params(c, ada_w[l], ada_b[l])
        sh_a, sc_a, g_a, sh_f, sc_f, g_f = jnp.split(mod, 6, axis=-1)

        if l < N_A:
            i = l
            h = modulate(x, sh_a, sc_a)
            proj = h @ fox_w_in[i]
            q = to_heads(proj[..., :D], H_A)
            k = to_heads(proj[..., D:2 * D], H_A)
            v = to_heads(proj[..., 2 * D:3 * D], H_A)
            logf = jax.nn.log_sigmoid((proj[..., 3 * D:] + fox_b_f[i]).astype(f32))
            o = fox_attention(q, k, v, logf.transpose(0, 2, 1))
            y = from_heads(o) @ fox_w_o[i]
        else:
            if l == N_A:
                kv_sh, kv_sc = jnp.split(ada_params(c, kv_ada_w, kv_ada_b), 2, axis=-1)
                hk = modulate(x, kv_sh, kv_sc)
                kv = hk @ kv_w
                kk = kv[..., :2 * kd].reshape(B, S, H_B, 2, d)
                k1 = kk[..., 0, :].transpose(0, 2, 1, 3)
                k2 = kk[..., 1, :].transpose(0, 2, 1, 3)
                v_sh = to_heads(kv[..., 2 * kd:], H_B)
            j = l - N_A
            lam_init = 0.8 - 0.6 * math.exp(-0.3 * l)
            lp = diff_lambda[j].astype(f32)
            lam = jnp.exp(jnp.sum(lp[0] * lp[1])) - jnp.exp(jnp.sum(lp[2] * lp[3])) + lam_init
            h = modulate(x, sh_a, sc_a)
            qq = (h @ diff_w_q[j]).reshape(B, S, H_B, 2, d)
            q1 = qq[..., 0, :].transpose(0, 2, 1, 3)
            q2 = qq[..., 1, :].transpose(0, 2, 1, 3)
            o = diff_attention(q1, q2, k1, k2, v_sh, lam)
            o = o * lax.rsqrt(jnp.mean(jnp.square(o), axis=-1, keepdims=True) + LN_EPS)
            o = o * diff_norm_g[j].astype(f32) * (1.0 - lam_init)
            y = from_heads(o.astype(x.dtype)) @ diff_w_o[j]

        x = post_norm_residual(x, y, g_a, ln_attn_g[l], ln_attn_b[l])

        h = modulate(x, sh_f, sc_f)
        m = grouped_moe(h, router_w, router_b, moe_w_gate[l], moe_w_up[l], moe_w_down[l])
        x = post_norm_residual(x, m, g_f, ln_ffn_g[l], ln_ffn_b[l])
    return x


_drawn_inputs = setup_inputs


def setup_inputs(seed=0):
    import zlib

    import numpy as np

    out = dict(_drawn_inputs(seed))
    spreads = {}
    factors = {'kv_ada_b': 3.612, 'diff_norm_g': 8.0}
    for name, (base, spread) in spreads.items():
        noise = np.random.default_rng([zlib.crc32(name.encode()), seed]).standard_normal(out[name].shape)
        drawn = base * np.exp(spread * noise) if base else spread * noise
        out[name] = __import__('jax').numpy.asarray(drawn.astype(out[name].dtype))
    for name, factor in factors.items():
        out[name] = (out[name] * factor).astype(out[name].dtype)
    return out
```

```python
import math
from contextlib import ExitStack

import concourse.bass as bass
from concourse import mybir

ALU = mybir.AluOpType
ACT = mybir.ActivationFunctionType
AX = mybir.AxisListType
F32 = mybir.dt.float32
I32 = mybir.dt.int32

P = 128
RING = 6
CAP = 64
BIG = 1e30
FAR = 1e33


def build(nc, x, c, ada_w, ada_b, ln_attn_g, ln_attn_b, ln_ffn_g, ln_ffn_b, fox_w_in, fox_b_f, fox_w_o,
          kv_ada_w, kv_ada_b, kv_w, diff_w_q, diff_lambda, diff_norm_g, diff_w_o,
          router_w, router_b, moe_w_gate, moe_w_up, moe_w_down, out):
    DEPTH, D, _ = ada_w.shape
    S = x.shape[1]
    NE = router_w.shape[1]
    FE = moe_w_gate.shape[3]
    HF = fox_b_f.shape[1]
    HD = D // (diff_norm_g.shape[1])
    KC = D // P
    NB = S // P
    NG, EG = 4, 4
    PAIRS = NE // 2
    ALPHA = (2 * DEPTH) ** 0.25
    EPS = 1e-5
    LAM_INIT = 0.8 - 0.6 * math.exp(-0.3 * 1)
    ROUNDS = S // CAP - 1
    QSCALE = 0.125
    assert (DEPTH, D, S, NE, FE, HF, HD) == (2, 1024, 256, 16, 512, 16, 8)

    ada_dram = [ada_w[0], kv_ada_w, ada_w[1]]
    pieces = []

    def ada_pieces(which, group):
        first = len(pieces)
        for b in range(4):
            col = 2048 * group + 512 * b
            pieces.append(ada_dram[which][:, col:col + 512].rearrange("(k p) n -> p k n", p=P))
        return first

    def col_pieces(w, lo, n):
        first = len(pieces)
        for b in range(n):
            pieces.append(w[:, lo + 512 * b:lo + 512 * b + 512].rearrange("(k p) n -> p k n", p=P))
        return first

    N_ADA = {}
    N_ADA[0] = ada_pieces(0, 0)
    N_FOXQK = col_pieces(fox_w_in[0], 0, 4)
    N_FOXV = col_pieces(fox_w_in[0], 2048, 2)
    N_ADA[1] = ada_pieces(0, 1)
    N_ADA[2] = ada_pieces(0, 2)
    N_WO = [col_pieces(fox_w_o[0], 0, 2), None]
    N_MOE = [len(pieces), None]
    pieces += [None] * (3 * NE)
    N_ADA[3] = ada_pieces(1, 0)
    N_ADA[4] = ada_pieces(2, 0)
    N_KVK = col_pieces(kv_w, 0, 2)
    N_KVV = col_pieces(kv_w, 1024, 2)
    N_WQ = col_pieces(diff_w_q[0], 0, 2)
    N_ADA[5] = ada_pieces(2, 1)
    N_ADA[6] = ada_pieces(2, 2)
    N_WO[1] = col_pieces(diff_w_o[0], 0, 2)
    N_MOE[1] = len(pieces)
    pieces += [None] * (3 * NE)

    def ada_row(layer_first, v):
        return layer_first + v // 2, 2 * (v % 2)
    ROW = {}
    for l, g0 in ((0, 0), (1, 4)):
        for v, name in enumerate(("sh_a", "sc_a", "g_a", "sh_f", "sc_f", "g_f")):
            ROW[name, l] = ada_row(g0, v)
        ROW["ln_a_g", l] = (7 + 2 * l, 0)
        ROW["ln_a_b", l] = (7 + 2 * l, 2)
        ROW["ln_f_g", l] = (8 + 2 * l, 0)
        ROW["ln_f_b", l] = (8 + 2 * l, 2)
    ROW["kv_sh"] = (3, 0)
    ROW["kv_sc"] = (3, 2)
    MODS = [(ROW["sc_a", 0], ROW["sh_a", 0]), (ROW["sc_f", 0], ROW["sh_f", 0]), (ROW["kv_sc"], ROW["kv_sh"]),
            (ROW["sc_a", 1], ROW["sh_a", 1]), (ROW["sc_f", 1], ROW["sh_f", 1])]

    with ExitStack() as ctx:
        def sb(name, shape, dt=F32):
            return ctx.enter_context(nc.sbuf_tensor(name, shape, dt))

        def sem(name):
            return ctx.enter_context(nc.semaphore(name))

        ring = sb("ring", [P, RING, 4096])
        xres = sb("xres", [P, NB, D])
        h = sb("h", [P, NB, D])
        hT = sb("hT", [P, KC, S])
        rows = sb("rows", [P, 11, 512])
        gbc = sb("gbc", [P, D])
        ident = sb("ident", [P, P])
        ones = sb("ones", [P, P])
        before = sb("before", [P, P])
        maskf = sb("maskf", [P, 3 * P])
        dist = sb("dist", [P, 3 * P])
        lane = sb("lane", [P, CAP])
        tri4 = sb("tri4", [P, EG, EG])
        ccol = sb("ccol", [P, KC])
        csig = sb("csig", [P, KC])
        crep = sb("crep", [P, KC, 32])
        wf = sb("wf", [P, KC, HF])
        bf = sb("bf", [HF, 1])
        rw = sb("rw", [P, KC, NE])
        rb = sb("rb", [P, NE])
        lamin = sb("lamin", [P, 4, 64])
        lamt = sb("lamt", [P, 64])
        lam2 = sb("lam2", [P, 4])
        normg = sb("normg", [P, P])
        st = sb("st", [P, 16])
        mhalf = sb("mhalf", [P, 16])
        tabn = sb("tabn", [1, NE], I32)
        tabb = sb("tabb", [1, NE], I32)
        rt = sb("rt", [P, 12, NB * NE])
        rg = sb("rg", [P, 6, 2 * 2 * 8])
        rc = sb("rc", [P, 3, NB * NG * EG * EG])
        gate = sb("gate", [P, NB, NE + 2])
        pos = sb("pos", [P, NB, NE + 2])
        cnt = sb("cnt", [1, 6, NE])
        arena = sb("arena", [P, 11264])
        ps = ctx.enter_context(nc.psum_tensor("ps", [P, 8, 512], F32))

        taken = [0]

        def part(rowcount, *shape):
            n = math.prod(shape)
            a = arena[0:rowcount, taken[0]:taken[0] + n]
            taken[0] += n
            assert taken[0] <= 11264
            names = "abc"[:len(shape)]
            if len(shape) == 1:
                return a
            return a.rearrange(f"p ({' '.join(names)}) -> p {' '.join(names)}",
                               **{names[i]: shape[i] for i in range(1, len(shape))})

        qT = part(P, KC, S)
        kT = part(P, 2 * KC, S)
        v = part(P, NB, D)
        oT = hT
        lg = part(P, 2, 3 * P)
        pT = part(P, 2, 3 * P)
        ncum = part(P, 3 * P)
        fz = part(HF, 4, S)
        negm = part(P, 2, 2)
        rs = part(P, 2, 2)
        rr = part(P, 2, 2)
        ss = part(P, 4, 2 * HD)
        taken[0] = 0
        xg = part(P, D)
        xT = part(P, KC, 2 * CAP)
        gu = part(P, 2, FE)
        sg = part(P, 2, 4, CAP)
        tg = part(P, 2, 4, CAP)
        aT = part(P, 2, 4 * CAP)
        y = part(P, D)
        pick = part(P, NB, 2 * CAP)
        put = part(P, NB, 2 * CAP)
        putT = part(P, S)
        opos = part(P, 2, NB)
        opick = part(P, NB, CAP)
        oput = part(P, NB, CAP)
        ox = part(P, FE)
        oxT = part(P, 4, 2 * CAP)
        osg = part(P, 4, CAP)
        oaT = part(P, 4 * CAP)
        oy = part(P, D)
        oputT = part(P, S)

        full = [sem(f"full{i}") for i in range(RING)]
        used = [sem(f"used{i}") for i in range(RING)]
        x_in = sem("x_in")
        c_in = sem("c_in")
        small_in = sem("small_in")
        consts = sem("consts")
        csil = sem("csil")
        rows_zero = sem("rows_zero")
        rows_one = sem("rows_one")
        mod_row = sem("mod_row")
        bc_mm = sem("bc_mm")
        h_ready = sem("h_ready")
        ht_mm = sem("ht_mm")
        ht_ready = sem("ht_ready")
        pj_mm = sem("pj_mm")
        pj_ev = [sem("pj_ev_act"), sem("pj_ev_dve")]
        lam_r = sem("lam_r")
        f_steps = sem("f_steps")
        f_act = sem("f_act")
        s_mm = sem("s_mm")
        s_ev = sem("s_ev")
        mx = sem("mx")
        ex = sem("ex")
        pn = sem("pn")
        pt_mm = sem("pt_mm")
        pt_ev = sem("pt_ev")
        pv_mm = sem("pv_mm")
        o_ev = sem("o_ev")
        o_rms = sem("o_rms")
        o_pow = sem("o_pow")
        o_nrm = sem("o_nrm")
        ot_mm = sem("ot_mm")
        ot_ev = sem("ot_ev")
        g_ev = sem("g_ev")
        r_sum = sem("r_sum")
        r_sq = sem("r_sq")
        r_std = sem("r_std")
        x_ready = sem("x_ready")
        rt_mm = sem("rt_mm")
        rt_dve = sem("rt_dve")
        rt_act = sem("rt_act")
        rt_mask = sem("rt_mask")
        tab = sem("tab")
        dch = sem("dch")
        pch = sem("pch")
        ach = sem("ach")
        picked = sem("picked")
        putted = sem("putted")
        ga_mm = sem("ga_mm")
        xg_ev = sem("xg_ev")
        tx_mm = sem("tx_mm")
        xt_ev = sem("xt_ev")
        gu_ev = [sem("gu_ev_a"), sem("gu_ev_b")]
        tg_mm = [sem("tg_mm_a"), sem("tg_mm_b")]
        sg_r = [sem("sg_r_a"), sem("sg_r_b")]
        tg_r = [sem("tg_r_a"), sem("tg_r_b")]
        at_r = [sem("at_r_a"), sem("at_r_b")]
        y_ev = [sem("y_ev_a"), sem("y_ev_b")]
        tp_mm = sem("tp_mm")
        tp_ev = sem("tp_ev")
        sc_mm = sem("sc_mm")
        z_mm = sem("z_mm")
        o_pe = sem("o_pe")
        o_act = sem("o_act")
        o_dve = sem("o_dve")
        o_pos = sem("o_pos")
        stored = sem("stored")

        def slot(n):
            return n % RING

        def landed(eng, n, i=None):
            val = 16 * (n // RING + 1)
            eng.wait_ge(full[n % RING], val if i is None else i * 16 + val)

        def spent(eng, n, i=None):
            val = n // RING + 1
            eng.wait_ge(used[n % RING], val if i is None else i + val)

        class Chain:
            def __init__(self, eng, s):
                self.eng, self.sem, self.n = eng, s, 0

            def __call__(self, ins):
                ins.then_inc(self.sem, 1)
                self.n += 1
                self.eng.wait_ge(self.sem, self.n)

        def wcols(n):
            return ring[:, slot(n), :].rearrange("p (k n) -> p k n", k=KC)

        def wdown(n):
            return ring[:, slot(n), :].rearrange("p (k n) -> p k n", k=4)

        def sel(rowno):
            return ident[:, rowno:rowno + 1].broadcast_to([P, P])

        SMALL = 21
        BC_MOD = (1, 4, 7, 8, 11)
        BC_GATE = (2, 5, 9, 12)
        BC_LN = (3, 6, 10, 13)

        UNITS0 = 8 + 8 + 1 + 4
        GATE_UNIT = 16
        pj_done = {}

        def number_units():
            count = [0]

            def unit(u, last_of):
                if last_of is None:
                    count[0] += 1
                    pj_done[u] = ("pj_mm", count[0])
                else:
                    pj_done[u] = ("piece", last_of)
            for u in range(16):
                unit(u, N_FOXQK + u // 4 if u % 4 == 3 else None)
            unit(GATE_UNIT, None)
            for u in range(4):
                unit(GATE_UNIT + 1 + u, N_FOXV + u // 2 if u % 2 else None)
            for u in range(8):
                unit(UNITS0 + u, N_KVK + u // 4 if u % 4 == 3 else None)
            for u in range(4):
                unit(UNITS0 + 8 + u, N_KVV + u // 2 if u % 2 else None)
            for u in range(8):
                unit(UNITS0 + 12 + u, N_WQ + u // 4 if u % 4 == 3 else None)
        number_units()

        def unit_filled(eng, u):
            kind, val = pj_done[u]
            if kind == "pj_mm":
                eng.wait_ge(pj_mm, val)
            else:
                spent(eng, val)

        def pj_even(n):
            return len([u for u in range(0, n, 2) if u != GATE_UNIT])

        def pj_odd(n):
            return n // 2

        def proj_units(l):
            if l == 0:
                us = [(u, "q", qT[:, u, :]) for u in range(8)]
                us += [(8 + u, "k", u) for u in range(8)]
                us += [(GATE_UNIT, "f", None)]
                us += [(GATE_UNIT + 1 + u, "v", v[:, u % 2, 512 * (u // 2):512 * (u // 2) + 512]) for u in range(4)]
                return us
            us = [(UNITS0 + u, "k", u) for u in range(8)]
            us += [(UNITS0 + 8 + u, "v", v[:, u % 2, 512 * (u // 2):512 * (u // 2) + 512]) for u in range(4)]
            us += [(UNITS0 + 12 + u, "q", qT[:, u, :]) for u in range(8)]
            return us

        block = ctx.enter_context(nc.Block())

        @block.sync
        def _(sp):
            def load(n):
                if n >= RING:
                    spent(sp, n - RING)
                sp.dma_start(wpiece(n), pieces[n]).then_inc(full[slot(n)], 16)

            def wpiece(n):
                return wcols(n) if len(pieces[n].shape) == 3 else ring[:, slot(n), :]

            def expert_loads(l):
                n0 = N_MOE[l]
                with sp.Fori(0, PAIRS) as i:
                    for j in range(6):
                        e = i * 2 + j // 3
                        sp.wait_ge(used[slot(n0 + j)], i + (n0 + j - RING) // RING + 1)
                        w = (moe_w_gate, moe_w_up, moe_w_down)[j % 3]
                        src = w[l, bass.ds(e, 1), :, :].rearrange("o (k p) n -> p (o k) n", p=P)
                        dst = (wcols, wcols, wdown)[j % 3](n0 + j)
                        sp.dma_start(dst, src).then_inc(full[slot(n0 + j)], 16)

            for n in range(N_MOE[0]):
                load(n)
            expert_loads(0)
            for n in range(N_MOE[0] + 3 * NE, N_MOE[1]):
                load(n)
            expert_loads(1)
            for b in range(NB):
                sp.wait_ge(x_ready, 3 * NB + b + 1)
                sp.dma_start(out[0, b * P:(b + 1) * P, :], xres[:, b, :]).then_inc(stored, 16)
            sp.wait_ge(stored, 16 * NB)

        @block.gpsimd
        def _(pool):
            link = Chain(pool, pch)
            g = nc.gpsimd
            g.memset(rows[:, :, :], 0.0).then_inc(rows_zero, 1)
            link(g.memset(ident[:, :], 0.0))
            g.affine_select(out=ident[:, :], in_=ident[:, :], compare_op=ALU.not_equal, fill=1.0, base=0,
                            pattern=[[-1, P]], channel_multiplier=1).then_inc(consts, 1)
            link(g.memset(ones[:, :], 1.0))
            g.affine_select(out=before[:, :], in_=ones[:, :], compare_op=ALU.is_ge, fill=0.0, base=-1,
                            pattern=[[1, P]], channel_multiplier=-1).then_inc(consts, 1)
            link(g.memset(tri4[:, :, :], 1.0))
            g.affine_select(out=tri4[:, :, :], in_=tri4[:, :, :], compare_op=ALU.is_ge, fill=0.0, base=-1,
                            pattern=[[1, EG], [-1, EG]], channel_multiplier=0).then_inc(consts, 1)
            link(g.memset(maskf[:, :], 0.0))
            g.affine_select(out=maskf[:, 0:P], in_=maskf[:, 0:P], compare_op=ALU.is_ge, fill=-BIG, base=0,
                            pattern=[[-1, P]], channel_multiplier=1).then_inc(consts, 1)
            g.affine_select(out=maskf[:, 2 * P:], in_=maskf[:, 2 * P:], compare_op=ALU.is_ge, fill=-BIG, base=0,
                            pattern=[[-1, P]], channel_multiplier=1).then_inc(consts, 1)
            for t, base in enumerate((0, P, 0)):
                link(g.iota(dist[:, t * P:(t + 1) * P], pattern=[[-1, P]], base=base, channel_multiplier=1,
                            allow_small_or_imprecise_dtypes=True))
            for t in (0, 2):
                g.affine_select(out=dist[:, t * P:(t + 1) * P], in_=dist[:, t * P:(t + 1) * P],
                                compare_op=ALU.is_ge, fill=FAR, base=0,
                                pattern=[[-1, P]], channel_multiplier=1).then_inc(consts, 1)
            g.iota(lane[:, :], pattern=[[1, CAP]], base=0, channel_multiplier=0,
                   allow_small_or_imprecise_dtypes=True).then_inc(consts, 1)
            g.memset(mhalf[:, :], -0.5).then_inc(consts, 1)

            pool.wait_ge(consts, 9)

            def inv_std(norm):
                for b in range(NB):
                    u = 2 * norm + b
                    pool.wait_ge(r_sq, u + 1)
                    link(g.tensor_scalar(st[:, 6 + b:7 + b], st[:, 4 + b:5 + b], 1.0 / D, EPS, ALU.mult, ALU.add))
                    g.tensor_tensor(st[:, 8 + b:9 + b], st[:, 6 + b:7 + b], mhalf[:, 0:1], ALU.pow).then_inc(r_std, 1)
            inv_std(0)
            inv_std(1)
            pool.wait_ge(o_rms, 1)
            link(g.tensor_scalar(ss[:, 1, :], ss[:, 0, :], 1.0 / P, EPS, ALU.mult, ALU.add))
            g.tensor_tensor(ss[:, 2, :], ss[:, 1, :], mhalf[:, :], ALU.pow).then_inc(o_pow, 1)
            inv_std(2)
            inv_std(3)

        @block.scalar
        def _(act):
            a = nc.scalar
            link = Chain(act, ach)

            act.dma_start(ccol[:, :], c.rearrange("o (k p) -> p (o k)", p=P), allow_slow_non_contiguous=True).then_inc(c_in, 16)
            for b in range(NB):
                act.dma_start(xres[:, b, :], x[0, b * P:(b + 1) * P, :]).then_inc(x_in, 16)
            act.wait_ge(rows_zero, 1)
            for l, g0 in ((0, 0), (1, 4)):
                for gi in range(3):
                    act.dma_start(rows[0:97:32, g0 + gi, :],
                                  ada_b[l, 2048 * gi:2048 * gi + 2048].rearrange("(j n) -> j n", j=4)).then_inc(small_in, 16)
                for gi, (u, w) in enumerate(((ln_attn_g, ln_attn_b), (ln_ffn_g, ln_ffn_b))):
                    for hh, vec in enumerate((u, w)):
                        act.dma_start(rows[64 * hh:64 * hh + 33:32, 7 + 2 * l + gi, :],
                                      vec[l, :].rearrange("(j n) -> j n", j=2)).then_inc(small_in, 16)
            act.dma_start(rows[0:97:32, 3, :], kv_ada_b.rearrange("(j n) -> j n", j=4)).then_inc(small_in, 16)
            act.dma_start(wf[:, :, :], fox_w_in[0][:, 3 * D:3 * D + HF].rearrange("(k p) n -> p k n", p=P)).then_inc(small_in, 16)
            act.dma_start(bf[:, :], fox_b_f[0:1, :].rearrange("o n -> n o"), allow_slow_non_contiguous=True).then_inc(small_in, 16)
            act.dma_start(rw[:, :, :], router_w.rearrange("(k p) n -> p k n", p=P)).then_inc(small_in, 16)
            act.dma_start(rb[:, :], router_b.partition_broadcast(P)).then_inc(small_in, 16)
            act.dma_start(lamin[:, :, :], diff_lambda[0].partition_broadcast(P)).then_inc(small_in, 16)
            act.dma_start(normg[:, :], diff_norm_g[0].partition_broadcast(P)).then_inc(small_in, 16)

            act.wait_ge(c_in, 16)
            a.activation(csig[:, :], ccol[:, :], ACT.Sigmoid).then_inc(csil, 1)

            def turned(m):
                act.wait_ge(ht_mm, m + 1)
                for q in range(2):
                    a.activation(hT[:, 2 * q:2 * q + 2, :].rearrange("p a b -> p (a b)"), ps[:, 4 + q, :],
                                 ACT.Copy).then_inc(ht_ready, 1)

            def unit_out(u, dst, kind):
                if u % 2:
                    return
                unit_filled(act, u)
                if kind == "k":
                    cc = dst
                    link(a.activation(kT[0:64, 2 * cc, :], ps[0:64, u % 4, 0:S], ACT.Copy))
                    a.activation(kT[64:P, 2 * cc + 1, :], ps[64:P, u % 4, 0:S], ACT.Copy).then_inc(pj_ev[0], 1)
                elif kind == "q":
                    a.activation(dst, ps[:, u % 4, 0:S], ACT.Copy, scale=QSCALE).then_inc(pj_ev[0], 1)
                else:
                    a.activation(dst, ps[:, u % 4, :], ACT.Copy).then_inc(pj_ev[0], 1)

            def forget_gate():
                unit_filled(act, GATE_UNIT)
                act.wait_ge(small_in, 16 * SMALL)
                link(a.activation(fz[:, 0, :], ps[0:HF, 0, 0:S], ACT.Abs, bias=bf[:, 0:1]))
                link(a.activation(fz[:, 1, :], fz[:, 0, :], ACT.Exp, scale=-1.0))
                a.activation(fz[:, 2, :], fz[:, 1, :], ACT.Ln, bias=1.0).then_inc(f_act, 1)

            def exps(H):
                t = H % 2
                act.wait_ge(mx, 2 * (H + 1))
                a.activation(lg[:, t, 0:P], lg[:, t, 0:P], ACT.Exp, bias=negm[:, t, 0:1],
                             accum_out=rs[:, t, 0:1]).then_inc(ex, 1)
                a.activation(lg[:, t, P:3 * P], lg[:, t, P:3 * P], ACT.Exp, bias=negm[:, t, 1:2],
                             accum_out=rs[:, t, 1:2]).then_inc(ex, 1)

            def probs_out(T):
                act.wait_ge(pt_mm, T + 1)
                if T >= 2:
                    act.wait_ge(pv_mm, T - 1)
                a.activation(pT[:, T % 2, :], ps[:, 2 + T % 2, 0:3 * P], ACT.Copy).then_inc(pt_ev, 1)

            def gate_out(norm):
                act.wait_ge(bc_mm, BC_GATE[norm])
                for q in range(2):
                    a.activation(gbc[:, q * 512:q * 512 + 512], ps[:, 4 + q, :], ACT.Copy).then_inc(g_ev, 1)

            def squares(norm):
                for b in range(NB):
                    u = 2 * norm + b
                    act.wait_ge(r_sum, u + 1)
                    a.activation(h[:, b, :], xres[:, b, :], ACT.Square, bias=st[:, 2 + b:3 + b],
                                 accum_out=st[:, 4 + b:5 + b]).then_inc(r_sq, 1)

            def router_exp(l):
                act.wait_ge(rt_dve, l + 1)
                a.activation(rt[:, 1, :], rt[:, 0, :], ACT.Exp).then_inc(rt_act, 1)

            def experts(l):
                n0 = N_MOE[l]

                def tokens_out(G):
                    act.wait_ge(ga_mm, G + 1)
                    a.activation(xg[:, 512:D], ps[:, 7, :], ACT.Copy).then_inc(xg_ev, 1)

                def turned_out(G):
                    act.wait_ge(tx_mm, G + 1)
                    a.activation(xT[:, 4:8, :].rearrange("p a b -> p (a b)"), ps[:, 7, :], ACT.Copy).then_inc(xt_ev, 1)

                def overflow(i, j):
                    n = act.value_load(tabn[0:1, bass.ds(i * 2 + j, 1)], min_val=0, max_val=ROUNDS)
                    b = act.value_load(tabb[0:1, bass.ds(i * 2 + j, 1)], min_val=0, max_val=2 * NE * ROUNDS)
                    with act.If(n > 0):
                        with act.Fori(b, b + n) as g:
                            act.wait_ge(o_pe, g * 7 + 1)
                            a.activation(ox[:, :], ps[:, 6, :], ACT.Copy).then_inc(o_act, 1)
                            act.wait_ge(o_pe, g * 7 + 3)
                            a.activation(ox[:, :], ps[:, 6, :], ACT.Copy).then_inc(o_act, 1)
                            act.wait_ge(o_pe, g * 7 + 4)
                            gt = ps[:, 7, :].rearrange("p (c s) -> p c s", c=4)
                            a.activation(osg[:, :, :], gt[:, :, 0:CAP], ACT.Sigmoid).then_inc(o_act, 1)
                            act.wait_ge(o_pe, g * 7 + 5)
                            a.activation(oy[0:CAP, 0:512], ps[0:CAP, 6, :], ACT.Copy).then_inc(o_act, 1)

                act.wait_ge(tab, l + 1)
                tokens_out(9 * l)
                turned_out(9 * l)
                with act.Fori(0, PAIRS) as i:
                    q = i + 8 * l
                    G = i + 9 * l
                    overflow(i, 0)
                    spent(act, n0 + 1, i)
                    a.activation(gu[:, 0, :], ps[:, 4, :], ACT.Copy).then_inc(gu_ev[0], 1)
                    overflow(i, 1)
                    tokens_out(G + 1)
                    act.wait_ge(tg_mm[0], q + 1)
                    gt = ps[:, 4, :].rearrange("p (c s) -> p c s", c=4)
                    a.activation(sg[:, 0, :, :], gt[:, :, 0:CAP], ACT.Sigmoid).then_inc(sg_r[0], 1)
                    spent(act, n0 + 4, i)
                    a.activation(gu[:, 1, :], ps[:, 5, :], ACT.Copy).then_inc(gu_ev[1], 1)
                    turned_out(G + 1)
                    act.wait_ge(tg_mm[1], q + 1)
                    gt = ps[:, 5, :].rearrange("p (c s) -> p c s", c=4)
                    a.activation(sg[:, 1, :, :], gt[:, :, 0:CAP], ACT.Sigmoid).then_inc(sg_r[1], 1)
                    act.wait_ge(sc_mm, G + 1)
                    spent(act, n0 + 2, i)
                    a.activation(y[0:CAP, 0:512], ps[0:CAP, 4, :], ACT.Copy).then_inc(y_ev[0], 1)
                    spent(act, n0 + 5, i)
                    a.activation(y[CAP:P, 0:512], ps[0:CAP, 5, :], ACT.Copy).then_inc(y_ev[1], 1)

            turned(0)
            for (u, kind, dst) in proj_units(0):
                if u == 16:
                    forget_gate()
                else:
                    unit_out(u, dst, kind)
            for t in range(HF + 1):
                if t < HF:
                    exps(t)
                if t >= 1:
                    probs_out(t - 1)
            gate_out(0)
            squares(0)
            turned(1)
            router_exp(0)
            experts(0)
            gate_out(1)
            squares(1)
            turned(2)
            us = proj_units(1)
            for (u, kind, dst) in us[:12]:
                unit_out(u, dst, kind)
            turned(3)
            for (u, kind, dst) in us[12:]:
                unit_out(u, dst, kind)
            act.wait_ge(lam_r, 1)
            a.activation(lam2[:, 2:4], lam2[:, 0:2], ACT.Exp).then_inc(lam_r, 1)
            for t in range(HD + 1):
                if t < HD:
                    exps(HF + 2 * t)
                    exps(HF + 2 * t + 1)
                if t >= 1:
                    probs_out(HF + t - 1)
            for q in range(2):
                act.wait_ge(ot_mm, 2 * q + 1)
                a.activation(oT[:, 4 * q:4 * q + 2, :].rearrange("p a b -> p (a b)"), ps[:, 2 * q, :],
                             ACT.Copy).then_inc(ot_ev, 1)
            gate_out(2)
            squares(2)
            turned(4)
            router_exp(1)
            experts(1)
            gate_out(3)
            squares(3)

        @block.vector
        def _(dve):
            d = nc.vector
            link = Chain(dve, dch)

            dve.sem_inc(y_ev[0], 2)
            dve.sem_inc(y_ev[1], 2)
            dve.sem_inc(tp_ev, 1)
            link(d.memset(kT[:, :, :], 0.0))
            link(d.memset(ncum[:, :], 0.0))
            dve.wait_ge(csil, 1)
            link(d.tensor_tensor(csig[:, :], csig[:, :], ccol[:, :], ALU.mult))
            d.tensor_copy(crep[:, :, :], csig[:, :].unsqueeze(2).broadcast_to([P, KC, 32])).then_inc(csil, 1)
            dve.wait_ge(small_in, 16 * SMALL)
            for g0 in (0, 4):
                link(d.tensor_scalar(rows[64:P, g0, :], rows[64:P, g0, :], 1.0, None, ALU.add))
                link(d.tensor_scalar(rows[0:64, g0 + 1, :], rows[0:64, g0 + 1, :], 1.0, None, ALU.add))
                link(d.tensor_scalar(rows[:, g0 + 2, :], rows[:, g0 + 2, :], 1.0, None, ALU.add))
            link(d.tensor_scalar(rows[64:P, 3, :], rows[64:P, 3, :], 1.0, None, ALU.add))
            for t in range(2):
                link(d.tensor_tensor(lamt[:, :], lamin[:, 2 * t, :], lamin[:, 2 * t + 1, :], ALU.mult))
                ins = d.tensor_reduce(lam2[:, t:t + 1], lamt[:, :], AX.X, ALU.add)
                if t == 0:
                    link(ins)
                else:
                    ins.then_inc(lam_r, 1)

            def mod_rows(gi):
                for j in range(4):
                    spent(dve, N_ADA[gi] + j)
                d.tensor_tensor(rows[:, gi, :], rows[:, gi, :], ps[:, 7, :], ALU.add).then_inc(mod_row, 1)

            def modulated(m):
                dve.wait_ge(bc_mm, BC_MOD[m])
                sc = ps[:, 0:2, :].rearrange("p a b -> p (a b)")
                sh = ps[:, 2:4, :].rearrange("p a b -> p (a b)")
                for b in range(NB):
                    link(d.tensor_tensor(h[:, b, :], xres[:, b, :], sc, ALU.mult))
                    d.tensor_tensor(h[:, b, :], h[:, b, :], sh, ALU.add).then_inc(h_ready, 1)
                dve.wait_ge(ht_mm, m + 1)
                for q in range(2, 4):
                    d.tensor_copy(hT[:, 2 * q:2 * q + 2, :].rearrange("p a b -> p (a b)"),
                                  ps[:, 4 + q, :]).then_inc(ht_ready, 1)

            def unit_out(u, dst, kind):
                if u % 2 == 0:
                    return
                unit_filled(dve, u)
                if kind == "k":
                    cc = dst
                    link(d.tensor_copy(kT[0:64, 2 * cc, :], ps[0:64, u % 4, 0:S]))
                    d.tensor_copy(kT[64:P, 2 * cc + 1, :], ps[64:P, u % 4, 0:S]).then_inc(pj_ev[1], 1)
                elif kind == "q":
                    d.tensor_scalar(dst, ps[:, u % 4, 0:S], QSCALE, None, ALU.mult).then_inc(pj_ev[1], 1)
                else:
                    d.tensor_copy(dst, ps[:, u % 4, :]).then_inc(pj_ev[1], 1)

            def forget_gate():
                dve.wait_ge(f_act, 1)
                link(d.tensor_scalar(fz[:, 0, :], ps[0:HF, 0, 0:S], bf[:, 0:1], 0.0, ALU.add, ALU.min))
                link(d.tensor_tensor(fz[:, 1, :], fz[:, 2, :], fz[:, 0, :], ALU.subtract))
                link(d.memset(fz[:, 3, :], 1.0))
                link(d.tensor_tensor_scan(ncum[0:HF, P:3 * P], fz[:, 3, :], fz[:, 1, :], 0.0, ALU.mult, ALU.add))
                d.tensor_copy(ncum[0:HF, 0:P], ncum[0:HF, P:2 * P]).then_inc(f_steps, 1)

            def soft(H, bias, factor):
                t = H % 2
                dve.wait_ge(s_mm, H + 1)
                link(d.scalar_tensor_tensor(out=lg[:, t, :], in0=bias[:, :], scalar=factor, in1=ps[:, t, 0:3 * P],
                                            op0=ALU.mult, op1=ALU.add))
                d.tensor_reduce(negm[:, t, 0:1], lg[:, t, 0:P], AX.X, ALU.max, negate=True).then_inc(mx, 1)
                d.tensor_reduce(negm[:, t, 1:2], lg[:, t, P:3 * P], AX.X, ALU.max, negate=True).then_inc(mx, 1)

            def fox_norm(H):
                t = H % 2
                dve.wait_ge(ex, 2 * (H + 1))
                link(d.reciprocal(rr[:, t, :], rs[:, t, :]))
                d.tensor_scalar(lg[:, t, 0:P], lg[:, t, 0:P], rr[:, t, 0:1], None, ALU.mult).then_inc(pn, 1)
                d.tensor_scalar(lg[:, t, P:3 * P], lg[:, t, P:3 * P], rr[:, t, 1:2], None, ALU.mult).then_inc(pn, 1)

            def diff_norm(hd):
                dve.wait_ge(ex, 2 * (HF + 2 * hd + 2))
                link(d.reciprocal(rr[:, 0, :], rs[:, 0, :]))
                link(d.reciprocal(rr[:, 1, :], rs[:, 1, :]))
                link(d.tensor_scalar(rr[:, 1, :], rr[:, 1, :], lam2[:, 0:1], None, ALU.mult))
                for q, (lo, hi) in enumerate(((0, P), (P, 3 * P))):
                    link(d.tensor_scalar(lg[:, 0, lo:hi], lg[:, 0, lo:hi], rr[:, 0, q:q + 1], None, ALU.mult))
                    d.scalar_tensor_tensor(out=lg[:, 0, lo:hi], in0=lg[:, 1, lo:hi], scalar=rr[:, 1, q:q + 1],
                                           in1=lg[:, 0, lo:hi], op0=ALU.mult, op1=ALU.add).then_inc(pn, 1)

            def post_norm(norm):
                dve.wait_ge(g_ev, 2 * (norm + 1))
                if norm % 2 == 0:
                    for j in range(2):
                        spent(dve, N_WO[norm // 2] + j)
                else:
                    dve.wait_ge(sc_mm, 9 * (norm // 2) + 9)
                for b in range(NB):
                    yb = ps[:, 2 * b:2 * b + 2, :].rearrange("p a b -> p (a b)")
                    link(d.tensor_tensor(h[:, b, :], gbc[:, :], yb, ALU.mult))
                    link(d.scalar_tensor_tensor(out=xres[:, b, :], in0=xres[:, b, :], scalar=ALPHA, in1=h[:, b, :],
                                                op0=ALU.mult, op1=ALU.add, accum_out=st[:, b:b + 1]))
                    d.tensor_scalar(st[:, 2 + b:3 + b], st[:, b:b + 1], -1.0 / D, None, ALU.mult).then_inc(r_sum, 1)
                dve.wait_ge(bc_mm, BC_LN[norm])
                lg_ = ps[:, 6:8, :].rearrange("p a b -> p (a b)")
                lb_ = ps[:, 4:6, :].rearrange("p a b -> p (a b)")
                for b in range(NB):
                    dve.wait_ge(r_std, 2 * norm + b + 1)
                    link(d.tensor_scalar(xres[:, b, :], xres[:, b, :], st[:, 2 + b:3 + b], st[:, 8 + b:9 + b],
                                         ALU.add, ALU.mult))
                    link(d.tensor_tensor(xres[:, b, :], xres[:, b, :], lg_, ALU.mult))
                    d.tensor_tensor(xres[:, b, :], xres[:, b, :], lb_, ALU.add).then_inc(x_ready, 1)

            def rank4(src, n, cmp, eq, dst):
                a4 = src.unsqueeze(2).broadcast_to([P, n, 4, 4])
                b4 = src.unsqueeze(3).broadcast_to([P, n, 4, 4])
                tri = tri4[:, :, :].unsqueeze(1).broadcast_to([P, n, 4, 4])
                link(d.tensor_tensor(cmp, a4, b4, ALU.is_gt))
                link(d.tensor_tensor(eq, a4, b4, ALU.is_equal))
                link(d.tensor_tensor(eq, eq, tri, ALU.mult))
                link(d.tensor_tensor(cmp, cmp, eq, ALU.add))
                link(d.tensor_reduce(dst, cmp, AX.X, ALU.add))

            def route(l):
                def t3(k):
                    return rt[:, k, :].rearrange("p (b e) -> p b e", b=NB)

                def t4(k):
                    return rt[:, k, :].rearrange("p (g e) -> p g e", e=EG)
                dve.wait_ge(rt_mm, 3 * l + 1)
                lgt = ps[:, 0, 0:NB * NE]
                mxr = st[:, 10:12]
                link(d.tensor_copy(rt[:, 2, :], lgt))
                link(d.tensor_reduce(mxr, t3(2), AX.X, ALU.max))
                d.tensor_tensor(t3(0), t3(2), mxr.unsqueeze(2).broadcast_to([P, NB, NE]), ALU.subtract).then_inc(rt_dve, 1)
                dve.wait_ge(rt_act, l + 1)
                link(d.tensor_reduce(st[:, 12:14], t3(1), AX.X, ALU.add))
                link(d.reciprocal(st[:, 12:14], st[:, 12:14]))
                link(d.tensor_tensor(t3(3), t3(1), st[:, 12:14].unsqueeze(2).broadcast_to([P, NB, NE]), ALU.mult))
                link(d.tensor_tensor(t3(4), t3(3), rb[:, :].unsqueeze(1).broadcast_to([P, NB, NE]), ALU.add))
                A, B = t4(4)[:, :, 0:4:2], t4(4)[:, :, 1:4:2]
                hi = rg[:, 0, 0:16].rearrange("p (g e) -> p g e", e=2)
                lo = rg[:, 1, 0:16].rearrange("p (g e) -> p g e", e=2)
                link(d.tensor_tensor(hi, A, B, ALU.max))
                link(d.tensor_tensor(lo, A, B, ALU.min))
                m1, x1, x2 = rg[:, 2, 0:8], rg[:, 3, 0:8], rg[:, 4, 0:8]
                link(d.tensor_tensor(m1, hi[:, :, 0], hi[:, :, 1], ALU.max))
                link(d.tensor_tensor(x1, hi[:, :, 0], hi[:, :, 1], ALU.min))
                link(d.tensor_tensor(x2, lo[:, :, 0], lo[:, :, 1], ALU.max))
                link(d.tensor_tensor(x1, x1, x2, ALU.max))
                link(d.tensor_tensor(m1, m1, x1, ALU.add))
                gsum = m1.rearrange("p (b g) -> p b g", b=NB)
                c2 = [rc[:, k, 0:NB * 16].rearrange("p (n i j) -> p n i j", i=4, j=4) for k in range(2)]
                rank4(gsum, NB, c2[0], c2[1], rg[:, 5, 0:8].rearrange("p (b g) -> p b g", b=NB))
                link(d.tensor_scalar(rg[:, 5, 0:8], rg[:, 5, 0:8], 0.5, None, ALU.is_lt))
                c8 = [rc[:, k, :].rearrange("p (n i j) -> p n i j", i=4, j=4) for k in range(2)]
                rank4(t4(4), NB * NG, c8[0], c8[1], t4(5))
                link(d.tensor_scalar(rt[:, 5, :], rt[:, 5, :], 1.5, None, ALU.is_lt))
                link(d.tensor_tensor(t4(6), t4(5), rg[:, 5, 0:8].unsqueeze(2).broadcast_to([P, NB * NG, EG]), ALU.mult))
                d.tensor_copy(rt[:, 7, :], rt[:, 6, :]).then_inc(rt_mask, 1)
                link(d.tensor_tensor(rt[:, 8, :], rt[:, 3, :], rt[:, 6, :], ALU.mult))
                link(d.tensor_reduce(st[:, 14:16], t3(8), AX.X, ALU.add))
                link(d.reciprocal(st[:, 14:16], st[:, 14:16]))
                link(d.memset(gate[:, :, :], 0.0))
                link(d.memset(pos[:, :, :], -1.0))
                link(d.tensor_tensor(gate[:, :, 0:NE], t3(8), st[:, 14:16].unsqueeze(2).broadcast_to([P, NB, NE]), ALU.mult))
                dve.wait_ge(rt_mm, 3 * l + 2)
                link(d.scalar_tensor_tensor(out=rt[:, 9, :], in0=ps[:, 1, 0:NB * NE], scalar=1.0, in1=rt[:, 6, :],
                                            op0=ALU.add, op1=ALU.mult))
                link(d.tensor_scalar(pos[:, :, 0:NE], t3(9), -1.0, None, ALU.add))
                dve.wait_ge(rt_mm, 3 * l + 3)
                tot = ps[0:1, 2, 0:NE]
                link(d.tensor_scalar(cnt[:, 0, :], tot, float(CAP) + 0.5, None, ALU.is_gt))
                for r in range(2, ROUNDS + 1):
                    link(d.tensor_scalar(cnt[:, 1, :], tot, r * float(CAP) + 0.5, None, ALU.is_gt))
                    link(d.tensor_tensor(cnt[:, 0, :], cnt[:, 0, :], cnt[:, 1, :], ALU.add))
                link(d.memset(cnt[:, 2, :], 1.0))
                start = 0.0 if l == 0 else cnt[:, 5, 0:1]
                link(d.tensor_tensor_scan(cnt[:, 3, :], cnt[:, 2, :], cnt[:, 0, :], start, ALU.mult, ALU.add))
                link(d.tensor_tensor(cnt[:, 4, :], cnt[:, 3, :], cnt[:, 0, :], ALU.subtract))
                link(d.tensor_copy(cnt[:, 5, 0:1], cnt[:, 3, NE - 1:NE]))
                link(d.tensor_copy(tabn[:, :], cnt[:, 0, :]))
                d.tensor_copy(tabb[:, :], cnt[:, 4, :]).then_inc(tab, 1)
                dve.wait_ge(tab, l + 1)

            def experts(l):
                n0 = N_MOE[l]

                def pick_pair(i):
                    for b in range(NB):
                        for j in range(2):
                            d.tensor_scalar(pick[:, b, j * CAP:(j + 1) * CAP], lane[:, :],
                                            pos[:, b, bass.ds(i * 2 + j, 1)], None, ALU.is_equal).then_inc(picked, 1)

                def put_pair(i):
                    for b in range(NB):
                        for j in range(2):
                            d.tensor_scalar(put[:, b, j * CAP:(j + 1) * CAP], lane[:, :],
                                            pos[:, b, bass.ds(i * 2 + j, 1)], gate[:, b, bass.ds(i * 2 + j, 1)],
                                            ALU.is_equal, ALU.mult).then_inc(putted, 1)

                def tokens_out(G):
                    dve.wait_ge(ga_mm, G + 1)
                    d.tensor_copy(xg[:, 0:512], ps[:, 6, :]).then_inc(xg_ev, 1)

                def turned_out(G):
                    dve.wait_ge(tx_mm, G + 1)
                    d.tensor_copy(xT[:, 0:4, :].rearrange("p a b -> p (a b)"), ps[:, 6, :]).then_inc(xt_ev, 1)

                def glu(j, q):
                    gt = ps[:, 4 + j, :].rearrange("p (c s) -> p c s", c=4)
                    dve.wait_ge(sg_r[j], q + 1)
                    d.tensor_tensor(tg[:, j, :, :], sg[:, j, :, :], gt[:, :, 0:CAP], ALU.mult).then_inc(tg_r[j], 1)
                    dve.wait_ge(tg_r[j], q + 1)
                    d.tensor_tensor(aT[:, j, :].rearrange("p (c s) -> p c s", c=4), tg[:, j, :, :],
                                    gt[:, :, CAP:2 * CAP], ALU.mult).then_inc(at_r[j], 1)

                def overflow(i, j):
                    e = i * 2 + j
                    n = dve.value_load(tabn[0:1, bass.ds(e, 1)], min_val=0, max_val=ROUNDS)
                    b0 = dve.value_load(tabb[0:1, bass.ds(e, 1)], min_val=0, max_val=2 * NE * ROUNDS)
                    d.tensor_copy(opos[:, j, :].unsqueeze(2), pos[:, :, bass.ds(e, 1)]).then_inc(o_pos, 1)
                    with dve.If(n > 0):
                        with dve.Fori(b0, b0 + n) as g:
                            k = g * 13
                            dve.wait_ge(o_pos, i * 2 + (16 * l + j + 1))
                            d.tensor_scalar(opos[:, j, :], opos[:, j, :], -float(CAP), None, ALU.add).then_inc(o_dve, 1)
                            dve.wait_ge(o_dve, k + 1)
                            for b in range(NB):
                                d.tensor_scalar(opick[:, b, :], lane[:, :], opos[:, j, b:b + 1], None,
                                                ALU.is_equal).then_inc(o_dve, 1)
                                d.tensor_scalar(oput[:, b, :], lane[:, :], opos[:, j, b:b + 1],
                                                gate[:, b, bass.ds(e, 1)], ALU.is_equal, ALU.mult).then_inc(o_dve, 1)
                            dve.wait_ge(o_pe, g * 7 + 2)
                            d.tensor_copy(oxT[:, :, :].rearrange("p a b -> p (a b)"), ps[:, 7, :]).then_inc(o_dve, 1)
                            dve.wait_ge(o_act, g * 4 + 3)
                            gt = ps[:, 7, :].rearrange("p (c s) -> p c s", c=4)
                            d.tensor_tensor(osg[:, :, :], osg[:, :, :], gt[:, :, 0:CAP], ALU.mult).then_inc(o_dve, 1)
                            dve.wait_ge(o_dve, k + 7)
                            d.tensor_tensor(oaT.rearrange("p (c s) -> p c s", c=4), osg[:, :, :],
                                            gt[:, :, CAP:2 * CAP], ALU.mult).then_inc(o_dve, 1)
                            dve.wait_ge(o_pe, g * 7 + 5)
                            d.tensor_copy(oy[0:CAP, 512:D], ps[CAP:P, 6, :]).then_inc(o_dve, 1)
                            dve.wait_ge(o_pe, g * 7 + 6)
                            d.tensor_copy(oputT[0:CAP, :], ps[0:CAP, 7, 0:S]).then_inc(o_dve, 1)
                            dve.wait_ge(o_pe, g * 7 + 7)
                            dve.sem_inc(o_dve, 3)
                            dve.wait_ge(o_dve, k + 13)

                link(d.memset(putT[:, :], 0.0))
                link(d.memset(y[:, :], 0.0))
                pick_pair(0)
                tokens_out(9 * l)
                turned_out(9 * l)
                with dve.Fori(0, PAIRS) as i:
                    q = i + 8 * l
                    G = i + 9 * l
                    overflow(i, 0)
                    dve.wait_ge(ga_mm, G + 1)
                    pick_pair(i + 1)
                    put_pair(i)
                    overflow(i, 1)
                    tokens_out(G + 1)
                    glu(0, q)
                    turned_out(G + 1)
                    glu(1, q)
                    dve.wait_ge(sc_mm, G + 1)
                    spent(dve, n0 + 2, i)
                    d.tensor_copy(y[0:CAP, 512:D], ps[CAP:P, 4, :]).then_inc(y_ev[0], 1)
                    spent(dve, n0 + 5, i)
                    d.tensor_copy(y[CAP:P, 512:D], ps[CAP:P, 5, :]).then_inc(y_ev[1], 1)
                    dve.wait_ge(tp_mm, q + 1)
                    d.tensor_copy(putT[:, :], ps[:, 6, 0:S]).then_inc(tp_ev, 1)

            mod_rows(0)
            dve.wait_ge(x_in, 16 * NB)
            modulated(0)
            for (u, kind, dst) in proj_units(0):
                if u == 16:
                    forget_gate()
                else:
                    unit_out(u, dst, kind)
            for t in range(HF + 1):
                if t < HF:
                    if t >= 2:
                        dve.wait_ge(pt_mm, t - 1)
                    soft(t, maskf, 1.0)
                if t >= 1 and t % 2 == 0:
                    pair = t // 2 - 1
                    dve.wait_ge(pv_mm, t)
                    d.tensor_copy(oT[:, pair, :], ps[:, 4 + pair % 2, 0:S]).then_inc(o_ev, 1)
                if t in (4, 10):
                    mod_rows(1 if t == 4 else 2)
                if t < HF:
                    fox_norm(t)
            post_norm(0)
            modulated(1)
            route(0)
            experts(0)
            post_norm(1)
            mod_rows(3)
            mod_rows(4)
            modulated(2)
            us = proj_units(1)
            link(d.memset(kT[:, :, :], 0.0))
            d.memset(ncum[:, 0:1], 0.0).then_inc(f_steps, 1)
            for (u, kind, dst) in us[:12]:
                unit_out(u, dst, kind)
            modulated(3)
            for (u, kind, dst) in us[12:]:
                unit_out(u, dst, kind)
            dve.wait_ge(lam_r, 2)
            link(d.scalar_tensor_tensor(out=lam2[:, 0:1], in0=lam2[:, 2:3], scalar=-1.0, in1=lam2[:, 3:4],
                                        op0=ALU.mult, op1=ALU.add))
            link(d.tensor_scalar(lam2[:, 0:1], lam2[:, 0:1], -LAM_INIT, None, ALU.add))
            for t in range(HD + 1):
                if t < HD:
                    slope = -(2.0 ** (-8.0 * (t + 1) / HD))
                    if t >= 1:
                        dve.wait_ge(pt_mm, HF + t)
                    soft(HF + 2 * t, dist, slope)
                    soft(HF + 2 * t + 1, dist, slope)
                if t >= 1:
                    hd = t - 1
                    dve.wait_ge(pv_mm, HF + hd + 1)
                    for b in range(NB):
                        d.tensor_copy(h[:, b, hd * P:(hd + 1) * P], ps[:, 4 + hd % 2, b * P:(b + 1) * P]).then_inc(o_ev, 1)
                if t in (3, 6):
                    mod_rows(5 if t == 3 else 6)
                if t < HD:
                    diff_norm(t)
            dve.wait_ge(o_ev, HD + 2 * HD)
            ov = h[:, :, :].rearrange("p b (e f) -> p (b e) f", f=P)
            sq = hT[:, :, :].rearrange("p k s -> p (k s)").rearrange("p (e f) -> p e f", f=P)
            link(d.tensor_tensor(sq, ov, ov, ALU.mult))
            link(d.tensor_reduce(ss[:, 0, :], sq, AX.X, ALU.add))
            link(d.tensor_scalar(normg[:, :], normg[:, :], 1.0 - LAM_INIT, None, ALU.mult))
            dve.sem_inc(o_rms, 1)
            dve.wait_ge(o_pow, 1)
            link(d.tensor_tensor(ov, ov, ss[:, 2, :].unsqueeze(2).broadcast_to([P, 2 * HD, P]), ALU.mult))
            d.tensor_tensor(ov, ov, normg[:, :].unsqueeze(1).broadcast_to([P, 2 * HD, P]), ALU.mult).then_inc(o_nrm, 1)
            for q in range(2):
                dve.wait_ge(ot_mm, 2 * q + 2)
                d.tensor_copy(oT[:, 4 * q + 2:4 * q + 4, :].rearrange("p a b -> p (a b)"), ps[:, 2 * q + 1, :]).then_inc(ot_ev, 1)
            post_norm(2)
            modulated(4)
            route(1)
            experts(1)
            post_norm(3)

        @block.tensor
        def _(pe):
            t = nc.tensor

            def mod_product(gi):
                if gi == 0:
                    pe.wait_ge(csil, 2)
                n = N_ADA[gi]
                for j in range(4):
                    landed(pe, n + j)
                if gi >= 1:
                    pe.wait_ge(mod_row, gi)
                if gi == 3:
                    pe.wait_ge(x_ready, 2 * NB)
                if gi == 5:
                    pe.wait_ge(ht_ready, 4 * 4)
                for k in range(KC):
                    for j in range(4):
                        mm = t.matmul(ps[32 * j:32 * j + 32, 7, :], crep[:, k, :], wcols(n + j)[:, k, :],
                                      start=(k == 0), stop=(k == KC - 1))
                        if k == KC - 1:
                            mm.then_inc(used[slot(n + j)], 1)

            def spread(row, bank, inc):
                gi, j = row
                for q in range(2):
                    mm = t.matmul(ps[:, bank + q, :], sel(32 * (j + q)), rows[:, gi, :], start=True, stop=True)
                if inc:
                    mm.then_inc(bc_mm, 1)

            def modulate(m):
                if m == 0:
                    pe.wait_ge(consts, 9)
                pe.wait_ge(mod_row, (1, 3, 4, 5, 7)[m])
                if m == 3:
                    pe.wait_ge(pj_ev[0], pj_even(UNITS0 + 12))
                    pe.wait_ge(pj_ev[1], pj_odd(UNITS0 + 12))
                elif m >= 1:
                    pe.wait_ge(x_ready, NB * (1, 1, 2, 2, 3)[m])
                spread(MODS[m][0], 0, False)
                spread(MODS[m][1], 2, True)
                for b in range(NB):
                    pe.wait_ge(h_ready, 2 * m + b + 1)
                    for k in range(KC):
                        o = (k % 2) * S + b * P
                        mm = t.transpose(ps[:, 4 + k // 2, o:o + P], h[:, b, k * P:(k + 1) * P], ident[:, :])
                mm.then_inc(ht_mm, 1)
                pe.wait_ge(ht_ready, 4 * (m + 1))

            def unit_free(u):
                if u >= 4 and u - UNITS0 not in (0, 1, 2, 3):
                    if u - 4 == GATE_UNIT:
                        pe.wait_ge(f_steps, 1)
                    else:
                        pe.wait_ge(pj_ev[u % 2], pj_even(u - 3) if u % 2 == 0 else pj_odd(u - 3))

            def turned_units(u, n, pieces_):
                for s_ in range(pieces_):
                    landed(pe, n + s_)
                    for cc in range(4):
                        unit_free(u)
                        for k in range(KC):
                            mm = t.matmul(ps[:, u % 4, 0:S], wcols(n + s_)[:, k, cc * P:(cc + 1) * P], hT[:, k, :],
                                          start=(k == 0), stop=(k == KC - 1))
                        mm.then_inc(used[slot(n + s_)] if cc == 3 else pj_mm, 1)
                        u += 1
                return u

            def natural_units(u, n, pieces_):
                for s_ in range(pieces_):
                    landed(pe, n + s_)
                    for b in range(NB):
                        unit_free(u)
                        for k in range(KC):
                            mm = t.matmul(ps[:, u % 4, :], hT[:, k, b * P:(b + 1) * P], wcols(n + s_)[:, k, :],
                                          start=(k == 0), stop=(k == KC - 1))
                        mm.then_inc(used[slot(n + s_)] if b == 1 else pj_mm, 1)
                        u += 1
                return u

            def scores(H, chunk, half, head):
                bank = H % 2
                if H >= 2:
                    pe.wait_ge(mx, 2 * (H - 1))
                if head is not None:
                    t.matmul(ps[:, bank, 0:3 * P], sel(head), ncum[:, :], start=True, stop=True)
                first = head is None
                kk = kT[:, 2 * chunk + half, :]
                t.matmul(ps[:, bank, 0:P], qT[:, chunk, 0:P], kk[:, 0:P], start=first, stop=True,
                         skip_group_check=True)
                t.matmul(ps[:, bank, P:3 * P], qT[:, chunk, P:2 * P], kk, start=first, stop=True,
                         skip_group_check=True).then_inc(s_mm, 1)

            def turn_probs(T, buf, pn_count):
                pe.wait_ge(pn, pn_count)
                if T >= 2:
                    pe.wait_ge(pt_ev, T - 1)
                for q in range(3):
                    mm = t.transpose(ps[:, 2 + T % 2, q * P:(q + 1) * P], lg[:, buf, q * P:(q + 1) * P], ident[:, :])
                mm.then_inc(pt_mm, 1)

            def fox_values(hh):
                pair = hh // 2
                lo = 64 * (hh % 2)
                bank = 4 + pair % 2
                pe.wait_ge(pt_ev, hh + 1)
                if hh % 2 == 0 and pair >= 2:
                    pe.wait_ge(o_ev, pair - 1)
                t.matmul(ps[lo:lo + 64, bank, 0:S], v[:, 0, 64 * hh:64 * hh + 64], pT[:, hh % 2, 0:S],
                         start=True, stop=True)
                t.matmul(ps[lo:lo + 64, bank, P:S], v[:, 1, 64 * hh:64 * hh + 64], pT[:, hh % 2, S:S + P],
                         start=False, stop=True, skip_group_check=True).then_inc(pv_mm, 1)

            def diff_values(hd):
                T = HF + hd
                bank = 4 + hd % 2
                pe.wait_ge(pt_ev, T + 1)
                if hd >= 2:
                    pe.wait_ge(o_ev, HD + 2 * (hd - 1))
                vv = [v[:, b, hd * P:(hd + 1) * P] for b in range(NB)]
                t.matmul(ps[:, bank, 0:P], pT[:, T % 2, 0:P], vv[0], start=True, stop=True)
                t.matmul(ps[:, bank, P:S], pT[:, T % 2, P:S], vv[0], start=True, stop=False)
                t.matmul(ps[:, bank, P:S], pT[:, T % 2, S:S + P], vv[1], start=False, stop=True).then_inc(pv_mm, 1)

            def out_product(l):
                n = N_WO[l]
                for s_ in range(2):
                    landed(pe, n + s_)
                    for b in range(NB):
                        for k in range(KC):
                            mm = t.matmul(ps[:, 2 * b + s_, :], oT[:, k, b * P:(b + 1) * P], wcols(n + s_)[:, k, :],
                                          start=(k == 0), stop=(k == KC - 1))
                    mm.then_inc(used[slot(n + s_)], 1)

            def norm_vectors(norm):
                name = "af"[norm % 2]
                l = norm // 2
                if norm % 2 == 0:
                    pe.wait_ge(mod_row, 3 if l == 0 else 7)
                spread(ROW["g_" + name, l], 4, True)
                spread(ROW["ln_" + name + "_g", l], 6, False)
                pe.wait_ge(g_ev, 2 * (norm + 1))
                spread(ROW["ln_" + name + "_b", l], 4, True)

            def route(l):
                for b in range(NB):
                    for k in range(KC):
                        mm = t.matmul(ps[:, 0, b * NE:(b + 1) * NE], hT[:, k, b * P:(b + 1) * P], rw[:, k, :],
                                      start=(k == 0), stop=(k == KC - 1))
                mm.then_inc(rt_mm, 1)
                pe.wait_ge(rt_mask, l + 1)
                m0, m1 = rt[:, 7, 0:NE], rt[:, 7, NE:2 * NE]
                t.matmul(ps[:, 1, 0:NE], before[:, :], m0, start=True, stop=True)
                t.matmul(ps[:, 1, NE:2 * NE], ones[:, :], m0, start=True, stop=False)
                t.matmul(ps[:, 1, NE:2 * NE], before[:, :], m1, start=False, stop=True).then_inc(rt_mm, 1)
                t.matmul(ps[:, 2, 0:NE], ones[:, :], m0, start=True, stop=False)
                t.matmul(ps[:, 2, 0:NE], ones[:, :], m1, start=False, stop=True).then_inc(rt_mm, 1)

            def experts(l):
                n0 = N_MOE[l]

                def gather(G):
                    pe.wait_ge(picked, (G + 1) * 4)
                    for q in range(2):
                        for b in range(NB):
                            mm = t.matmul(ps[:, 6 + q, :], pick[:, b, :], h[:, b, q * 512:q * 512 + 512],
                                          start=(b == 0), stop=(b == NB - 1))
                    mm.then_inc(ga_mm, 1)

                def turn_tokens(G):
                    pe.wait_ge(xg_ev, (G + 1) * 2)
                    for k in range(KC):
                        mm = t.transpose(ps[:, 6 + k // 4, (k % 4) * P:(k % 4 + 1) * P], xg[:, k * P:(k + 1) * P], ident[:, :])
                    mm.then_inc(tx_mm, 1)

                def gate_up(j, i, lhs, bank, ks, last):
                    ng, nu = n0 + 3 * j, n0 + 3 * j + 1
                    for k in ks:
                        mg = t.matmul(ps[0:CAP, bank, :], lhs(k), wcols(ng)[:, k, :], start=(k == 0), stop=(k == KC - 1))
                        mu = t.matmul(ps[CAP:P, bank, :], lhs(k), wcols(nu)[:, k, :], start=(k == 0), stop=(k == KC - 1))
                    if last:
                        mg.then_inc(used[slot(ng)], 1)
                        mu.then_inc(used[slot(nu)], 1)
                    return mu

                def down(j, lhs, bank):
                    n = n0 + 3 * j + 2
                    for f in range(4):
                        t.matmul(ps[0:CAP, bank, :], lhs(f), wdown(n)[:, f, 0:512], start=(f == 0), stop=(f == 3))
                        mm = t.matmul(ps[CAP:P, bank, :], lhs(f), wdown(n)[:, f, 512:D], start=(f == 0), stop=(f == 3))
                    return mm

                def add_back(lhs, yy):
                    for b in range(NB):
                        for q in range(2):
                            mm = t.matmul(ps[:, 2 * b + q, :], lhs(b), yy(q), start=False, stop=True,
                                          skip_group_check=True)
                    return mm

                def overflow(i, j):
                    n = pe.value_load(tabn[0:1, bass.ds(i * 2 + j, 1)], min_val=0, max_val=ROUNDS)
                    b = pe.value_load(tabb[0:1, bass.ds(i * 2 + j, 1)], min_val=0, max_val=2 * NE * ROUNDS)
                    with pe.If(n > 0):
                        with pe.Fori(b, b + n) as g:
                            k = g * 13
                            for w in range(3):
                                landed(pe, n0 + 3 * j + w, i)
                            pe.wait_ge(o_dve, k + 5)
                            for q in range(2):
                                for bb in range(NB):
                                    mm = t.matmul(ps[q * CAP:(q + 1) * CAP, 6, :], opick[:, bb, :],
                                                  h[:, bb, q * 512:q * 512 + 512], start=(bb == 0), stop=(bb == 1))
                            mm.then_inc(o_pe, 1)
                            pe.wait_ge(o_act, g * 4 + 1)
                            for q in range(4):
                                mm = t.transpose(ps[:, 7, q * P:(q + 1) * P], ox[:, q * P:(q + 1) * P], ident[:, :])
                            mm.then_inc(o_pe, 1)
                            pe.wait_ge(o_dve, k + 6)
                            gate_up(j, i, lambda kk: oxT[:, kk % 4, (kk // 4) * CAP:(kk // 4 + 1) * CAP],
                                    6, range(KC), False).then_inc(o_pe, 1)
                            pe.wait_ge(o_act, g * 4 + 2)
                            for q in range(4):
                                mm = t.transpose(ps[:, 7, q * P:(q + 1) * P], ox[:, q * P:(q + 1) * P], ident[:, :])
                            mm.then_inc(o_pe, 1)
                            pe.wait_ge(o_dve, k + 8)
                            down(j, lambda f: oaT[:, f * CAP:(f + 1) * CAP], 6).then_inc(o_pe, 1)
                            for bb in range(NB):
                                mm = t.transpose(ps[0:CAP, 7, bb * P:(bb + 1) * P], oput[:, bb, :], ident[:, :])
                            mm.then_inc(o_pe, 1)
                            pe.wait_ge(o_act, g * 4 + 4)
                            pe.wait_ge(o_dve, k + 10)
                            add_back(lambda bb: oputT[0:CAP, bb * P:(bb + 1) * P],
                                     lambda q: oy[0:CAP, q * 512:q * 512 + 512]).then_inc(o_pe, 1)

                pe.wait_ge(tab, l + 1)
                gather(9 * l)
                turn_tokens(9 * l)
                for bank in range(4):
                    t.matmul(ps[:, bank, :], ones[:, :], y[:, 0:512], start=True, stop=True)
                with pe.Fori(0, PAIRS) as i:
                    q = i + 8 * l
                    G = i + 9 * l
                    pe.wait_ge(xt_ev, (G + 1) * 2)
                    pe.wait_ge(tp_ev, q + 1)
                    overflow(i, 0)
                    pe.wait_ge(y_ev[0], (q + 1) * 2)
                    landed(pe, n0, i)
                    landed(pe, n0 + 1, i)
                    gate_up(0, i, lambda k: xT[:, k, 0:CAP], 4, range(KC), True)
                    pe.wait_ge(y_ev[1], (q + 1) * 2)
                    add_back(lambda b: putT[:, b * P:(b + 1) * P],
                             lambda qq: y[:, qq * 512:qq * 512 + 512]).then_inc(sc_mm, 1)
                    overflow(i, 1)
                    gather(G + 1)
                    landed(pe, n0 + 3, i)
                    landed(pe, n0 + 4, i)
                    gate_up(1, i, lambda k: xT[:, k, CAP:P], 5, range(4), False)
                    pe.wait_ge(gu_ev[0], q + 1)
                    for f in range(4):
                        mm = t.transpose(ps[:, 4, f * P:(f + 1) * P], gu[:, 0, f * P:(f + 1) * P], ident[:, :])
                    mm.then_inc(tg_mm[0], 1)
                    gate_up(1, i, lambda k: xT[:, k, CAP:P], 5, range(4, KC), True)
                    turn_tokens(G + 1)
                    pe.wait_ge(at_r[0], q + 1)
                    landed(pe, n0 + 2, i)
                    down(0, lambda f: aT[:, 0, f * CAP:(f + 1) * CAP], 4).then_inc(used[slot(n0 + 2)], 1)
                    pe.wait_ge(gu_ev[1], q + 1)
                    for f in range(4):
                        mm = t.transpose(ps[:, 5, f * P:(f + 1) * P], gu[:, 1, f * P:(f + 1) * P], ident[:, :])
                    mm.then_inc(tg_mm[1], 1)
                    pe.wait_ge(xt_ev, (G + 2) * 2)
                    pe.wait_ge(putted, (q + 1) * 4)
                    for b in range(NB):
                        mm = t.transpose(ps[:, 6, b * P:(b + 1) * P], put[:, b, :], ident[:, :])
                    mm.then_inc(tp_mm, 1)
                    pe.wait_ge(at_r[1], q + 1)
                    landed(pe, n0 + 5, i)
                    down(1, lambda f: aT[:, 1, f * CAP:(f + 1) * CAP], 5).then_inc(used[slot(n0 + 5)], 1)
                pe.wait_ge(tp_ev, 8 * (l + 1) + 1)
                pe.wait_ge(y_ev[0], (8 * (l + 1) + 1) * 2)
                pe.wait_ge(y_ev[1], (8 * (l + 1) + 1) * 2)
                add_back(lambda b: putT[:, b * P:(b + 1) * P],
                         lambda qq: y[:, qq * 512:qq * 512 + 512]).then_inc(sc_mm, 1)

            mod_product(0)
            modulate(0)
            u = turned_units(0, N_FOXQK, 4)
            unit_free(u)
            for k in range(KC):
                mm = t.matmul(ps[0:HF, 0, 0:S], wf[:, k, :], hT[:, k, :], start=(k == 0), stop=(k == KC - 1))
            mm.then_inc(pj_mm, 1)
            natural_units(u + 1, N_FOXV, 2)
            pe.wait_ge(pj_ev[0], pj_even(UNITS0))
            pe.wait_ge(pj_ev[1], pj_odd(UNITS0))
            pe.wait_ge(f_steps, 1)
            for hh in range(HF + 1):
                if hh < HF:
                    scores(hh, hh // 2, hh % 2, hh)
                if hh >= 1:
                    turn_probs(hh - 1, (hh - 1) % 2, 2 * hh)
                    fox_values(hh - 1)
                if hh in (3, 9):
                    mod_product(1 if hh == 3 else 2)
            pe.wait_ge(o_ev, HD)
            pe.wait_ge(pt_ev, HF)
            out_product(0)
            norm_vectors(0)
            modulate(1)
            route(0)
            experts(0)
            norm_vectors(1)
            mod_product(3)
            mod_product(4)
            modulate(2)
            pe.wait_ge(f_steps, 2)
            u = turned_units(UNITS0, N_KVK, 2)
            u = natural_units(u, N_KVV, 2)
            modulate(3)
            turned_units(u, N_WQ, 2)
            pe.wait_ge(pj_ev[0], pj_even(UNITS0 + 20))
            pe.wait_ge(pj_ev[1], pj_odd(UNITS0 + 20))
            for hd in range(HD + 1):
                if hd < HD:
                    scores(HF + 2 * hd, hd, 0, None)
                    scores(HF + 2 * hd + 1, hd, 1, None)
                if hd >= 1:
                    turn_probs(HF + hd - 1, 0, 2 * HF + 2 * hd)
                    diff_values(hd - 1)
                if hd in (2, 5):
                    mod_product(5 if hd == 2 else 6)
            pe.wait_ge(o_nrm, 1)
            pe.wait_ge(pt_ev, HF + HD)
            for k in range(KC):
                for b in range(NB):
                    o = (k % 2) * S + b * P
                    bank = {0: 0, 1: 1, 2: 2, 3: 3}[k // 2]
                    mm = t.transpose(ps[:, bank, o:o + P], h[:, b, k * P:(k + 1) * P], ident[:, :])
                if k % 2:
                    mm.then_inc(ot_mm, 1)
            pe.wait_ge(ot_ev, 4)
            out_product(1)
            norm_vectors(2)
            modulate(4)
            route(1)
            experts(1)
            norm_vectors(3)


_INS = ["x", "c", "ada_w", "ada_b", "ln_attn_g", "ln_attn_b", "ln_ffn_g", "ln_ffn_b", "fox_w_in", "fox_b_f", "fox_w_o",
        "kv_ada_w", "kv_ada_b", "kv_w", "diff_w_q", "diff_lambda", "diff_norm_g", "diff_w_o",
        "router_w", "router_b", "moe_w_gate", "moe_w_up", "moe_w_down"]
_OUTS = [((1, 256, 1024), "float32")]


def kernel(**inputs):
    import numpy as _np
    import concourse.bacc as _bacc
    from concourse import mybir as _mybir
    from concourse.bass_utils import run_bass_kernel_spmd as _run

    nc = _bacc.Bacc("TRN2", target_bir_lowering=False, num_devices=1)
    arrays, args = {}, []
    for name in _INS:
        a = _np.ascontiguousarray(inputs[name])
        arrays[f"in_{name}_dram"] = a
        args.append(nc.dram_tensor(f"in_{name}_dram", a.shape, _mybir.dt.from_np(a.dtype), kind="ExternalInput").ap())
    for i, (shape, dtype) in enumerate(_OUTS):
        dt = _mybir.dt.from_np(_np.dtype(dtype))
        args.append(nc.dram_tensor(f"out_{i}_dram", shape, dt, kind="ExternalOutput").ap())
    build(nc, *args)
    r = _run(nc, [arrays], core_ids=[0])
    return r.results[0]["out_0_dram"]
```

```python
import math
from contextlib import ExitStack

import concourse.bass as bass
from concourse import mybir

ALU = mybir.AluOpType
ACT = mybir.ActivationFunctionType
AX = mybir.AxisListType
F32 = mybir.dt.float32
I32 = mybir.dt.int32

P = 128
RING = 6
CAP = 64
BIG = 1e30
FAR = 1e33


def build(nc, x, c, ada_w, ada_b, ln_attn_g, ln_attn_b, ln_ffn_g, ln_ffn_b, fox_w_in, fox_b_f, fox_w_o,
          kv_ada_w, kv_ada_b, kv_w, diff_w_q, diff_lambda, diff_norm_g, diff_w_o,
          router_w, router_b, moe_w_gate, moe_w_up, moe_w_down, out):
    DEPTH, D, _ = ada_w.shape
    S = x.shape[1]
    NE = router_w.shape[1]
    FE = moe_w_gate.shape[3]
    HF = fox_b_f.shape[1]
    HD = D // (diff_norm_g.shape[1])
    KC = D // P
    NB = S // P
    NG, EG = 4, 4
    PAIRS = NE // 2
    ALPHA = (2 * DEPTH) ** 0.25
    EPS = 1e-5
    LAM_INIT = 0.8 - 0.6 * math.exp(-0.3 * 1)
    ROUNDS = S // CAP - 1
    QSCALE = 0.125
    assert (DEPTH, D, S, NE, FE, HF, HD) == (2, 1024, 256, 16, 512, 16, 8)

    ada_dram = [ada_w[0], kv_ada_w, ada_w[1]]
    pieces = []

    def ada_pieces(which, group):
        first = len(pieces)
        for b in range(4):
            col = 2048 * group + 512 * b
            pieces.append(ada_dram[which][:, col:col + 512].rearrange("(k p) n -> p k n", p=P))
        return first

    def col_pieces(w, lo, n):
        first = len(pieces)
        for b in range(n):
            pieces.append(w[:, lo + 512 * b:lo + 512 * b + 512].rearrange("(k p) n -> p k n", p=P))
        return first

    N_ADA = {}
    N_ADA[0] = ada_pieces(0, 0)
    N_FOXQK = col_pieces(fox_w_in[0], 0, 4)
    N_ADA[1] = ada_pieces(0, 1)
    N_FOXV = col_pieces(fox_w_in[0], 2048, 2)
    N_ADA[2] = ada_pieces(0, 2)
    N_ADA[3] = ada_pieces(1, 0)
    N_ADA[4] = ada_pieces(2, 0)
    N_WO = [col_pieces(fox_w_o[0], 0, 2), None]
    N_MOE = [len(pieces), None]
    pieces += [None] * (3 * NE)
    N_KVK = col_pieces(kv_w, 0, 2)
    N_KVV = col_pieces(kv_w, 1024, 2)
    N_WQ = col_pieces(diff_w_q[0], 0, 2)
    N_ADA[5] = ada_pieces(2, 1)
    N_ADA[6] = ada_pieces(2, 2)
    N_WO[1] = col_pieces(diff_w_o[0], 0, 2)
    N_MOE[1] = len(pieces)
    pieces += [None] * (3 * NE)

    def ada_row(layer_first, v):
        return layer_first + v // 2, 2 * (v % 2)
    ROW = {}
    for l, g0 in ((0, 0), (1, 4)):
        for v, name in enumerate(("sh_a", "sc_a", "g_a", "sh_f", "sc_f", "g_f")):
            ROW[name, l] = ada_row(g0, v)
        ROW["ln_a_g", l] = (7 + 2 * l, 0)
        ROW["ln_a_b", l] = (7 + 2 * l, 2)
        ROW["ln_f_g", l] = (8 + 2 * l, 0)
        ROW["ln_f_b", l] = (8 + 2 * l, 2)
    ROW["kv_sh"] = (3, 0)
    ROW["kv_sc"] = (3, 2)
    MODS = [(ROW["sc_a", 0], ROW["sh_a", 0]), (ROW["sc_f", 0], ROW["sh_f", 0]), (ROW["kv_sc"], ROW["kv_sh"]),
            (ROW["sc_a", 1], ROW["sh_a", 1]), (ROW["sc_f", 1], ROW["sh_f", 1])]

    with ExitStack() as ctx:
        def sb(name, shape, dt=F32):
            return ctx.enter_context(nc.sbuf_tensor(name, shape, dt))

        def sem(name):
            return ctx.enter_context(nc.semaphore(name))

        ring = sb("ring", [P, RING, 4096])
        xres = sb("xres", [P, NB, D])
        h = sb("h", [P, NB, D])
        hT = sb("hT", [P, KC, S])
        rows = sb("rows", [P, 11, 512])
        gbc = sb("gbc", [P, D])
        ident = sb("ident", [P, P])
        ones = sb("ones", [P, P])
        before = sb("before", [P, P])
        maskf = sb("maskf", [P, 3 * P])
        dist = sb("dist", [P, 3 * P])
        lane = sb("lane", [P, CAP])
        tri4 = sb("tri4", [P, EG, EG])
        ccol = sb("ccol", [P, KC])
        csig = sb("csig", [P, KC])
        strips = sb("strips", [P, 1])
        crep = sb("crep", [P, KC, 32])
        wf = sb("wf", [P, KC, HF])
        bf = sb("bf", [HF, 1])
        rw = sb("rw", [P, KC, NE])
        rb = sb("rb", [P, NE])
        lamin = sb("lamin", [P, 4, 64])
        lamt = sb("lamt", [P, 64])
        lam2 = sb("lam2", [P, 4])
        normg = sb("normg", [P, 1])
        st = sb("st", [P, 16])
        mhalf = sb("mhalf", [P, NB])
        fold = sb("fold", [P, 2, 512])
        tabn = sb("tabn", [1, NE], I32)
        tabb = sb("tabb", [1, NE], I32)
        rt = sb("rt", [P, 12, NB * NE])
        rg = sb("rg", [P, 6, 2 * 2 * 8])
        rc = sb("rc", [P, 3, NB * NG * EG * EG])
        gate = sb("gate", [P, NB, NE + 2])
        pos = sb("pos", [P, NB, NE + 2])
        cnt = sb("cnt", [1, 6, NE])
        arena = sb("arena", [P, 11264])
        ps = ctx.enter_context(nc.psum_tensor("ps", [P, 8, 512], F32))

        taken = [0]

        def part(rowcount, *shape):
            n = math.prod(shape)
            a = arena[0:rowcount, taken[0]:taken[0] + n]
            taken[0] += n
            assert taken[0] <= 11264
            names = "abc"[:len(shape)]
            if len(shape) == 1:
                return a
            return a.rearrange(f"p ({' '.join(names)}) -> p {' '.join(names)}",
                               **{names[i]: shape[i] for i in range(1, len(shape))})

        qT = part(P, KC, S)
        taken[0] = 0
        parts = part(P, 4, 512)
        osq = part(P, NB, P)
        kT = part(P, 2 * KC, S)
        v = part(P, NB, D)
        oT = hT
        lg = part(P, 4, 3 * P)
        lg_end = taken[0]
        pT = part(P, 2, 3 * P)
        ncum = part(P, 3 * P)
        negm = part(P, 4, 2)
        rs = part(P, 4, 2)
        rr = part(P, 4, 2)
        ss = part(P, HD, 4, NB)
        taken[0] = lg_end - 4 * 3 * P
        fz = part(HF, 4, S)
        taken[0] = 0
        xg = part(P, D)
        xT = part(P, KC, 2 * CAP)
        gu = part(P, 2, FE)
        sg = part(P, 2, 4, CAP)
        tg = part(P, 2, 4, CAP)
        aT = part(P, 2, 4 * CAP)
        y = part(P, D)
        pick = part(P, NB, 2 * CAP)
        put = part(P, NB, 2 * CAP)
        putT = part(P, S)
        opos = part(P, 2, NB)
        opick = part(P, NB, CAP)
        oput = part(P, NB, CAP)
        ox = part(P, FE)
        oxT = part(P, 4, 2 * CAP)
        osg = part(P, 4, CAP)
        oaT = part(P, 4 * CAP)
        oy = part(P, D)
        oputT = part(P, S)
        lng = part(P, D)
        lnb = oy

        full = [sem(f"full{i}") for i in range(RING)]
        used = [sem(f"used{i}") for i in range(RING)]
        x_in = sem("x_in")
        c_in = sem("c_in")
        small_in = sem("small_in")
        consts = sem("consts")
        csil = sem("csil")
        rows_zero = sem("rows_zero")
        rows_one = sem("rows_one")
        mod_row = sem("mod_row")
        fold_ch = sem("fold_ch")
        gate_mm = sem("gate_mm")
        fold_mm = sem("fold_mm")
        lnx_mm = sem("lnx_mm")
        y_mm = sem("y_mm")
        folded = sem("folded")
        h_ready = sem("h_ready")
        ht_mm = sem("ht_mm")
        ht_ready = [sem("ht_ready_act"), sem("ht_ready_dve")]
        bias0_in = sem("bias0_in")
        bias0 = sem("bias0")
        part_ev = [sem("part_ev_act"), sem("part_ev_dve")]
        ln_ev = sem("ln_ev")
        pj_mm = sem("pj_mm")
        pj_ev = [sem("pj_ev_act"), sem("pj_ev_dve")]
        lam_r = sem("lam_r")
        f_steps = sem("f_steps")
        f_act = sem("f_act")
        s_mm = sem("s_mm")
        s_ev = sem("s_ev")
        mx = sem("mx")
        ex = sem("ex")
        pn = sem("pn")
        pt_mm = sem("pt_mm")
        pt_ev = sem("pt_ev")
        pv_mm = sem("pv_mm")
        o_ev = sem("o_ev")
        o_rms = sem("o_rms")
        o_pow = sem("o_pow")
        normg_r = sem("normg_r")
        ot_mm = sem("ot_mm")
        ot_ev = sem("ot_ev")
        g_ev = sem("g_ev")
        r_sum = sem("r_sum")
        r_sq = sem("r_sq")
        r_std = sem("r_std")
        x_ready = sem("x_ready")
        rt_mm = sem("rt_mm")
        rt_dve = sem("rt_dve")
        rt_act = sem("rt_act")
        rt_mask = sem("rt_mask")
        tab = sem("tab")
        dch = sem("dch")
        pch = sem("pch")
        ach = sem("ach")
        picked = sem("picked")
        putted = sem("putted")
        ga_mm = sem("ga_mm")
        xg_ev = sem("xg_ev")
        tx_mm = sem("tx_mm")
        xt_ev = sem("xt_ev")
        gu_ev = [sem("gu_ev_a"), sem("gu_ev_b")]
        tg_mm = [sem("tg_mm_a"), sem("tg_mm_b")]
        sg_r = [sem("sg_r_a"), sem("sg_r_b")]
        tg_r = [sem("tg_r_a"), sem("tg_r_b")]
        at_r = [sem("at_r_a"), sem("at_r_b")]
        y_ev = [sem("y_ev_a"), sem("y_ev_b")]
        tp_mm = sem("tp_mm")
        tp_ev = sem("tp_ev")
        sc_mm = sem("sc_mm")
        o_pe = sem("o_pe")
        o_act = sem("o_act")
        o_dve = sem("o_dve")
        o_pos = sem("o_pos")
        stored = sem("stored")

        def slot(n):
            return n % RING

        def landed(eng, n, i=None):
            val = 16 * (n // RING + 1)
            eng.wait_ge(full[n % RING], val if i is None else i * 16 + val)

        def spent(eng, n, i=None):
            val = n // RING + 1
            eng.wait_ge(used[n % RING], val if i is None else i + val)

        class Chain:
            def __init__(self, eng, s):
                self.eng, self.sem, self.n = eng, s, 0

            def __call__(self, ins):
                ins.then_inc(self.sem, 1)
                self.n += 1
                self.eng.wait_ge(self.sem, self.n)

        def turn_bank(m):
            return 4 if m == 3 else 0

        def wcols(n):
            return ring[:, slot(n), :].rearrange("p (k n) -> p k n", k=KC)

        def wdown(n):
            return ring[:, slot(n), :].rearrange("p (k n) -> p k n", k=4)

        def sel(rowno):
            return ident[:, rowno:rowno + 1].broadcast_to([P, P])

        SMALL = 20

        UNITS0 = 8 + 8 + 1 + 4
        GATE_UNIT = 16
        pj_done = {}

        def number_units():
            count = [0]

            def unit(u, last_of):
                if last_of is None:
                    count[0] += 1
                    pj_done[u] = ("pj_mm", count[0])
                else:
                    pj_done[u] = ("piece", last_of)
            for u in range(16):
                unit(u, N_FOXQK + u // 4 if u % 4 == 3 else None)
            unit(GATE_UNIT, None)
            for u in range(4):
                unit(GATE_UNIT + 1 + u, N_FOXV + u // 2 if u % 2 else None)
            for u in range(8):
                unit(UNITS0 + u, N_KVK + u // 4 if u % 4 == 3 else None)
            for u in range(4):
                unit(UNITS0 + 8 + u, N_KVV + u // 2 if u % 2 else None)
            for u in range(8):
                unit(UNITS0 + 12 + u, N_WQ + u // 4 if u % 4 == 3 else None)
        number_units()

        def unit_filled(eng, u):
            kind, val = pj_done[u]
            if kind == "pj_mm":
                eng.wait_ge(pj_mm, val)
            else:
                spent(eng, val)

        def pj_even(n):
            return len([u for u in range(0, n, 2) if u != GATE_UNIT])

        def pj_odd(n):
            return n // 2

        def proj_units(l):
            if l == 0:
                us = [(u, "q", qT[:, u, :]) for u in range(8)]
                us += [(8 + u, "k", u) for u in range(8)]
                us += [(GATE_UNIT, "f", None)]
                us += [(GATE_UNIT + 1 + u, "v", v[:, u % 2, 512 * (u // 2):512 * (u // 2) + 512]) for u in range(4)]
                return us
            us = [(UNITS0 + u, "k", u) for u in range(8)]
            us += [(UNITS0 + 8 + u, "v", v[:, u % 2, 512 * (u // 2):512 * (u // 2) + 512]) for u in range(4)]
            us += [(UNITS0 + 12 + u, "q", qT[:, u, :]) for u in range(8)]
            return us

        block = ctx.enter_context(nc.Block())

        @block.sync
        def _(sp):
            def load(n):
                if n >= RING:
                    spent(sp, n - RING)
                sp.dma_start(wpiece(n), pieces[n]).then_inc(full[slot(n)], 16)

            def wpiece(n):
                return wcols(n) if len(pieces[n].shape) == 3 else ring[:, slot(n), :]

            def expert_loads(l):
                n0 = N_MOE[l]
                with sp.Fori(0, PAIRS) as i:
                    for j in range(6):
                        e = i * 2 + j // 3
                        sp.wait_ge(used[slot(n0 + j)], i + (n0 + j - RING) // RING + 1)
                        w = (moe_w_gate, moe_w_up, moe_w_down)[j % 3]
                        src = w[l, bass.ds(e, 1), :, :].rearrange("o (k p) n -> p (o k) n", p=P)
                        dst = (wcols, wcols, wdown)[j % 3](n0 + j)
                        sp.dma_start(dst, src).then_inc(full[slot(n0 + j)], 16)

            for n in range(N_MOE[0]):
                if 2 <= n < RING:
                    landed(sp, n - 2)
                load(n)
            expert_loads(0)
            for n in range(N_MOE[0] + 3 * NE, N_MOE[1]):
                load(n)
            expert_loads(1)
            for b in range(NB):
                sp.wait_ge(x_ready, 3 * NB + b + 1)
                sp.dma_start(out[0, b * P:(b + 1) * P, :], xres[:, b, :]).then_inc(stored, 16)
            sp.wait_ge(stored, 16 * NB)

        @block.gpsimd
        def _(pool):
            link = Chain(pool, pch)
            g = nc.gpsimd
            g.memset(rows[:, :, :], 0.0).then_inc(rows_zero, 1)
            link(g.memset(ident[:, :], 0.0))
            g.affine_select(out=ident[:, :], in_=ident[:, :], compare_op=ALU.not_equal, fill=1.0, base=0,
                            pattern=[[-1, P]], channel_multiplier=1).then_inc(consts, 1)
            link(g.memset(ones[:, :], 1.0))
            g.affine_select(out=before[:, :], in_=ones[:, :], compare_op=ALU.is_ge, fill=0.0, base=-1,
                            pattern=[[1, P]], channel_multiplier=-1).then_inc(consts, 1)
            link(g.memset(tri4[:, :, :], 1.0))
            g.affine_select(out=tri4[:, :, :], in_=tri4[:, :, :], compare_op=ALU.is_ge, fill=0.0, base=-1,
                            pattern=[[1, EG], [-1, EG]], channel_multiplier=0).then_inc(consts, 1)
            link(g.memset(maskf[:, :], 0.0))
            g.affine_select(out=maskf[:, 0:P], in_=maskf[:, 0:P], compare_op=ALU.is_ge, fill=-BIG, base=0,
                            pattern=[[-1, P]], channel_multiplier=1).then_inc(consts, 1)
            g.affine_select(out=maskf[:, 2 * P:], in_=maskf[:, 2 * P:], compare_op=ALU.is_ge, fill=-BIG, base=0,
                            pattern=[[-1, P]], channel_multiplier=1).then_inc(consts, 1)
            for t, base in enumerate((0, P, 0)):
                link(g.iota(dist[:, t * P:(t + 1) * P], pattern=[[-1, P]], base=base, channel_multiplier=1,
                            allow_small_or_imprecise_dtypes=True))
            for t in (0, 2):
                g.affine_select(out=dist[:, t * P:(t + 1) * P], in_=dist[:, t * P:(t + 1) * P],
                                compare_op=ALU.is_ge, fill=FAR, base=0,
                                pattern=[[-1, P]], channel_multiplier=1).then_inc(consts, 1)
            g.iota(lane[:, :], pattern=[[1, CAP]], base=0, channel_multiplier=0,
                   allow_small_or_imprecise_dtypes=True).then_inc(consts, 1)
            g.memset(mhalf[:, :], -0.5).then_inc(consts, 1)

            pool.wait_ge(consts, 9)

            def inv_std(norm):
                for b in range(NB):
                    u = 2 * norm + b
                    pool.wait_ge(r_sq, u + 1)
                    link(g.tensor_scalar(st[:, 6 + b:7 + b], st[:, 4 + b:5 + b], 1.0 / D, EPS, ALU.mult, ALU.add))
                    g.tensor_tensor(st[:, 8 + b:9 + b], st[:, 6 + b:7 + b], mhalf[:, 0:1], ALU.pow).then_inc(r_std, 1)
            def gained(norm):
                pool.wait_ge(ln_ev, 4 * (norm // 2 + 1))
                for b in range(NB):
                    link(g.tensor_tensor(xres[:, b, :], xres[:, b, :], lng, ALU.mult))
                    g.tensor_tensor(xres[:, b, :], xres[:, b, :], lnb, ALU.add).then_inc(x_ready, 1)
            inv_std(0)
            gained(0)
            inv_std(1)
            for hd in range(HD):
                pool.wait_ge(o_rms, NB * (hd + 1))
                link(g.tensor_scalar(ss[:, hd, 1, :], ss[:, hd, 0, :], 1.0 / P, EPS, ALU.mult, ALU.add))
                g.tensor_tensor(ss[:, hd, 2, :], ss[:, hd, 1, :], mhalf[:, :], ALU.pow).then_inc(o_pow, 1)
            inv_std(2)
            gained(2)
            inv_std(3)

        @block.scalar
        def _(act):
            a = nc.scalar
            link = Chain(act, ach)

            act.dma_start(ccol[:, :], c.rearrange("o (k p) -> p (o k)", p=P), allow_slow_non_contiguous=True).then_inc(c_in, 16)
            act.wait_ge(rows_zero, 1)
            for l, g0 in ((0, 0), (1, 4)):
                for gi in range(3):
                    act.dma_start(rows[0:97:32, g0 + gi, :],
                                  ada_b[l, 2048 * gi:2048 * gi + 2048].rearrange("(j n) -> j n", j=4)
                                  ).then_inc(bias0_in if g0 + gi == 0 else small_in, 16)
                for gi, (u, w) in enumerate(((ln_attn_g, ln_attn_b), (ln_ffn_g, ln_ffn_b))):
                    for hh, vec in enumerate((u, w)):
                        act.dma_start(rows[64 * hh:64 * hh + 33:32, 7 + 2 * l + gi, :],
                                      vec[l, :].rearrange("(j n) -> j n", j=2)).then_inc(small_in, 16)
            act.dma_start(rows[0:97:32, 3, :], kv_ada_b.rearrange("(j n) -> j n", j=4)).then_inc(small_in, 16)
            act.dma_start(wf[:, :, :], fox_w_in[0][:, 3 * D:3 * D + HF].rearrange("(k p) n -> p k n", p=P)).then_inc(small_in, 16)
            act.dma_start(bf[:, :], fox_b_f[0:1, :].rearrange("o n -> n o"), allow_slow_non_contiguous=True).then_inc(small_in, 16)
            act.dma_start(rw[:, :, :], router_w.rearrange("(k p) n -> p k n", p=P)).then_inc(small_in, 16)
            act.dma_start(rb[:, :], router_b.partition_broadcast(P)).then_inc(small_in, 16)
            act.dma_start(lamin[:, :, :], diff_lambda[0].partition_broadcast(P)).then_inc(small_in, 16)
            act.dma_start(normg[:, :], diff_norm_g.rearrange("o n -> n o"), allow_slow_non_contiguous=True).then_inc(small_in, 16)

            act.wait_ge(c_in, 16)
            a.activation(csig[:, :], ccol[:, :], ACT.Sigmoid).then_inc(csil, 1)
            landed(act, N_ADA[0] + 1)
            for b in range(NB):
                act.dma_start(xres[:, b, :], x[0, b * P:(b + 1) * P, :]).then_inc(x_in, 16)
            for j in (0, 2):
                spent(act, N_ADA[0] + j)
                a.activation(parts[:, j, :], ps[:, j, :], ACT.Copy).then_inc(part_ev[0], 1)

            def turned(m):
                for b in range(NB):
                    act.wait_ge(ht_mm, NB * m + b + 1)
                    a.activation(hT[:, 0:4, b * P:(b + 1) * P],
                                 ps[:, turn_bank(m) + 2 * b, :].rearrange("p (k s) -> p k s", k=4),
                                 ACT.Copy).then_inc(ht_ready[0], 1)

            def unit_out(u, dst, kind):
                if u % 2:
                    return
                unit_filled(act, u)
                if kind == "k":
                    cc = dst
                    link(a.activation(kT[0:64, 2 * cc, :], ps[0:64, u % 4, 0:S], ACT.Copy))
                    a.activation(kT[64:P, 2 * cc + 1, :], ps[64:P, u % 4, 0:S], ACT.Copy).then_inc(pj_ev[0], 1)
                elif kind == "q":
                    a.activation(dst, ps[:, u % 4, 0:S], ACT.Copy, scale=QSCALE).then_inc(pj_ev[0], 1)
                else:
                    a.activation(dst, ps[:, u % 4, :], ACT.Copy).then_inc(pj_ev[0], 1)

            def forget_gate():
                unit_filled(act, GATE_UNIT)
                act.wait_ge(small_in, 16 * SMALL)
                link(a.activation(fz[:, 0, :], ps[0:HF, 0, 0:S], ACT.Abs, bias=bf[:, 0:1]))
                link(a.activation(fz[:, 1, :], fz[:, 0, :], ACT.Exp, scale=-1.0))
                a.activation(fz[:, 2, :], fz[:, 1, :], ACT.Ln, bias=1.0).then_inc(f_act, 1)

            def exps(H):
                t = H % 4
                act.wait_ge(mx, 2 * (H + 1))
                a.activation(lg[:, t, 0:P], lg[:, t, 0:P], ACT.Exp, bias=negm[:, t, 0:1],
                             accum_out=rs[:, t, 0:1]).then_inc(ex, 1)
                a.activation(lg[:, t, P:3 * P], lg[:, t, P:3 * P], ACT.Exp, bias=negm[:, t, 1:2],
                             accum_out=rs[:, t, 1:2]).then_inc(ex, 1)

            def probs_out(T):
                act.wait_ge(pt_mm, T + 1)
                if T >= 2:
                    act.wait_ge(pv_mm, T - 1)
                a.activation(pT[:, T % 2, :], ps[:, 2 + T % 2, 0:3 * P], ACT.Copy).then_inc(pt_ev, 1)

            def gate_out(norm):
                act.wait_ge(gate_mm, norm + 1)
                for q in range(2):
                    a.activation(gbc[:, q * 512:q * 512 + 512], ps[:, 4 + q, :], ACT.Copy).then_inc(g_ev, 1)

            def norm_out(norm):
                act.wait_ge(lnx_mm, norm + 1)
                for q in range(4):
                    dst = (lng, lnb)[q // 2]
                    a.activation(dst[:, q % 2 * 512:q % 2 * 512 + 512], ps[:, 4 + q, :], ACT.Copy).then_inc(ln_ev, 1)

            def squares(norm):
                for b in range(NB):
                    u = 2 * norm + b
                    act.wait_ge(r_sum, u + 1)
                    a.activation(h[:, b, :], xres[:, b, :], ACT.Square, bias=st[:, 2 + b:3 + b],
                                 accum_out=st[:, 4 + b:5 + b]).then_inc(r_sq, 1)

            def router_exp(l):
                act.wait_ge(rt_dve, l + 1)
                a.activation(rt[:, 1, :], rt[:, 0, :], ACT.Exp).then_inc(rt_act, 1)

            def experts(l):
                n0 = N_MOE[l]

                def tokens_out(G):
                    act.wait_ge(ga_mm, G + 1)
                    a.activation(xg[:, 512:D], ps[:, 7, :], ACT.Copy).then_inc(xg_ev, 1)

                def turned_out(G):
                    act.wait_ge(tx_mm, G + 1)
                    a.activation(xT[:, 4:8, :].rearrange("p a b -> p (a b)"), ps[:, 7, :], ACT.Copy).then_inc(xt_ev, 1)

                def overflow(i, j):
                    n = act.value_load(tabn[0:1, bass.ds(i * 2 + j, 1)], min_val=0, max_val=ROUNDS)
                    b = act.value_load(tabb[0:1, bass.ds(i * 2 + j, 1)], min_val=0, max_val=2 * NE * ROUNDS)
                    with act.If(n > 0):
                        with act.Fori(b, b + n) as g:
                            act.wait_ge(o_pe, g * 7 + 1)
                            a.activation(ox[:, :], ps[:, 6, :], ACT.Copy).then_inc(o_act, 1)
                            act.wait_ge(o_pe, g * 7 + 3)
                            a.activation(ox[:, :], ps[:, 6, :], ACT.Copy).then_inc(o_act, 1)
                            act.wait_ge(o_pe, g * 7 + 4)
                            gt = ps[:, 7, :].rearrange("p (c s) -> p c s", c=4)
                            a.activation(osg[:, :, :], gt[:, :, 0:CAP], ACT.Sigmoid).then_inc(o_act, 1)
                            act.wait_ge(o_pe, g * 7 + 5)
                            act.wait_ge(x_ready, NB * (2 * l + 1))
                            a.activation(oy[0:CAP, 0:512], ps[0:CAP, 6, :], ACT.Copy).then_inc(o_act, 1)

                act.wait_ge(tab, l + 1)
                tokens_out(9 * l)
                turned_out(9 * l)
                with act.Fori(0, PAIRS) as i:
                    q = i + 8 * l
                    G = i + 9 * l
                    overflow(i, 0)
                    spent(act, n0 + 1, i)
                    a.activation(gu[:, 0, :], ps[:, 4, :], ACT.Copy).then_inc(gu_ev[0], 1)
                    overflow(i, 1)
                    tokens_out(G + 1)
                    act.wait_ge(tg_mm[0], q + 1)
                    gt = ps[:, 4, :].rearrange("p (c s) -> p c s", c=4)
                    a.activation(sg[:, 0, :, :], gt[:, :, 0:CAP], ACT.Sigmoid).then_inc(sg_r[0], 1)
                    spent(act, n0 + 4, i)
                    a.activation(gu[:, 1, :], ps[:, 5, :], ACT.Copy).then_inc(gu_ev[1], 1)
                    turned_out(G + 1)
                    act.wait_ge(tg_mm[1], q + 1)
                    gt = ps[:, 5, :].rearrange("p (c s) -> p c s", c=4)
                    a.activation(sg[:, 1, :, :], gt[:, :, 0:CAP], ACT.Sigmoid).then_inc(sg_r[1], 1)
                    act.wait_ge(sc_mm, i + (10 * l + 1))
                    spent(act, n0 + 2, i)
                    a.activation(y[0:CAP, 0:512], ps[0:CAP, 4, :], ACT.Copy).then_inc(y_ev[0], 1)
                    spent(act, n0 + 5, i)
                    a.activation(y[CAP:P, 0:512], ps[0:CAP, 5, :], ACT.Copy).then_inc(y_ev[1], 1)

            turned(0)
            for (u, kind, dst) in proj_units(0):
                if u == 16:
                    forget_gate()
                else:
                    unit_out(u, dst, kind)
            for t in range(HF + 2):
                if t < HF:
                    exps(t)
                if t >= 2:
                    probs_out(t - 2)
            gate_out(0)
            squares(0)
            turned(1)
            router_exp(0)
            norm_out(0)
            gate_out(1)
            experts(0)
            squares(1)
            turned(2)
            us = proj_units(1)
            for (u, kind, dst) in us[:12]:
                unit_out(u, dst, kind)
            turned(3)
            for (u, kind, dst) in us[12:]:
                unit_out(u, dst, kind)
            act.wait_ge(lam_r, 1)
            a.activation(lam2[:, 2:4], lam2[:, 0:2], ACT.Exp).then_inc(lam_r, 1)
            for t in range(HD + 3):
                if t < HD:
                    exps(HF + 2 * t)
                    exps(HF + 2 * t + 1)
                if 2 <= t < HD + 2:
                    probs_out(HF + t - 2)
                if t >= 3:
                    hd = t - 3
                    act.wait_ge(pv_mm, HF + hd + 1)
                    for b in range(NB):
                        a.activation(osq[:, b, :], ps[:, 4 + hd % 3, b * P:(b + 1) * P], ACT.Square,
                                     accum_out=ss[:, hd, 0, b:b + 1]).then_inc(o_rms, 1)
                        act.wait_ge(o_rms, NB * hd + b + 1)
            act.wait_ge(normg_r, 1)
            for q in range(2):
                act.wait_ge(ot_mm, 2 * q + 1)
                a.activation(oT[:, 4 * q:4 * q + 2, :].rearrange("p a b -> p (a b)"), ps[:, 2 * q, :],
                             ACT.Copy, scale=normg[:, 0:1]).then_inc(ot_ev, 1)
            gate_out(2)
            squares(2)
            turned(4)
            router_exp(1)
            norm_out(2)
            gate_out(3)
            experts(1)
            squares(3)

        @block.vector
        def _(dve):
            d = nc.vector
            link = Chain(dve, dch)
            Fold = Chain(dve, fold_ch)

            dve.sem_inc(y_ev[0], 2)
            dve.sem_inc(y_ev[1], 2)
            dve.sem_inc(tp_ev, 1)
            link(d.memset(kT[:, :, :], 0.0))
            link(d.memset(ncum[:, :], 0.0))
            dve.wait_ge(csil, 1)
            link(d.tensor_tensor(csig[:, :], csig[:, :], ccol[:, :], ALU.mult))
            d.tensor_copy(crep[:, :, :], csig[:, :].unsqueeze(2).broadcast_to([P, KC, 32])).then_inc(csil, 1)
            dve.wait_ge(bias0_in, 16)
            d.tensor_scalar(rows[64:P, 0, :], rows[64:P, 0, :], 1.0, None, ALU.add).then_inc(bias0, 1)
            dve.wait_ge(consts, 9)
            d.tensor_reduce(strips[:, :], ident[:, 0:P:32], AX.X, ALU.add).then_inc(bias0, 1)
            dve.wait_ge(small_in, 16 * SMALL)
            for g0 in (0, 4):
                if g0:
                    link(d.tensor_scalar(rows[64:P, g0, :], rows[64:P, g0, :], 1.0, None, ALU.add))
                link(d.tensor_scalar(rows[0:64, g0 + 1, :], rows[0:64, g0 + 1, :], 1.0, None, ALU.add))
                link(d.tensor_scalar(rows[:, g0 + 2, :], rows[:, g0 + 2, :], 1.0, None, ALU.add))
            link(d.tensor_scalar(rows[64:P, 3, :], rows[64:P, 3, :], 1.0, None, ALU.add))
            d.tensor_scalar(normg[:, :], normg[:, :], 1.0 - LAM_INIT, None, ALU.mult).then_inc(normg_r, 1)
            for t in range(2):
                link(d.tensor_tensor(lamt[:, :], lamin[:, 2 * t, :], lamin[:, 2 * t + 1, :], ALU.mult))
                ins = d.tensor_reduce(lam2[:, t:t + 1], lamt[:, :], AX.X, ALU.add)
                if t == 0:
                    link(ins)
                else:
                    ins.then_inc(lam_r, 1)

            def mod_rows(gi):
                for j in range(4):
                    spent(dve, N_ADA[gi] + j)
                d.tensor_tensor(rows[:, gi, :], rows[:, gi, :], ps[:, 7, :], ALU.add).then_inc(mod_row, 1)

            def fold_rows(m):
                (cg, cj), (sg_, sj) = MODS[m]
                norm = (None, 0, 1, 1, 2)[m]
                lg_, _ = ROW["ln_" + "af"[norm % 2] + "_g", norm // 2]
                c = rows[32 * cj:32 * cj + 64, cg, :]
                sh = rows[32 * sj:32 * sj + 64, sg_, :]
                t0, t1 = fold[32 * cj:32 * cj + 64, 0, :], fold[32 * cj:32 * cj + 64, 1, :]
                u1 = fold[32 * sj:32 * sj + 64, 1, :]
                f = Fold
                dve.wait_ge(mod_row, max(cg, sg_))
                if m >= 2:
                    dve.wait_ge(folded, m - 1)
                f(d.tensor_copy(t0, rows[64:P, lg_, :]))
                f(d.tensor_tensor(t1, t0, c, ALU.mult))
                f(d.tensor_copy(u1, t1))
                f(d.tensor_tensor(sh, sh, u1, ALU.add))
                f(d.tensor_copy(t0, rows[0:64, lg_, :]))
                d.tensor_tensor(c, c, t0, ALU.mult).then_inc(folded, 1)

            def streamed(m):
                dve.wait_ge(fold_mm, m + 1)
                fac = ps[:, 4:6, :].rearrange("p a b -> p (a b)")
                add = ps[:, 6:8, :].rearrange("p a b -> p (a b)")
                for b in range(NB):
                    if m in (1, 2, 4):
                        norm_block((None, 0, 1, None, 2)[m], b)
                    if m == 3:
                        dve.wait_ge(ht_mm, NB * 3)
                    link(d.tensor_tensor(h[:, b, :], xres[:, b, :], fac, ALU.mult))
                    d.tensor_tensor(h[:, b, :], h[:, b, :], add, ALU.add).then_inc(h_ready, 1)

            def turned(m):
                for b in range(NB):
                    dve.wait_ge(ht_mm, NB * m + b + 1)
                    d.tensor_copy(hT[:, 4:8, b * P:(b + 1) * P],
                                  ps[:, turn_bank(m) + 2 * b + 1, :].rearrange("p (k s) -> p k s", k=4)).then_inc(ht_ready[1], 1)

            def unit_out(u, dst, kind):
                if u % 2 == 0:
                    return
                unit_filled(dve, u)
                if kind == "k":
                    cc = dst
                    link(d.tensor_copy(kT[0:64, 2 * cc, :], ps[0:64, u % 4, 0:S]))
                    d.tensor_copy(kT[64:P, 2 * cc + 1, :], ps[64:P, u % 4, 0:S]).then_inc(pj_ev[1], 1)
                elif kind == "q":
                    d.tensor_scalar(dst, ps[:, u % 4, 0:S], QSCALE, None, ALU.mult).then_inc(pj_ev[1], 1)
                else:
                    d.tensor_copy(dst, ps[:, u % 4, :]).then_inc(pj_ev[1], 1)

            def forget_gate():
                dve.wait_ge(f_act, 1)
                link(d.tensor_scalar(fz[:, 0, :], ps[0:HF, 0, 0:S], bf[:, 0:1], 0.0, ALU.add, ALU.min))
                link(d.tensor_tensor(fz[:, 1, :], fz[:, 2, :], fz[:, 0, :], ALU.subtract))
                link(d.memset(fz[:, 3, :], 1.0))
                link(d.tensor_tensor_scan(ncum[0:HF, P:3 * P], fz[:, 3, :], fz[:, 1, :], 0.0, ALU.mult, ALU.add))
                d.tensor_copy(ncum[0:HF, 0:P], ncum[0:HF, P:2 * P]).then_inc(f_steps, 1)

            def soft(H, bias, factor):
                t = H % 4
                dve.wait_ge(s_mm, H + 1)
                link(d.scalar_tensor_tensor(out=lg[:, t, :], in0=bias[:, :], scalar=factor, in1=ps[:, H % 2, 0:3 * P],
                                            op0=ALU.mult, op1=ALU.add))
                d.tensor_reduce(negm[:, t, 0:1], lg[:, t, 0:P], AX.X, ALU.max, negate=True).then_inc(mx, 1)
                d.tensor_reduce(negm[:, t, 1:2], lg[:, t, P:3 * P], AX.X, ALU.max, negate=True).then_inc(mx, 1)

            def fox_norm(H):
                t = H % 4
                dve.wait_ge(ex, 2 * (H + 1))
                link(d.reciprocal(rr[:, t, :], rs[:, t, :]))
                d.tensor_scalar(lg[:, t, 0:P], lg[:, t, 0:P], rr[:, t, 0:1], None, ALU.mult).then_inc(pn, 1)
                d.tensor_scalar(lg[:, t, P:3 * P], lg[:, t, P:3 * P], rr[:, t, 1:2], None, ALU.mult).then_inc(pn, 1)

            def diff_norm(hd):
                dve.wait_ge(ex, 2 * (HF + 2 * hd + 2))
                t = 2 * (hd % 2)
                link(d.reciprocal(rr[:, t:t + 2, :], rs[:, t:t + 2, :]))
                link(d.tensor_scalar(rr[:, t + 1, :], rr[:, t + 1, :], lam2[:, 0:1], None, ALU.mult))
                for q, (lo, hi) in enumerate(((0, P), (P, 3 * P))):
                    link(d.tensor_scalar(lg[:, t, lo:hi], lg[:, t, lo:hi], rr[:, t, q:q + 1], None, ALU.mult))
                    d.scalar_tensor_tensor(out=lg[:, t, lo:hi], in0=lg[:, t + 1, lo:hi], scalar=rr[:, t + 1, q:q + 1],
                                           in1=lg[:, t, lo:hi], op0=ALU.mult, op1=ALU.add).then_inc(pn, 1)

            def norm_sums(norm, b):
                yb = ps[:, 2 * b:2 * b + 2, :].rearrange("p a b -> p (a b)")
                link(d.tensor_tensor(h[:, b, :], gbc[:, :], yb, ALU.mult))
                link(d.scalar_tensor_tensor(out=xres[:, b, :], in0=xres[:, b, :], scalar=ALPHA, in1=h[:, b, :],
                                            op0=ALU.mult, op1=ALU.add, accum_out=st[:, b:b + 1]))
                d.tensor_scalar(st[:, 2 + b:3 + b], st[:, b:b + 1], -1.0 / D, None, ALU.mult).then_inc(r_sum, 1)

            def norm_block(norm, b):
                dve.wait_ge(r_std, 2 * norm + b + 1)
                link(d.tensor_scalar(xres[:, b, :], xres[:, b, :], st[:, 2 + b:3 + b], st[:, 8 + b:9 + b],
                                     ALU.add, ALU.mult))

            def y_ready(norm, b):
                if norm % 2 == 0 and b == 0:
                    dve.wait_ge(y_mm, norm // 2 + 1)
                elif norm % 2 == 0:
                    spent(dve, N_WO[norm // 2])
                    spent(dve, N_WO[norm // 2] + 1)
                else:
                    dve.wait_ge(sc_mm, 10 * (norm // 2) + 9 + b)

            def post_norm(norm):
                dve.wait_ge(g_ev, 2 * (norm + 1))
                if norm:
                    dve.wait_ge(x_ready, NB * norm)
                for b in range(NB):
                    y_ready(norm, b)
                    norm_sums(norm, b)

            def gained(norm):
                dve.wait_ge(lnx_mm, norm + 1)
                lg_ = ps[:, 4:6, :].rearrange("p a b -> p (a b)")
                lb_ = ps[:, 6:8, :].rearrange("p a b -> p (a b)")
                for b in range(NB):
                    if norm == 3:
                        norm_block(3, b)
                    link(d.tensor_tensor(xres[:, b, :], xres[:, b, :], lg_, ALU.mult))
                    d.tensor_tensor(xres[:, b, :], xres[:, b, :], lb_, ALU.add).then_inc(x_ready, 1)

            def rank4(src, n, cmp, eq, dst):
                a4 = src.unsqueeze(2).broadcast_to([P, n, 4, 4])
                b4 = src.unsqueeze(3).broadcast_to([P, n, 4, 4])
                tri = tri4[:, :, :].unsqueeze(1).broadcast_to([P, n, 4, 4])
                link(d.tensor_tensor(cmp, a4, b4, ALU.is_gt))
                link(d.tensor_tensor(eq, a4, b4, ALU.is_equal))
                link(d.tensor_tensor(eq, eq, tri, ALU.mult))
                link(d.tensor_tensor(cmp, cmp, eq, ALU.add))
                link(d.tensor_reduce(dst, cmp, AX.X, ALU.add))

            def pick_pair(i):
                for b in range(NB):
                    for j in range(2):
                        d.tensor_scalar(pick[:, b, j * CAP:(j + 1) * CAP], lane[:, :],
                                        pos[:, b, bass.ds(i * 2 + j, 1)], None, ALU.is_equal).then_inc(picked, 1)

            def nothing_added():
                link(d.memset(putT[:, :], 0.0))
                link(d.memset(y[:, :], 0.0))

            def route(l):
                def t3(k):
                    return rt[:, k, :].rearrange("p (b e) -> p b e", b=NB)

                def t4(k):
                    return rt[:, k, :].rearrange("p (g e) -> p g e", e=EG)
                dve.wait_ge(rt_mm, 2 * l + 1)
                lgt = ps[:, 0, 0:NB * NE]
                mxr = st[:, 10:12]
                link(d.tensor_copy(rt[:, 2, :], lgt))
                link(d.tensor_reduce(mxr, t3(2), AX.X, ALU.max))
                d.tensor_tensor(t3(0), t3(2), mxr.unsqueeze(2).broadcast_to([P, NB, NE]), ALU.subtract).then_inc(rt_dve, 1)
                dve.wait_ge(rt_act, l + 1)
                link(d.tensor_reduce(st[:, 12:14], t3(1), AX.X, ALU.add))
                link(d.reciprocal(st[:, 12:14], st[:, 12:14]))
                link(d.tensor_tensor(t3(3), t3(1), st[:, 12:14].unsqueeze(2).broadcast_to([P, NB, NE]), ALU.mult))
                link(d.tensor_tensor(t3(4), t3(3), rb[:, :].unsqueeze(1).broadcast_to([P, NB, NE]), ALU.add))
                A, B = t4(4)[:, :, 0:4:2], t4(4)[:, :, 1:4:2]
                hi = rg[:, 0, 0:16].rearrange("p (g e) -> p g e", e=2)
                lo = rg[:, 1, 0:16].rearrange("p (g e) -> p g e", e=2)
                link(d.tensor_tensor(hi, A, B, ALU.max))
                link(d.tensor_tensor(lo, A, B, ALU.min))
                m1, x1, x2 = rg[:, 2, 0:8], rg[:, 3, 0:8], rg[:, 4, 0:8]
                link(d.tensor_tensor(m1, hi[:, :, 0], hi[:, :, 1], ALU.max))
                link(d.tensor_tensor(x1, hi[:, :, 0], hi[:, :, 1], ALU.min))
                link(d.tensor_tensor(x2, lo[:, :, 0], lo[:, :, 1], ALU.max))
                link(d.tensor_tensor(x1, x1, x2, ALU.max))
                link(d.tensor_tensor(m1, m1, x1, ALU.add))
                gsum = m1.rearrange("p (b g) -> p b g", b=NB)
                c2 = [rc[:, k, 0:NB * 16].rearrange("p (n i j) -> p n i j", i=4, j=4) for k in range(2)]
                rank4(gsum, NB, c2[0], c2[1], rg[:, 5, 0:8].rearrange("p (b g) -> p b g", b=NB))
                link(d.tensor_scalar(rg[:, 5, 0:8], rg[:, 5, 0:8], 0.5, None, ALU.is_lt))
                c8 = [rc[:, k, :].rearrange("p (n i j) -> p n i j", i=4, j=4) for k in range(2)]
                rank4(t4(4), NB * NG, c8[0], c8[1], t4(5))
                link(d.tensor_scalar(rt[:, 5, :], rt[:, 5, :], 1.5, None, ALU.is_lt))
                link(d.tensor_tensor(t4(6), t4(5), rg[:, 5, 0:8].unsqueeze(2).broadcast_to([P, NB * NG, EG]), ALU.mult))
                d.tensor_copy(rt[:, 7, :], rt[:, 6, :]).then_inc(rt_mask, 1)
                link(d.tensor_tensor(rt[:, 8, :], rt[:, 3, :], rt[:, 6, :], ALU.mult))
                link(d.tensor_reduce(st[:, 14:16], t3(8), AX.X, ALU.add))
                link(d.reciprocal(st[:, 14:16], st[:, 14:16]))
                link(d.memset(gate[:, :, :], 0.0))
                link(d.memset(pos[:, :, :], -1.0))
                link(d.tensor_tensor(gate[:, :, 0:NE], t3(8), st[:, 14:16].unsqueeze(2).broadcast_to([P, NB, NE]), ALU.mult))
                dve.wait_ge(rt_mm, 2 * l + 2)
                link(d.scalar_tensor_tensor(out=rt[:, 9, :], in0=ps[:, 0, NB * NE:2 * NB * NE], scalar=1.0, in1=rt[:, 6, :],
                                            op0=ALU.add, op1=ALU.mult))
                link(d.tensor_scalar(pos[:, :, 0:NE], t3(9), -1.0, None, ALU.add))
                pick_pair(0)
                tot = ps[0:1, 0, 2 * NB * NE:2 * NB * NE + NE]
                link(d.tensor_scalar(cnt[:, 0, :], tot, float(CAP) + 0.5, None, ALU.is_gt))
                for r in range(2, ROUNDS + 1):
                    link(d.tensor_scalar(cnt[:, 1, :], tot, r * float(CAP) + 0.5, None, ALU.is_gt))
                    link(d.tensor_tensor(cnt[:, 0, :], cnt[:, 0, :], cnt[:, 1, :], ALU.add))
                link(d.memset(cnt[:, 2, :], 1.0))
                start = 0.0 if l == 0 else cnt[:, 5, 0:1]
                link(d.tensor_tensor_scan(cnt[:, 3, :], cnt[:, 2, :], cnt[:, 0, :], start, ALU.mult, ALU.add))
                link(d.tensor_tensor(cnt[:, 4, :], cnt[:, 3, :], cnt[:, 0, :], ALU.subtract))
                link(d.tensor_copy(cnt[:, 5, 0:1], cnt[:, 3, NE - 1:NE]))
                link(d.tensor_copy(tabn[:, :], cnt[:, 0, :]))
                d.tensor_copy(tabb[:, :], cnt[:, 4, :]).then_inc(tab, 1)
                dve.wait_ge(tab, l + 1)

            def experts(l):
                n0 = N_MOE[l]

                def put_pair(i):
                    for b in range(NB):
                        for j in range(2):
                            d.tensor_scalar(put[:, b, j * CAP:(j + 1) * CAP], lane[:, :],
                                            pos[:, b, bass.ds(i * 2 + j, 1)], gate[:, b, bass.ds(i * 2 + j, 1)],
                                            ALU.is_equal, ALU.mult).then_inc(putted, 1)

                def tokens_out(G):
                    dve.wait_ge(ga_mm, G + 1)
                    d.tensor_copy(xg[:, 0:512], ps[:, 6, :]).then_inc(xg_ev, 1)

                def turned_out(G):
                    dve.wait_ge(tx_mm, G + 1)
                    d.tensor_copy(xT[:, 0:4, :].rearrange("p a b -> p (a b)"), ps[:, 6, :]).then_inc(xt_ev, 1)

                def glu(j, q):
                    gt = ps[:, 4 + j, :].rearrange("p (c s) -> p c s", c=4)
                    dve.wait_ge(sg_r[j], q + 1)
                    d.tensor_tensor(tg[:, j, :, :], sg[:, j, :, :], gt[:, :, 0:CAP], ALU.mult).then_inc(tg_r[j], 1)
                    dve.wait_ge(tg_r[j], q + 1)
                    d.tensor_tensor(aT[:, j, :].rearrange("p (c s) -> p c s", c=4), tg[:, j, :, :],
                                    gt[:, :, CAP:2 * CAP], ALU.mult).then_inc(at_r[j], 1)

                def overflow(i, j):
                    e = i * 2 + j
                    n = dve.value_load(tabn[0:1, bass.ds(e, 1)], min_val=0, max_val=ROUNDS)
                    b0 = dve.value_load(tabb[0:1, bass.ds(e, 1)], min_val=0, max_val=2 * NE * ROUNDS)
                    d.tensor_copy(opos[:, j, :].unsqueeze(2), pos[:, :, bass.ds(e, 1)]).then_inc(o_pos, 1)
                    with dve.If(n > 0):
                        with dve.Fori(b0, b0 + n) as g:
                            k = g * 13
                            dve.wait_ge(o_pos, i * 2 + (16 * l + j + 1))
                            d.tensor_scalar(opos[:, j, :], opos[:, j, :], -float(CAP), None, ALU.add).then_inc(o_dve, 1)
                            dve.wait_ge(o_dve, k + 1)
                            for b in range(NB):
                                d.tensor_scalar(opick[:, b, :], lane[:, :], opos[:, j, b:b + 1], None,
                                                ALU.is_equal).then_inc(o_dve, 1)
                                d.tensor_scalar(oput[:, b, :], lane[:, :], opos[:, j, b:b + 1],
                                                gate[:, b, bass.ds(e, 1)], ALU.is_equal, ALU.mult).then_inc(o_dve, 1)
                            dve.wait_ge(o_pe, g * 7 + 2)
                            d.tensor_copy(oxT[:, :, :].rearrange("p a b -> p (a b)"), ps[:, 7, :]).then_inc(o_dve, 1)
                            dve.wait_ge(o_act, g * 4 + 3)
                            gt = ps[:, 7, :].rearrange("p (c s) -> p c s", c=4)
                            d.tensor_tensor(osg[:, :, :], osg[:, :, :], gt[:, :, 0:CAP], ALU.mult).then_inc(o_dve, 1)
                            dve.wait_ge(o_dve, k + 7)
                            d.tensor_tensor(oaT.rearrange("p (c s) -> p c s", c=4), osg[:, :, :],
                                            gt[:, :, CAP:2 * CAP], ALU.mult).then_inc(o_dve, 1)
                            dve.wait_ge(o_pe, g * 7 + 5)
                            dve.wait_ge(x_ready, NB * (2 * l + 1))
                            d.tensor_copy(oy[0:CAP, 512:D], ps[CAP:P, 6, :]).then_inc(o_dve, 1)
                            dve.wait_ge(o_pe, g * 7 + 6)
                            d.tensor_copy(oputT[0:CAP, :], ps[0:CAP, 7, 0:S]).then_inc(o_dve, 1)
                            dve.wait_ge(o_pe, g * 7 + 7)
                            dve.sem_inc(o_dve, 3)
                            dve.wait_ge(o_dve, k + 13)

                tokens_out(9 * l)
                turned_out(9 * l)
                with dve.Fori(0, PAIRS) as i:
                    q = i + 8 * l
                    G = i + 9 * l
                    overflow(i, 0)
                    dve.wait_ge(ga_mm, G + 1)
                    pick_pair(i + 1)
                    put_pair(i)
                    overflow(i, 1)
                    tokens_out(G + 1)
                    glu(0, q)
                    turned_out(G + 1)
                    glu(1, q)
                    dve.wait_ge(sc_mm, i + (10 * l + 1))
                    dve.wait_ge(tp_mm, q + 1)
                    d.tensor_copy(putT[:, :], ps[:, 6, 0:S]).then_inc(tp_ev, 1)
                    spent(dve, n0 + 2, i)
                    d.tensor_copy(y[0:CAP, 512:D], ps[CAP:P, 4, :]).then_inc(y_ev[0], 1)
                    spent(dve, n0 + 5, i)
                    d.tensor_copy(y[CAP:P, 512:D], ps[CAP:P, 5, :]).then_inc(y_ev[1], 1)

            for j in (1, 3):
                spent(dve, N_ADA[0] + j)
                d.tensor_copy(parts[:, j, :], ps[:, j, :]).then_inc(part_ev[1], 1)
            dve.wait_ge(x_in, 16 * NB)
            streamed(0)
            turned(0)
            for (u, kind, dst) in proj_units(0):
                if u == GATE_UNIT:
                    mod_rows(1)
                    forget_gate()
                else:
                    unit_out(u, dst, kind)
            mod_rows(2)
            for t in range(HF + 5):
                if t < HF:
                    if t >= 4:
                        dve.wait_ge(pt_mm, t - 3)
                    soft(t, maskf, 1.0)
                if 1 <= t <= HF:
                    fox_norm(t - 1)
                if t >= 5 and t % 2:
                    pair = (t - 5) // 2
                    dve.wait_ge(pv_mm, 2 * pair + 2)
                    d.tensor_copy(oT[:, pair, :], ps[:, 4 + pair % 2, 0:S]).then_inc(o_ev, 1)
                if t in (5, 11):
                    mod_rows(3 if t == 5 else 4)
            nothing_added()
            dve.wait_ge(gate_mm, 1)
            for m in (1, 2, 3):
                fold_rows(m)
            post_norm(0)
            streamed(1)
            turned(1)
            route(0)
            experts(0)
            post_norm(1)
            streamed(2)
            turned(2)
            us = proj_units(1)
            link(d.memset(kT[:, :, :], 0.0))
            d.memset(ncum[:, 0:1], 0.0).then_inc(f_steps, 1)
            streamed(3)
            for (u, kind, dst) in us[:8]:
                unit_out(u, dst, kind)
            gained(1)
            for (u, kind, dst) in us[8:12]:
                unit_out(u, dst, kind)
            turned(3)
            for (u, kind, dst) in us[12:]:
                unit_out(u, dst, kind)
            dve.wait_ge(lam_r, 2)
            link(d.scalar_tensor_tensor(out=lam2[:, 0:1], in0=lam2[:, 2:3], scalar=-1.0, in1=lam2[:, 3:4],
                                        op0=ALU.mult, op1=ALU.add))
            link(d.tensor_scalar(lam2[:, 0:1], lam2[:, 0:1], -LAM_INIT, None, ALU.add))
            for t in range(HD + 4):
                if t < HD:
                    slope = -(2.0 ** (-8.0 * (t + 1) / HD))
                    if t >= 2:
                        dve.wait_ge(pt_mm, HF + t - 1)
                    soft(HF + 2 * t, dist, slope)
                    soft(HF + 2 * t + 1, dist, slope)
                if 1 <= t <= HD:
                    diff_norm(t - 1)
                if t >= 4:
                    hd = t - 4
                    dve.wait_ge(o_pow, hd + 1)
                    for b in range(NB):
                        d.tensor_scalar(h[:, b, hd * P:(hd + 1) * P], ps[:, 4 + hd % 3, b * P:(b + 1) * P],
                                        ss[:, hd, 2, b:b + 1], None, ALU.mult).then_inc(o_ev, 1)
                if t in (3, 6):
                    mod_rows(5 if t == 3 else 6)
            for q in range(2):
                dve.wait_ge(ot_mm, 2 * q + 2)
                d.tensor_scalar(oT[:, 4 * q + 2:4 * q + 4, :].rearrange("p a b -> p (a b)"), ps[:, 2 * q + 1, :],
                                normg[:, 0:1], None, ALU.mult).then_inc(ot_ev, 1)
            nothing_added()
            dve.wait_ge(gate_mm, 3)
            fold_rows(4)
            post_norm(2)
            streamed(4)
            turned(4)
            route(1)
            experts(1)
            post_norm(3)
            gained(3)

        @block.tensor
        def _(pe):
            t = nc.tensor

            def mod_product(gi):
                n = N_ADA[gi]
                for j in range(4):
                    landed(pe, n + j)
                if gi == 1:
                    pe.wait_ge(h_ready, 2)
                else:
                    pe.wait_ge(mod_row, gi - 1)
                if gi == 5:
                    stream_turned(3)
                for k in range(KC):
                    for j in range(4):
                        mm = t.matmul(ps[32 * j:32 * j + 32, 7, :], crep[:, k, :], wcols(n + j)[:, k, :],
                                      start=(k == 0), stop=(k == KC - 1))
                        if k == KC - 1:
                            mm.then_inc(used[slot(n + j)], 1)

            def first_modulation():
                pe.wait_ge(consts, 9)
                pe.wait_ge(bias0, 2)
                (cg, cj), (sg_, sj) = MODS[0]
                bank = {}
                for first, j0 in ((4, cj), (6, sj)):
                    for q in range(2):
                        bank[j0 + q] = first + q
                        t.matmul(ps[:, first + q, :], sel(32 * (j0 + q)), rows[:, 0, :], start=True, stop=False)
                pe.wait_ge(csil, 2)
                for j in range(4):
                    n = N_ADA[0] + j
                    landed(pe, n)
                    for k in range(2):
                        for strip in range(4):
                            mm = t.matmul(ps[32 * strip:32 * strip + 32, j, :], crep[:, 2 * strip + k, :],
                                          wcols(n)[:, 2 * strip + k, :], start=(k == 0), stop=(k == 1))
                    mm.then_inc(used[slot(n)], 1)
                for j in range(4):
                    pe.wait_ge(part_ev[j % 2], j // 2 + 1)
                    mm = t.matmul(ps[:, bank[j], :], strips[:, :].broadcast_to([P, P]), parts[:, j, :],
                                  start=False, stop=True)
                mm.then_inc(fold_mm, 1)

            def spread(row, bank):
                gi, j = row
                for q in range(2):
                    mm = t.matmul(ps[:, bank + q, :], sel(32 * (j + q)), rows[:, gi, :], start=True, stop=True)
                return mm

            def spread_gate(norm):
                pe.wait_ge(mod_row, ROW["g_" + "af"[norm % 2], norm // 2][0])
                spread(ROW["g_" + "af"[norm % 2], norm // 2], 4).then_inc(gate_mm, 1)

            def spread_fold(m):
                pe.wait_ge(folded, m)
                spread(MODS[m][0], 4)
                spread(MODS[m][1], 6).then_inc(fold_mm, 1)

            def spread_norm(norm):
                name, l = "af"[norm % 2], norm // 2
                spread(ROW["ln_" + name + "_g", l], 4)
                spread(ROW["ln_" + name + "_b", l], 6).then_inc(lnx_mm, 1)

            def turn_stream(m):
                for b in range(NB):
                    pe.wait_ge(h_ready, 2 * m + b + 1)
                    for k in range(KC):
                        o = (k % 4) * P
                        mm = t.transpose(ps[:, turn_bank(m) + 2 * b + k // 4, o:o + P], h[:, b, k * P:(k + 1) * P], ident[:, :])
                    mm.then_inc(ht_mm, 1)

            def stream_turned(m, b=NB - 1):
                for s_ in range(2):
                    pe.wait_ge(ht_ready[s_], NB * m + b + 1)

            def unit_free(u):
                if u >= 4 and u - UNITS0 not in (0, 1, 2, 3):
                    if u - 4 == GATE_UNIT:
                        pe.wait_ge(f_steps, 1)
                    else:
                        pe.wait_ge(pj_ev[u % 2], pj_even(u - 3) if u % 2 == 0 else pj_odd(u - 3))

            def turned_units(u, n, pieces_):
                for s_ in range(pieces_):
                    landed(pe, n + s_)
                    for cc in range(4):
                        unit_free(u)
                        for k in range(KC):
                            mm = t.matmul(ps[:, u % 4, 0:S], wcols(n + s_)[:, k, cc * P:(cc + 1) * P], hT[:, k, :],
                                          start=(k == 0), stop=(k == KC - 1))
                        mm.then_inc(used[slot(n + s_)] if cc == 3 else pj_mm, 1)
                        u += 1
                return u

            def natural_units(u, n, pieces_):
                for s_ in range(pieces_):
                    landed(pe, n + s_)
                    for b in range(NB):
                        unit_free(u)
                        for k in range(KC):
                            mm = t.matmul(ps[:, u % 4, :], hT[:, k, b * P:(b + 1) * P], wcols(n + s_)[:, k, :],
                                          start=(k == 0), stop=(k == KC - 1))
                        mm.then_inc(used[slot(n + s_)] if b == 1 else pj_mm, 1)
                        u += 1
                return u

            def scores(H, chunk, half, head):
                bank = H % 2
                if H >= 2:
                    pe.wait_ge(mx, 2 * (H - 1))
                if head is not None:
                    t.matmul(ps[:, bank, 0:3 * P], sel(head), ncum[:, :], start=True, stop=True)
                first = head is None
                kk = kT[:, 2 * chunk + half, :]
                t.matmul(ps[:, bank, 0:P], qT[:, chunk, 0:P], kk[:, 0:P], start=first, stop=True,
                         skip_group_check=True)
                t.matmul(ps[:, bank, P:3 * P], qT[:, chunk, P:2 * P], kk, start=first, stop=True,
                         skip_group_check=True).then_inc(s_mm, 1)

            def turn_probs(T, buf, pn_count):
                pe.wait_ge(pn, pn_count)
                if T >= 2:
                    pe.wait_ge(pt_ev, T - 1)
                for q in range(3):
                    mm = t.transpose(ps[:, 2 + T % 2, q * P:(q + 1) * P], lg[:, buf, q * P:(q + 1) * P], ident[:, :])
                mm.then_inc(pt_mm, 1)

            def fox_values(hh):
                pair = hh // 2
                lo = 64 * (hh % 2)
                bank = 4 + pair % 2
                pe.wait_ge(pt_ev, hh + 1)
                if hh % 2 == 0 and pair >= 2:
                    pe.wait_ge(o_ev, pair - 1)
                t.matmul(ps[lo:lo + 64, bank, 0:S], v[:, 0, 64 * hh:64 * hh + 64], pT[:, hh % 2, 0:S],
                         start=True, stop=True)
                t.matmul(ps[lo:lo + 64, bank, P:S], v[:, 1, 64 * hh:64 * hh + 64], pT[:, hh % 2, S:S + P],
                         start=False, stop=True, skip_group_check=True).then_inc(pv_mm, 1)

            def diff_values(hd):
                T = HF + hd
                bank = 4 + hd % 3
                pe.wait_ge(pt_ev, T + 1)
                if hd >= 3:
                    pe.wait_ge(o_ev, HD + 2 * (hd - 2))
                vv = [v[:, b, hd * P:(hd + 1) * P] for b in range(NB)]
                t.matmul(ps[:, bank, 0:P], pT[:, T % 2, 0:P], vv[0], start=True, stop=True)
                t.matmul(ps[:, bank, P:S], pT[:, T % 2, P:S], vv[0], start=True, stop=False)
                t.matmul(ps[:, bank, P:S], pT[:, T % 2, S:S + P], vv[1], start=False, stop=True).then_inc(pv_mm, 1)

            def out_product(l):
                n = N_WO[l]
                norm = 2 * l
                spread_gate(norm)
                landed(pe, n)
                landed(pe, n + 1)
                for b in range(NB):
                    for s_ in range(2):
                        for k in range(KC):
                            mm = t.matmul(ps[:, 2 * b + s_, :], oT[:, k, b * P:(b + 1) * P], wcols(n + s_)[:, k, :],
                                          start=(k == 0), stop=(k == KC - 1))
                        if b == 0 and s_ == 1:
                            mm.then_inc(y_mm, 1)
                            pe.wait_ge(g_ev, 2 * (norm + 1))
                            spread_fold((1, None, 4)[norm])
                        if b == 1 and s_ == 0:
                            mm.then_inc(used[slot(n)], 1)
                mm.then_inc(used[slot(n + 1)], 1)

            def route(l):
                m = (1, 4)[l]
                for b in range(NB):
                    stream_turned(m, b)
                    for k in range(KC):
                        mm = t.matmul(ps[:, 0, b * NE:(b + 1) * NE], hT[:, k, b * P:(b + 1) * P], rw[:, k, :],
                                      start=(k == 0), stop=(k == KC - 1))
                mm.then_inc(rt_mm, 1)
                spread_norm(2 * l)
                for bank in (1, 2, 3):
                    t.matmul(ps[:, bank, :], ones[:, :], y[:, 0:512], start=True, stop=True)
                pe.wait_ge(ln_ev, 4 * (l + 1))
                spread_gate(2 * l + 1)
                pe.wait_ge(rt_mask, l + 1)
                m0, m1 = rt[:, 7, 0:NE], rt[:, 7, NE:2 * NE]
                ra, rb_, tt = (ps[:, 0, o:o + NE] for o in (NB * NE, (NB + 1) * NE, 2 * NB * NE))
                t.matmul(ra, before[:, :], m0, start=True, stop=True)
                t.matmul(rb_, ones[:, :], m0, start=True, stop=False)
                t.matmul(rb_, before[:, :], m1, start=False, stop=True)
                t.matmul(tt, ones[:, :], m0, start=True, stop=False)
                t.matmul(tt, ones[:, :], m1, start=False, stop=True).then_inc(rt_mm, 1)

            def experts(l):
                n0 = N_MOE[l]

                def gather(G):
                    pe.wait_ge(picked, (G + 1) * 4)
                    for q in range(2):
                        for b in range(NB):
                            mm = t.matmul(ps[:, 6 + q, :], pick[:, b, :], h[:, b, q * 512:q * 512 + 512],
                                          start=(b == 0), stop=(b == NB - 1))
                    mm.then_inc(ga_mm, 1)

                def turn_tokens(G):
                    pe.wait_ge(xg_ev, (G + 1) * 2)
                    for k in range(KC):
                        mm = t.transpose(ps[:, 6 + k // 4, (k % 4) * P:(k % 4 + 1) * P], xg[:, k * P:(k + 1) * P], ident[:, :])
                    mm.then_inc(tx_mm, 1)

                def gate_up(j, i, lhs, bank, ks, last):
                    ng, nu = n0 + 3 * j, n0 + 3 * j + 1
                    for k in ks:
                        mg = t.matmul(ps[0:CAP, bank, :], lhs(k), wcols(ng)[:, k, :], start=(k == 0), stop=(k == KC - 1))
                        mu = t.matmul(ps[CAP:P, bank, :], lhs(k), wcols(nu)[:, k, :], start=(k == 0), stop=(k == KC - 1))
                    if last:
                        mg.then_inc(used[slot(ng)], 1)
                        mu.then_inc(used[slot(nu)], 1)
                    return mu

                def down(j, lhs, bank):
                    n = n0 + 3 * j + 2
                    for f in range(4):
                        t.matmul(ps[0:CAP, bank, :], lhs(f), wdown(n)[:, f, 0:512], start=(f == 0), stop=(f == 3))
                        mm = t.matmul(ps[CAP:P, bank, :], lhs(f), wdown(n)[:, f, 512:D], start=(f == 0), stop=(f == 3))
                    return mm

                def add_back(lhs, yy, blocks=range(NB)):
                    for b in blocks:
                        for q in range(2):
                            mm = t.matmul(ps[:, 2 * b + q, :], lhs(b), yy(q), start=False, stop=True,
                                          skip_group_check=True)
                    return mm

                def overflow(i, j):
                    n = pe.value_load(tabn[0:1, bass.ds(i * 2 + j, 1)], min_val=0, max_val=ROUNDS)
                    b = pe.value_load(tabb[0:1, bass.ds(i * 2 + j, 1)], min_val=0, max_val=2 * NE * ROUNDS)
                    with pe.If(n > 0):
                        with pe.Fori(b, b + n) as g:
                            k = g * 13
                            pe.wait_ge(o_dve, k + 5)
                            for q in range(2):
                                for bb in range(NB):
                                    mm = t.matmul(ps[q * CAP:(q + 1) * CAP, 6, :], opick[:, bb, :],
                                                  h[:, bb, q * 512:q * 512 + 512], start=(bb == 0), stop=(bb == 1))
                            mm.then_inc(o_pe, 1)
                            pe.wait_ge(o_act, g * 4 + 1)
                            for q in range(4):
                                mm = t.transpose(ps[:, 7, q * P:(q + 1) * P], ox[:, q * P:(q + 1) * P], ident[:, :])
                            mm.then_inc(o_pe, 1)
                            pe.wait_ge(o_dve, k + 6)
                            landed(pe, n0 + 3 * j, i)
                            landed(pe, n0 + 3 * j + 1, i)
                            gate_up(j, i, lambda kk: oxT[:, kk % 4, (kk // 4) * CAP:(kk // 4 + 1) * CAP],
                                    6, range(KC), False).then_inc(o_pe, 1)
                            pe.wait_ge(o_act, g * 4 + 2)
                            for q in range(4):
                                mm = t.transpose(ps[:, 7, q * P:(q + 1) * P], ox[:, q * P:(q + 1) * P], ident[:, :])
                            mm.then_inc(o_pe, 1)
                            pe.wait_ge(o_dve, k + 8)
                            landed(pe, n0 + 3 * j + 2, i)
                            down(j, lambda f: oaT[:, f * CAP:(f + 1) * CAP], 6).then_inc(o_pe, 1)
                            for bb in range(NB):
                                mm = t.transpose(ps[0:CAP, 7, bb * P:(bb + 1) * P], oput[:, bb, :], ident[:, :])
                            mm.then_inc(o_pe, 1)
                            pe.wait_ge(o_act, g * 4 + 4)
                            pe.wait_ge(o_dve, k + 10)
                            add_back(lambda bb: oputT[0:CAP, bb * P:(bb + 1) * P],
                                     lambda q: oy[0:CAP, q * 512:q * 512 + 512]).then_inc(o_pe, 1)

                gather(9 * l)
                pe.wait_ge(tab, l + 1)
                t.matmul(ps[:, 0, :], ones[:, :], y[:, 0:512], start=True, stop=True)
                turn_tokens(9 * l)
                pe.wait_ge(g_ev, 2 * (2 * l + 2))
                with pe.Fori(0, PAIRS) as i:
                    q = i + 8 * l
                    G = i + 9 * l
                    pe.wait_ge(xt_ev, (G + 1) * 2)
                    pe.wait_ge(tp_ev, q + 1)
                    overflow(i, 0)
                    pe.wait_ge(y_ev[0], (q + 1) * 2)
                    landed(pe, n0, i)
                    landed(pe, n0 + 1, i)
                    gate_up(0, i, lambda k: xT[:, k, 0:CAP], 4, range(KC), True)
                    pe.wait_ge(y_ev[1], (q + 1) * 2)
                    add_back(lambda b: putT[:, b * P:(b + 1) * P],
                             lambda qq: y[:, qq * 512:qq * 512 + 512]).then_inc(sc_mm, 1)
                    overflow(i, 1)
                    gather(G + 1)
                    landed(pe, n0 + 3, i)
                    landed(pe, n0 + 4, i)
                    gate_up(1, i, lambda k: xT[:, k, CAP:P], 5, range(4), False)
                    pe.wait_ge(gu_ev[0], q + 1)
                    for f in range(4):
                        mm = t.transpose(ps[:, 4, f * P:(f + 1) * P], gu[:, 0, f * P:(f + 1) * P], ident[:, :])
                    mm.then_inc(tg_mm[0], 1)
                    gate_up(1, i, lambda k: xT[:, k, CAP:P], 5, range(4, KC), True)
                    turn_tokens(G + 1)
                    pe.wait_ge(gu_ev[1], q + 1)
                    for f in range(4):
                        mm = t.transpose(ps[:, 5, f * P:(f + 1) * P], gu[:, 1, f * P:(f + 1) * P], ident[:, :])
                    mm.then_inc(tg_mm[1], 1)
                    pe.wait_ge(at_r[0], q + 1)
                    landed(pe, n0 + 2, i)
                    down(0, lambda f: aT[:, 0, f * CAP:(f + 1) * CAP], 4).then_inc(used[slot(n0 + 2)], 1)
                    pe.wait_ge(xt_ev, (G + 2) * 2)
                    pe.wait_ge(putted, (q + 1) * 4)
                    for b in range(NB):
                        mm = t.transpose(ps[:, 6, b * P:(b + 1) * P], put[:, b, :], ident[:, :])
                    mm.then_inc(tp_mm, 1)
                    pe.wait_ge(at_r[1], q + 1)
                    landed(pe, n0 + 5, i)
                    down(1, lambda f: aT[:, 1, f * CAP:(f + 1) * CAP], 5).then_inc(used[slot(n0 + 5)], 1)
                pe.wait_ge(tp_ev, 8 * (l + 1) + 1)
                pe.wait_ge(y_ev[0], (8 * (l + 1) + 1) * 2)
                pe.wait_ge(y_ev[1], (8 * (l + 1) + 1) * 2)
                for b in range(NB):
                    add_back(lambda b: putT[:, b * P:(b + 1) * P],
                             lambda qq: y[:, qq * 512:qq * 512 + 512], (b,)).then_inc(sc_mm, 1)

            first_modulation()
            turn_stream(0)
            stream_turned(0)
            u = turned_units(0, N_FOXQK, 4)
            mod_product(1)
            unit_free(u)
            for k in range(KC):
                mm = t.matmul(ps[0:HF, 0, 0:S], wf[:, k, :], hT[:, k, :], start=(k == 0), stop=(k == KC - 1))
            mm.then_inc(pj_mm, 1)
            natural_units(u + 1, N_FOXV, 2)
            mod_product(2)
            pe.wait_ge(pj_ev[0], pj_even(UNITS0))
            pe.wait_ge(pj_ev[1], pj_odd(UNITS0))
            pe.wait_ge(f_steps, 1)
            for hh in range(HF + 3):
                if hh < HF:
                    scores(hh, hh // 2, hh % 2, hh)
                if 2 <= hh < HF + 2:
                    turn_probs(hh - 2, (hh - 2) % 4, 2 * (hh - 1))
                if hh >= 3:
                    fox_values(hh - 3)
                if hh in (4, 10):
                    mod_product(3 if hh == 4 else 4)
            pe.wait_ge(o_ev, HD)
            pe.wait_ge(pt_ev, HF)
            out_product(0)
            turn_stream(1)
            route(0)
            experts(0)
            spread_fold(2)
            turn_stream(2)
            spread_fold(3)
            stream_turned(2)
            pe.wait_ge(f_steps, 2)
            u = turned_units(UNITS0, N_KVK, 2)
            pe.wait_ge(h_ready, 2 * 4)
            spread_norm(1)
            u = natural_units(u, N_KVV, 2)
            pe.wait_ge(x_ready, NB * 2)
            turn_stream(3)
            stream_turned(3)
            turned_units(u, N_WQ, 2)
            pe.wait_ge(pj_ev[0], pj_even(UNITS0 + 20))
            pe.wait_ge(pj_ev[1], pj_odd(UNITS0 + 20))
            for hd in range(HD + 3):
                if hd < HD:
                    scores(HF + 2 * hd, hd, 0, None)
                    scores(HF + 2 * hd + 1, hd, 1, None)
                if 2 <= hd < HD + 2:
                    turn_probs(HF + hd - 2, 2 * (hd % 2), 2 * HF + 2 * (hd - 1))
                if hd >= 3:
                    diff_values(hd - 3)
                if hd in (2, 5):
                    mod_product(5 if hd == 2 else 6)
            pe.wait_ge(o_ev, HD + 2 * HD)
            pe.wait_ge(pt_ev, HF + HD)
            for k in range(KC):
                for b in range(NB):
                    o = (k % 2) * S + b * P
                    mm = t.transpose(ps[:, k // 2, o:o + P], h[:, b, k * P:(k + 1) * P], ident[:, :])
                if k % 2:
                    mm.then_inc(ot_mm, 1)
            pe.wait_ge(ot_ev, 4)
            out_product(1)
            turn_stream(4)
            route(1)
            experts(1)
            spread_norm(3)


_INS = ["x", "c", "ada_w", "ada_b", "ln_attn_g", "ln_attn_b", "ln_ffn_g", "ln_ffn_b", "fox_w_in", "fox_b_f", "fox_w_o",
        "kv_ada_w", "kv_ada_b", "kv_w", "diff_w_q", "diff_lambda", "diff_norm_g", "diff_w_o",
        "router_w", "router_b", "moe_w_gate", "moe_w_up", "moe_w_down"]
_OUTS = [((1, 256, 1024), "float32")]


def kernel(**inputs):
    import numpy as _np
    import concourse.bacc as _bacc
    from concourse import mybir as _mybir
    from concourse.bass_utils import run_bass_kernel_spmd as _run

    nc = _bacc.Bacc("TRN2", target_bir_lowering=False, num_devices=1)
    arrays, args = {}, []
    for name in _INS:
        a = _np.ascontiguousarray(inputs[name])
        arrays[f"in_{name}_dram"] = a
        args.append(nc.dram_tensor(f"in_{name}_dram", a.shape, _mybir.dt.from_np(a.dtype), kind="ExternalInput").ap())
    for i, (shape, dtype) in enumerate(_OUTS):
        dt = _mybir.dt.from_np(_np.dtype(dtype))
        args.append(nc.dram_tensor(f"out_{i}_dram", shape, dt, kind="ExternalOutput").ap())
    build(nc, *args)
    r = _run(nc, [arrays], core_ids=[0])
    return r.results[0]["out_0_dram"]
```

```python
import math
from contextlib import ExitStack

import concourse.bass as bass
from concourse import mybir

ALU = mybir.AluOpType
ACT = mybir.ActivationFunctionType
AX = mybir.AxisListType
F32 = mybir.dt.float32
I32 = mybir.dt.int32

P = 128
RING = 6
CAP = 64
BIG = 1e30
FAR = 1e33


def build(nc, x, c, ada_w, ada_b, ln_attn_g, ln_attn_b, ln_ffn_g, ln_ffn_b, fox_w_in, fox_b_f, fox_w_o,
          kv_ada_w, kv_ada_b, kv_w, diff_w_q, diff_lambda, diff_norm_g, diff_w_o,
          router_w, router_b, moe_w_gate, moe_w_up, moe_w_down, out):
    DEPTH, D, _ = ada_w.shape
    S = x.shape[1]
    NE = router_w.shape[1]
    FE = moe_w_gate.shape[3]
    HF = fox_b_f.shape[1]
    HD = D // (diff_norm_g.shape[1])
    KC = D // P
    NB = S // P
    NG, EG = 4, 4
    PAIRS = NE // 2
    ALPHA = (2 * DEPTH) ** 0.25
    EPS = 1e-5
    LAM_INIT = 0.8 - 0.6 * math.exp(-0.3 * 1)
    ROUNDS = S // CAP - 1
    QSCALE = 0.125
    assert (DEPTH, D, S, NE, FE, HF, HD) == (2, 1024, 256, 16, 512, 16, 8)

    ada_dram = [ada_w[0], kv_ada_w, ada_w[1]]
    N_ADA = {gi: [] for gi in range(7)}
    N_FOXQK, N_FOXV, N_KVK, N_KVV, N_WQ = [], [], [], [], []
    N_WO, N_MOE = [[], []], []
    pieces = []

    def ada(gi, *quarters):
        which, group = ((0, 0), (0, 1), (0, 2), (1, 0), (2, 0), (2, 1), (2, 2))[gi]
        for b in quarters:
            col = 2048 * group + 512 * b
            N_ADA[gi].append(len(pieces))
            pieces.append(ada_dram[which][:, col:col + 512].rearrange("(k p) n -> p k n", p=P))

    def cols(names, w, lo, *parts_):
        for b in parts_:
            names.append(len(pieces))
            pieces.append(w[:, lo + 512 * b:lo + 512 * b + 512].rearrange("(k p) n -> p k n", p=P))

    def experts_pieces():
        N_MOE.append(len(pieces))
        pieces.extend([None] * (3 * NE))

    ada(0, 0, 1, 2, 3)
    cols(N_FOXQK, fox_w_in[0], 0, 0, 1)
    ada(1, 0, 1)
    cols(N_FOXQK, fox_w_in[0], 0, 2)
    ada(1, 2, 3)
    cols(N_FOXQK, fox_w_in[0], 0, 3)
    ada(2, 0, 1)
    cols(N_FOXV, fox_w_in[0], 2048, 0)
    ada(2, 2, 3)
    cols(N_FOXV, fox_w_in[0], 2048, 1)
    ada(3, 0, 1, 2, 3)
    ada(4, 0, 1, 2, 3)
    cols(N_WO[0], fox_w_o[0], 0, 0, 1)
    experts_pieces()
    cols(N_KVK, kv_w, 0, 0, 1)
    ada(5, 0, 1)
    cols(N_KVV, kv_w, 1024, 0)
    ada(5, 2, 3)
    cols(N_KVV, kv_w, 1024, 1)
    ada(6, 0, 1)
    cols(N_WQ, diff_w_q[0], 0, 0)
    ada(6, 2, 3)
    cols(N_WQ, diff_w_q[0], 0, 1)
    cols(N_WO[1], diff_w_o[0], 0, 0, 1)
    experts_pieces()

    def ada_row(layer_first, v):
        return layer_first + v // 2, 2 * (v % 2)
    ROW = {}
    for l, g0 in ((0, 0), (1, 4)):
        for v, name in enumerate(("sh_a", "sc_a", "g_a", "sh_f", "sc_f", "g_f")):
            ROW[name, l] = ada_row(g0, v)
        ROW["ln_a_g", l] = (7 + 2 * l, 0)
        ROW["ln_a_b", l] = (7 + 2 * l, 2)
        ROW["ln_f_g", l] = (8 + 2 * l, 0)
        ROW["ln_f_b", l] = (8 + 2 * l, 2)
    ROW["kv_sh"] = (3, 0)
    ROW["kv_sc"] = (3, 2)
    MODS = [(ROW["sc_a", 0], ROW["sh_a", 0]), (ROW["sc_f", 0], ROW["sh_f", 0]), (ROW["kv_sc"], ROW["kv_sh"]),
            (ROW["sc_a", 1], ROW["sh_a", 1]), (ROW["sc_f", 1], ROW["sh_f", 1])]

    with ExitStack() as ctx:
        def sb(name, shape, dt=F32):
            return ctx.enter_context(nc.sbuf_tensor(name, shape, dt))

        def sem(name):
            return ctx.enter_context(nc.semaphore(name))

        ring = sb("ring", [P, RING, 4096])
        xres = sb("xres", [P, NB, D])
        h = sb("h", [P, NB, D])
        hT = sb("hT", [P, KC, S])
        rows = sb("rows", [P, 11, 512])
        gbc = sb("gbc", [P, D])
        ident = sb("ident", [P, P])
        ones = sb("ones", [P, P])
        before = sb("before", [P, P])
        maskf = sb("maskf", [P, 3 * P])
        dist = sb("dist", [P, 3 * P])
        lane = sb("lane", [P, CAP])
        tri4 = sb("tri4", [P, EG, EG])
        ccol = sb("ccol", [P, KC])
        csig = sb("csig", [P, KC])
        strips = sb("strips", [P, 1])
        crep = sb("crep", [P, KC, 32])
        wf = sb("wf", [P, KC, HF])
        bf = sb("bf", [HF, 1])
        rw = sb("rw", [P, KC, NE])
        rb = sb("rb", [P, NE])
        lamin = sb("lamin", [P, 4, 64])
        lamt = sb("lamt", [P, 64])
        lam2 = sb("lam2", [P, 4])
        normg = sb("normg", [P, 1])
        st = sb("st", [P, 16])
        mhalf = sb("mhalf", [P, NB])
        fold = sb("fold", [P, 2, 512])
        tabn = sb("tabn", [1, NE], I32)
        tabb = sb("tabb", [1, NE], I32)
        rt = sb("rt", [P, 12, NB * NE])
        rg = sb("rg", [P, 6, 2 * 2 * 8])
        rc = sb("rc", [P, 3, NB * NG * EG * EG])
        gate = sb("gate", [P, NB, NE + 2])
        pos = sb("pos", [P, NB, NE + 2])
        cnt = sb("cnt", [1, 6, NE])
        arena = sb("arena", [P, 11264])
        ps = ctx.enter_context(nc.psum_tensor("ps", [P, 8, 512], F32))

        taken = [0]

        def part(rowcount, *shape):
            n = math.prod(shape)
            a = arena[0:rowcount, taken[0]:taken[0] + n]
            taken[0] += n
            assert taken[0] <= 11264
            names = "abc"[:len(shape)]
            if len(shape) == 1:
                return a
            return a.rearrange(f"p ({' '.join(names)}) -> p {' '.join(names)}",
                               **{names[i]: shape[i] for i in range(1, len(shape))})

        qT = part(P, KC, S)
        taken[0] = 0
        parts = part(P, 4, 512)
        osq = part(P, NB, P)
        kT = part(P, 2 * KC, S)
        v = part(P, NB, D)
        oT = hT
        lg_start = taken[0]
        lg = part(P, 4, 3 * P)
        pT = part(P, 2, 3 * P)
        ncum = part(P, 3 * P)
        negm = part(P, 4, 2)
        rs = part(P, 4, 2)
        rr = part(P, 4, 2)
        ss = part(P, HD, 4, NB)
        taken[0] = lg_start
        acc = part(P, 4, 512)
        fz = fold[0:HF, :, :].rearrange("p a (b s) -> p (a b) s", s=S)
        taken[0] = 0
        xg = part(P, D)
        xT = part(P, KC, 2 * CAP)
        gu = part(P, 2, FE)
        sg = part(P, 2, 4, CAP)
        tg = part(P, 2, 4, CAP)
        aT = part(P, 2, 4 * CAP)
        y = part(P, D)
        pick = part(P, NB, 2 * CAP)
        put = part(P, NB, 2 * CAP)
        putT = part(P, S)
        opos = part(P, NB)
        opick = part(P, NB, CAP)
        oput = part(P, NB, CAP)
        ox = part(P, FE)
        oxT = part(P, 4, 2 * CAP)
        osg = part(P, 4, CAP)
        oaT = part(P, 4 * CAP)
        oy = part(P, D)
        oputT = part(P, S)
        lng = part(P, D)
        lnb = oy

        full = [sem(f"full{i}") for i in range(RING)]
        used = [sem(f"used{i}") for i in range(RING)]
        x_in = sem("x_in")
        c_in = sem("c_in")
        small_in = sem("small_in")
        consts = sem("consts")
        csil = sem("csil")
        rows_zero = sem("rows_zero")
        acc_ch = sem("acc_ch")
        accp_ch = sem("accp_ch")
        mod_mm = sem("mod_mm")
        mod_row = sem("mod_row")
        fold_ch = sem("fold_ch")
        gate_mm = sem("gate_mm")
        fold_mm = sem("fold_mm")
        lnx_mm = sem("lnx_mm")
        y_mm = sem("y_mm")
        folded = sem("folded")
        h_ready = sem("h_ready")
        ht_mm = sem("ht_mm")
        ht_ready = [sem("ht_ready_act"), sem("ht_ready_dve")]
        bias0_in = sem("bias0_in")
        bias0 = sem("bias0")
        part_ev = [sem("part_ev_act"), sem("part_ev_dve")]
        ln_ev = sem("ln_ev")
        pj_mm = sem("pj_mm")
        pj_ev = [sem("pj_ev_act"), sem("pj_ev_dve")]
        lam_r = sem("lam_r")
        f_steps = sem("f_steps")
        f_act = sem("f_act")
        s_mm = sem("s_mm")
        mx = sem("mx")
        ex = sem("ex")
        pn = sem("pn")
        pt_mm = sem("pt_mm")
        pt_ev = sem("pt_ev")
        pv_mm = sem("pv_mm")
        o_ev = sem("o_ev")
        sum1_inv = sem("sum1_inv")
        o_rms = sem("o_rms")
        o_pow = sem("o_pow")
        normg_r = sem("normg_r")
        ot_mm = sem("ot_mm")
        ot_ev = sem("ot_ev")
        g_ev = sem("g_ev")
        r_sum = sem("r_sum")
        r_sq = sem("r_sq")
        r_std = sem("r_std")
        x_ready = sem("x_ready")
        rt_mm = sem("rt_mm")
        rt_dve = sem("rt_dve")
        rt_act = sem("rt_act")
        rt_mask = sem("rt_mask")
        tab = sem("tab")
        dch = sem("dch")
        pch = sem("pch")
        ach = sem("ach")
        picked = sem("picked")
        putted = sem("putted")
        ga_mm = sem("ga_mm")
        xg_ev = sem("xg_ev")
        tx_mm = sem("tx_mm")
        xt_ev = sem("xt_ev")
        gu_ev = [sem("gu_ev_a"), sem("gu_ev_b")]
        tg_mm = [sem("tg_mm_a"), sem("tg_mm_b")]
        sg_r = [sem("sg_r_a"), sem("sg_r_b")]
        tg_r = [sem("tg_r_a"), sem("tg_r_b")]
        at_r = [sem("at_r_a"), sem("at_r_b")]
        y_ev = [sem("y_ev_a"), sem("y_ev_b")]
        tp_mm = sem("tp_mm")
        tp_ev = sem("tp_ev")
        sc_mm = sem("sc_mm")
        o_pe = sem("o_pe")
        o_act = sem("o_act")
        o_dve = sem("o_dve")
        o_pos = sem("o_pos")
        o_pick = sem("o_pick")
        stored = sem("stored")

        def slot(n):
            return n % RING

        def landed(eng, n, i=None):
            val = 16 * (n // RING + 1)
            eng.wait_ge(full[n % RING], val if i is None else i * 16 + val)

        def spent(eng, n, i=None):
            val = n // RING + 1
            eng.wait_ge(used[n % RING], val if i is None else i + val)

        class Chain:
            def __init__(self, eng, s):
                self.eng, self.sem, self.n = eng, s, 0

            def __call__(self, ins):
                ins.then_inc(self.sem, 1)
                self.n += 1
                self.eng.wait_ge(self.sem, self.n)

        def turn_bank(m):
            return 4 if m == 3 else 0

        def wcols(n):
            return ring[:, slot(n), :].rearrange("p (k n) -> p k n", k=KC)

        def wdown(n):
            return ring[:, slot(n), :].rearrange("p (k n) -> p k n", k=4)

        def sel(rowno):
            return ident[:, rowno:rowno + 1].broadcast_to([P, P])

        SUMS = {1: 1, 2: 2, 3: 4, 5: 5, 6: 6}

        def part3(j):
            return gbc[:, 512:D] if j == 3 else fold[:, j % 2, :]

        def mod_bank(gi):
            return 6 if gi == 4 else 7

        def weigh(eng, alu, chain, gi, j, dst, tmp=None, ks=range(KC)):
            n = N_ADA[gi][j]
            landed(eng, n)
            w = wcols(n)
            for k in ks:
                if k == 0:
                    ins = alu.tensor_scalar(dst, w[:, 0, :], csig[:, 0:1], None, ALU.mult)
                elif tmp is None:
                    ins = alu.scalar_tensor_tensor(out=dst, in0=w[:, k, :], scalar=csig[:, k:k + 1], in1=dst,
                                                   op0=ALU.mult, op1=ALU.add)
                else:
                    chain(alu.tensor_scalar(tmp, w[:, k, :], csig[:, k:k + 1], None, ALU.mult))
                    ins = alu.tensor_tensor(dst, dst, tmp, ALU.add)
                if k < KC - 1:
                    chain(ins)
                else:
                    ins.then_inc(used[slot(n)], 1)

        SMALL = 20

        UNITS0 = 8 + 8 + 1 + 4
        GATE_UNIT = 16
        pj_done = {}

        def number_units():
            count = [0]

            def unit(u, last_of):
                if last_of is None:
                    count[0] += 1
                    pj_done[u] = ("pj_mm", count[0])
                else:
                    pj_done[u] = ("piece", last_of)
            for u in range(16):
                unit(u, N_FOXQK[u // 4] if u % 4 == 3 else None)
            unit(GATE_UNIT, None)
            for u in range(4):
                unit(GATE_UNIT + 1 + u, N_FOXV[u // 2] if u % 2 else None)
            for u in range(8):
                unit(UNITS0 + u, N_KVK[u // 4] if u % 4 == 3 else None)
            for u in range(4):
                unit(UNITS0 + 8 + u, N_KVV[u // 2] if u % 2 else None)
            for u in range(8):
                unit(UNITS0 + 12 + u, N_WQ[u // 4] if u % 4 == 3 else None)
        number_units()

        def unit_filled(eng, u):
            kind, val = pj_done[u]
            if kind == "pj_mm":
                eng.wait_ge(pj_mm, val)
            else:
                spent(eng, val)

        def pj_even(n):
            return len([u for u in range(0, n, 2) if u != GATE_UNIT])

        def pj_odd(n):
            return n // 2

        def proj_units(l):
            if l == 0:
                us = [(u, "q", qT[:, u, :]) for u in range(8)]
                us += [(8 + u, "k", u) for u in range(8)]
                us += [(GATE_UNIT, "f", None)]
                us += [(GATE_UNIT + 1 + u, "v", v[:, u % 2, 512 * (u // 2):512 * (u // 2) + 512]) for u in range(4)]
                return us
            us = [(UNITS0 + u, "k", u) for u in range(8)]
            us += [(UNITS0 + 8 + u, "v", v[:, u % 2, 512 * (u // 2):512 * (u // 2) + 512]) for u in range(4)]
            us += [(UNITS0 + 12 + u, "q", qT[:, u, :]) for u in range(8)]
            return us

        block = ctx.enter_context(nc.Block())

        @block.sync
        def _(sp):
            def load(n):
                if n >= RING:
                    spent(sp, n - RING)
                sp.dma_start(wpiece(n), pieces[n]).then_inc(full[slot(n)], 16)

            def wpiece(n):
                return wcols(n) if len(pieces[n].shape) == 3 else ring[:, slot(n), :]

            def expert_loads(l):
                n0 = N_MOE[l]
                with sp.Fori(0, PAIRS) as i:
                    for j in range(6):
                        e = i * 2 + (j // 2 if j < 4 else j - 4)
                        kind = j % 2 if j < 4 else 2
                        sp.wait_ge(used[slot(n0 + j)], i + (n0 + j - RING) // RING + 1)
                        w = (moe_w_gate, moe_w_up, moe_w_down)[kind]
                        src = w[l, bass.ds(e, 1), :, :].rearrange("o (k p) n -> p (o k) n", p=P)
                        dst = (wcols, wcols, wdown)[kind](n0 + j)
                        sp.dma_start(dst, src).then_inc(full[slot(n0 + j)], 16)

            sp.dma_start(ccol[:, :], c.rearrange("o (k p) -> p (o k)", p=P), allow_slow_non_contiguous=True).then_inc(c_in, 16)
            for n in range(N_MOE[0]):
                if n == 4:
                    for b in range(NB):
                        sp.dma_start(xres[:, b, :], x[0, b * P:(b + 1) * P, :]).then_inc(x_in, 16)
                if 2 <= n < RING:
                    landed(sp, n - 2)
                load(n)
            expert_loads(0)
            for n in range(N_MOE[0] + 3 * NE, N_MOE[1]):
                load(n)
            expert_loads(1)
            for b in range(NB):
                sp.wait_ge(x_ready, 3 * NB + b + 1)
                sp.dma_start(out[0, b * P:(b + 1) * P, :], h[:, b, :]).then_inc(stored, 16)
            sp.wait_ge(stored, 16 * NB)

        @block.gpsimd
        def _(pool):
            link = Chain(pool, pch)
            g = nc.gpsimd
            g.memset(rows[:, :, :], 0.0).then_inc(rows_zero, 1)
            link(g.memset(ident[:, :], 0.0))
            g.affine_select(out=ident[:, :], in_=ident[:, :], compare_op=ALU.not_equal, fill=1.0, base=0,
                            pattern=[[-1, P]], channel_multiplier=1).then_inc(consts, 1)
            link(g.memset(ones[:, :], 1.0))
            g.affine_select(out=before[:, :], in_=ones[:, :], compare_op=ALU.is_ge, fill=0.0, base=-1,
                            pattern=[[1, P]], channel_multiplier=-1).then_inc(consts, 1)
            link(g.memset(tri4[:, :, :], 1.0))
            g.affine_select(out=tri4[:, :, :], in_=tri4[:, :, :], compare_op=ALU.is_ge, fill=0.0, base=-1,
                            pattern=[[1, EG], [-1, EG]], channel_multiplier=0).then_inc(consts, 1)
            link(g.memset(maskf[:, :], 0.0))
            g.affine_select(out=maskf[:, 0:P], in_=maskf[:, 0:P], compare_op=ALU.is_ge, fill=-BIG, base=0,
                            pattern=[[-1, P]], channel_multiplier=1).then_inc(consts, 1)
            g.affine_select(out=maskf[:, 2 * P:], in_=maskf[:, 2 * P:], compare_op=ALU.is_ge, fill=-BIG, base=0,
                            pattern=[[-1, P]], channel_multiplier=1).then_inc(consts, 1)
            for t, base in enumerate((0, P, 0)):
                link(g.iota(dist[:, t * P:(t + 1) * P], pattern=[[-1, P]], base=base, channel_multiplier=1,
                            allow_small_or_imprecise_dtypes=True))
            for t in (0, 2):
                g.affine_select(out=dist[:, t * P:(t + 1) * P], in_=dist[:, t * P:(t + 1) * P],
                                compare_op=ALU.is_ge, fill=FAR, base=0,
                                pattern=[[-1, P]], channel_multiplier=1).then_inc(consts, 1)
            g.iota(lane[:, :], pattern=[[1, CAP]], base=0, channel_multiplier=0,
                   allow_small_or_imprecise_dtypes=True).then_inc(consts, 1)
            g.memset(mhalf[:, :], -0.5).then_inc(consts, 1)

            pool.wait_ge(consts, 9)

            def inv_std(norm):
                for b in range(NB):
                    u = 2 * norm + b
                    pool.wait_ge(r_sq, u + 1)
                    link(g.tensor_scalar(st[:, 6 + b:7 + b], st[:, 4 + b:5 + b], 1.0 / D, EPS, ALU.mult, ALU.add))
                    g.tensor_tensor(st[:, 8 + b:9 + b], st[:, 6 + b:7 + b], mhalf[:, 0:1], ALU.pow).then_inc(r_std, 1)
            def gained(norm):
                pool.wait_ge(ln_ev, 4 * (norm // 2 + 1))
                for b in range(NB):
                    link(g.tensor_scalar(xres[:, b, :], xres[:, b, :], st[:, 2 + b:3 + b], st[:, 8 + b:9 + b],
                                         ALU.add, ALU.mult))
                    link(g.tensor_tensor(xres[:, b, :], xres[:, b, :], lng, ALU.mult))
                    g.tensor_tensor(xres[:, b, :], xres[:, b, :], lnb, ALU.add).then_inc(x_ready, 1)
            heap = Chain(pool, accp_ch)

            def share(gi):
                weigh(pool, g, heap, gi, 1, acc[:, 1, :], gbc[:, 0:512])
            pool.wait_ge(csil, 2)
            share(1)
            pool.wait_ge(mod_mm, SUMS[1])
            share(2)
            pool.wait_ge(f_steps, 1)
            for j in (1, 3):
                weigh(pool, g, heap, 3, j, part3(j), gbc[:, 0:512])
            inv_std(0)
            gained(0)
            inv_std(1)
            share(5)
            pool.wait_ge(mod_mm, SUMS[5])
            share(6)
            for hd in range(HD):
                pool.wait_ge(o_rms, NB * (hd + 1))
                link(g.tensor_scalar(ss[:, hd, 1, :], ss[:, hd, 0, :], 1.0 / P, EPS, ALU.mult, ALU.add))
                link(g.tensor_tensor(ss[:, hd, 2, :], ss[:, hd, 1, :], mhalf[:, :], ALU.pow))
                g.tensor_tensor(ss[:, hd, 2, :], ss[:, hd, 2, :], ss[:, hd, 3, :], ALU.mult).then_inc(o_pow, 1)
            inv_std(2)
            gained(2)
            inv_std(3)

        @block.scalar
        def _(act):
            a = nc.scalar
            link = Chain(act, ach)

            act.wait_ge(c_in, 16)
            a.activation(csig[:, :], ccol[:, :], ACT.Sigmoid).then_inc(csil, 1)
            act.wait_ge(rows_zero, 1)
            for l, g0 in ((0, 0), (1, 4)):
                for gi in range(3):
                    act.dma_start(rows[0:97:32, g0 + gi, :],
                                  ada_b[l, 2048 * gi:2048 * gi + 2048].rearrange("(j n) -> j n", j=4)
                                  ).then_inc(bias0_in if g0 + gi == 0 else small_in, 16)
                for gi, (u, w) in enumerate(((ln_attn_g, ln_attn_b), (ln_ffn_g, ln_ffn_b))):
                    for hh, vec in enumerate((u, w)):
                        act.dma_start(rows[64 * hh:64 * hh + 33:32, 7 + 2 * l + gi, :],
                                      vec[l, :].rearrange("(j n) -> j n", j=2)).then_inc(small_in, 16)
            act.dma_start(rows[0:97:32, 3, :], kv_ada_b.rearrange("(j n) -> j n", j=4)).then_inc(small_in, 16)
            act.dma_start(wf[:, :, :], fox_w_in[0][:, 3 * D:3 * D + HF].rearrange("(k p) n -> p k n", p=P)).then_inc(small_in, 16)
            act.dma_start(bf[:, :], fox_b_f[0:1, :].rearrange("o n -> n o"), allow_slow_non_contiguous=True).then_inc(small_in, 16)
            act.dma_start(rw[:, :, :], router_w.rearrange("(k p) n -> p k n", p=P)).then_inc(small_in, 16)
            act.dma_start(rb[:, :], router_b.partition_broadcast(P)).then_inc(small_in, 16)
            act.dma_start(lamin[:, :, :], diff_lambda[0].partition_broadcast(P)).then_inc(small_in, 16)
            act.dma_start(normg[:, :], diff_norm_g.rearrange("o n -> n o"), allow_slow_non_contiguous=True).then_inc(small_in, 16)

            for j in (0, 2):
                spent(act, N_ADA[0][j])
                a.activation(parts[:, j, :], ps[:, j, :], ACT.Copy).then_inc(part_ev[0], 1)

            def turned(m):
                for b in range(NB):
                    act.wait_ge(ht_mm, NB * m + b + 1)
                    a.activation(hT[:, 0:4, b * P:(b + 1) * P],
                                 ps[:, turn_bank(m) + 2 * b, :].rearrange("p (k s) -> p k s", k=4),
                                 ACT.Copy).then_inc(ht_ready[0], 1)

            def unit_out(u, dst, kind):
                if u % 2:
                    return
                unit_filled(act, u)
                if kind == "k":
                    cc = dst
                    link(a.activation(kT[0:64, 2 * cc, :], ps[0:64, u % 4, 0:S], ACT.Copy))
                    a.activation(kT[64:P, 2 * cc + 1, :], ps[64:P, u % 4, 0:S], ACT.Copy).then_inc(pj_ev[0], 1)
                elif kind == "q":
                    a.activation(dst, ps[:, u % 4, 0:S], ACT.Copy, scale=QSCALE).then_inc(pj_ev[0], 1)
                else:
                    a.activation(dst, ps[:, u % 4, :], ACT.Copy).then_inc(pj_ev[0], 1)

            def forget_gate():
                unit_filled(act, GATE_UNIT)
                act.wait_ge(small_in, 16 * SMALL)
                link(a.activation(fz[:, 0, :], ps[0:HF, 0, 0:S], ACT.Abs, bias=bf[:, 0:1]))
                link(a.activation(fz[:, 1, :], fz[:, 0, :], ACT.Exp, scale=-1.0))
                a.activation(fz[:, 2, :], fz[:, 1, :], ACT.Ln, bias=1.0).then_inc(f_act, 1)

            def exps(H):
                t = H % 4
                act.wait_ge(mx, 2 * (H + 1))
                a.activation(lg[:, t, 0:P], lg[:, t, 0:P], ACT.Exp, bias=negm[:, t, 0:1],
                             accum_out=rs[:, t, 0:1]).then_inc(ex, 1)
                a.activation(lg[:, t, P:3 * P], lg[:, t, P:3 * P], ACT.Exp, bias=negm[:, t, 1:2],
                             accum_out=rs[:, t, 1:2]).then_inc(ex, 1)

            def probs_out(T):
                act.wait_ge(pt_mm, T + 1)
                if T >= 2:
                    act.wait_ge(pv_mm, T - 1)
                a.activation(pT[:, T % 2, :], ps[:, 2 + T % 2, 0:3 * P], ACT.Copy).then_inc(pt_ev, 1)

            def gate_out(norm):
                act.wait_ge(gate_mm, norm + 1)
                for q in range(2):
                    a.activation(gbc[:, q * 512:q * 512 + 512], ps[:, 4 + q, :], ACT.Copy).then_inc(g_ev, 1)

            def norm_out(norm):
                act.wait_ge(lnx_mm, norm + 1)
                for q in range(4):
                    dst = (lng, lnb)[q // 2]
                    a.activation(dst[:, q % 2 * 512:q % 2 * 512 + 512], ps[:, 4 + q, :], ACT.Copy).then_inc(ln_ev, 1)

            def squares(norm):
                for b in range(NB):
                    u = 2 * norm + b
                    act.wait_ge(r_sum, u + 1)
                    if u:
                        act.wait_ge(r_sq, u)
                    a.activation(fold[:, :, :].rearrange("p a b -> p (a b)"), xres[:, b, :], ACT.Square,
                                 bias=st[:, 2 + b:3 + b],
                                 accum_out=st[:, 4 + b:5 + b]).then_inc(r_sq, 1)

            def router_exp(l):
                act.wait_ge(rt_dve, l + 1)
                a.activation(rt[:, 1, :], rt[:, 0, :], ACT.Exp).then_inc(rt_act, 1)

            def experts(l):
                n0 = N_MOE[l]

                def tokens_out(G):
                    act.wait_ge(ga_mm, G + 1)
                    a.activation(xg[:, 512:D], ps[:, 7, :], ACT.Copy).then_inc(xg_ev, 1)

                def turned_out(G):
                    act.wait_ge(tx_mm, G + 1)
                    a.activation(xT[:, 4:8, :].rearrange("p a b -> p (a b)"), ps[:, 7, :], ACT.Copy).then_inc(xt_ev, 1)

                def overflow(i, j):
                    n = act.value_load(tabn[0:1, bass.ds(i * 2 + j, 1)], min_val=0, max_val=ROUNDS)
                    b = act.value_load(tabb[0:1, bass.ds(i * 2 + j, 1)], min_val=0, max_val=2 * NE * ROUNDS)
                    with act.If(n > 0):
                        with act.Fori(b, b + n) as g:
                            act.wait_ge(o_pe, g * 7 + 1)
                            a.activation(ox[:, :], ps[:, 6, :], ACT.Copy).then_inc(o_act, 1)
                            act.wait_ge(o_pe, g * 7 + 3)
                            a.activation(ox[:, :], ps[:, 6, :], ACT.Copy).then_inc(o_act, 1)
                            act.wait_ge(o_pe, g * 7 + 4)
                            gt = ps[:, 7, :].rearrange("p (c s) -> p c s", c=4)
                            a.activation(osg[:, :, :], gt[:, :, 0:CAP], ACT.Sigmoid).then_inc(o_act, 1)
                            act.wait_ge(o_pe, g * 7 + 5)
                            act.wait_ge(x_ready, NB * (2 * l + 1))
                            a.activation(oy[0:CAP, 0:512], ps[0:CAP, 6, :], ACT.Copy).then_inc(o_act, 1)

                act.wait_ge(tab, l + 1)
                tokens_out(9 * l)
                turned_out(9 * l)
                with act.Fori(0, PAIRS) as i:
                    q = i + 8 * l
                    G = i + 9 * l
                    overflow(i, 0)
                    spent(act, n0 + 1, i)
                    a.activation(gu[:, 0, :], ps[:, 4, :], ACT.Copy).then_inc(gu_ev[0], 1)
                    overflow(i, 1)
                    tokens_out(G + 1)
                    act.wait_ge(tg_mm[0], q + 1)
                    gt = ps[:, 4, :].rearrange("p (c s) -> p c s", c=4)
                    a.activation(sg[:, 0, :, :], gt[:, :, 0:CAP], ACT.Sigmoid).then_inc(sg_r[0], 1)
                    spent(act, n0 + 3, i)
                    a.activation(gu[:, 1, :], ps[:, 5, :], ACT.Copy).then_inc(gu_ev[1], 1)
                    turned_out(G + 1)
                    act.wait_ge(tg_mm[1], q + 1)
                    gt = ps[:, 5, :].rearrange("p (c s) -> p c s", c=4)
                    a.activation(sg[:, 1, :, :], gt[:, :, 0:CAP], ACT.Sigmoid).then_inc(sg_r[1], 1)
                    act.wait_ge(sc_mm, i + (10 * l + 1))
                    spent(act, n0 + 4, i)
                    a.activation(y[0:CAP, 0:512], ps[0:CAP, 4, :], ACT.Copy).then_inc(y_ev[0], 1)
                    spent(act, n0 + 5, i)
                    a.activation(y[CAP:P, 0:512], ps[0:CAP, 5, :], ACT.Copy).then_inc(y_ev[1], 1)

            turned(0)
            for (u, kind, dst) in proj_units(0):
                if u == 16:
                    forget_gate()
                else:
                    unit_out(u, dst, kind)
            for t in range(HF + 2):
                if t < HF:
                    exps(t)
                if t >= 2:
                    probs_out(t - 2)
            gate_out(0)
            squares(0)
            turned(1)
            router_exp(0)
            norm_out(0)
            gate_out(1)
            experts(0)
            squares(1)
            turned(2)
            us = proj_units(1)
            for (u, kind, dst) in us[:12]:
                unit_out(u, dst, kind)
            turned(3)
            for (u, kind, dst) in us[12:]:
                unit_out(u, dst, kind)
            act.wait_ge(lam_r, 1)
            a.activation(lam2[:, 2:4], lam2[:, 0:2], ACT.Exp).then_inc(lam_r, 1)
            for t in range(HD + 3):
                if t < HD:
                    exps(HF + 2 * t)
                    exps(HF + 2 * t + 1)
                if 2 <= t < HD + 2:
                    probs_out(HF + t - 2)
                if t >= 3:
                    hd = t - 3
                    act.wait_ge(pv_mm, HF + hd + 1)
                    act.wait_ge(sum1_inv, hd + 1)
                    for b in range(NB):
                        a.activation(osq[:, b, :], ps[:, 4 + hd % 3, b * P:(b + 1) * P], ACT.Square,
                                     scale=ss[:, hd, 3, b:b + 1], accum_out=ss[:, hd, 0, b:b + 1]).then_inc(o_rms, 1)
                        act.wait_ge(o_rms, NB * hd + b + 1)
            act.wait_ge(normg_r, 1)
            for q in range(2):
                act.wait_ge(ot_mm, 2 * q + 1)
                a.activation(oT[:, 4 * q:4 * q + 2, :].rearrange("p a b -> p (a b)"), ps[:, 2 * q, :],
                             ACT.Copy, scale=normg[:, 0:1]).then_inc(ot_ev, 1)
            gate_out(2)
            squares(2)
            turned(4)
            router_exp(1)
            norm_out(2)
            gate_out(3)
            experts(1)
            squares(3)

        @block.vector
        def _(dve):
            d = nc.vector
            link = Chain(dve, dch)
            Fold = Chain(dve, fold_ch)
            heap = Chain(dve, acc_ch)

            dve.sem_inc(y_ev[0], 2)
            dve.sem_inc(y_ev[1], 2)
            dve.sem_inc(tp_ev, 1)
            dve.sem_inc(o_dve, 1)
            link(d.memset(kT[:, :, :], 0.0))
            link(d.memset(ncum[:, :], 0.0))
            dve.wait_ge(csil, 1)
            link(d.tensor_tensor(csig[:, :], csig[:, :], ccol[:, :], ALU.mult))
            d.tensor_copy(crep[:, :, :], csig[:, :].unsqueeze(2).broadcast_to([P, KC, 32])).then_inc(csil, 1)
            dve.wait_ge(bias0_in, 16)
            d.tensor_scalar(rows[64:P, 0, :], rows[64:P, 0, :], 1.0, None, ALU.add).then_inc(bias0, 1)
            dve.wait_ge(consts, 9)
            d.tensor_reduce(strips[:, :], ident[:, 0:P:32], AX.X, ALU.add).then_inc(bias0, 1)
            def share(gi, j):
                if j == 0 and gi in (2, 6):
                    dve.wait_ge(mod_mm, SUMS[gi - 1])
                weigh(dve, d, heap, gi, j, acc[:, j, :])

            def mod_rows(gi):
                if gi == 4:
                    for n in N_ADA[gi]:
                        spent(dve, n)
                else:
                    dve.wait_ge(mod_mm, SUMS[gi])
                d.tensor_tensor(rows[:, gi, :], rows[:, gi, :], ps[:, mod_bank(gi), :], ALU.add).then_inc(mod_row, 1)

            def fold_rows(m):
                (cg, cj), (sg_, sj) = MODS[m]
                norm = (None, 0, 1, 1, 2)[m]
                lg_, _ = ROW["ln_" + "af"[norm % 2] + "_g", norm // 2]
                c = rows[32 * cj:32 * cj + 64, cg, :]
                sh = rows[32 * sj:32 * sj + 64, sg_, :]
                t0, t1 = fold[32 * cj:32 * cj + 64, 0, :], fold[32 * cj:32 * cj + 64, 1, :]
                u1 = fold[32 * sj:32 * sj + 64, 1, :]
                f = Fold
                dve.wait_ge(mod_row, max(cg, sg_))
                if m >= 2:
                    dve.wait_ge(folded, m - 1)
                f(d.tensor_copy(t0, rows[64:P, lg_, :]))
                f(d.tensor_tensor(t1, t0, c, ALU.mult))
                f(d.tensor_copy(u1, t1))
                f(d.tensor_tensor(sh, sh, u1, ALU.add))
                f(d.tensor_copy(t0, rows[0:64, lg_, :]))
                d.tensor_tensor(c, c, t0, ALU.mult).then_inc(folded, 1)

            def affine(norm, b, dst, fac, add):
                link(d.scalar_tensor_tensor(out=dst, in0=xres[:, b, :], scalar=st[:, 2 + b:3 + b], in1=fac,
                                            op0=ALU.add, op1=ALU.mult))
                dve.wait_ge(r_std, 2 * norm + b + 1)
                return d.scalar_tensor_tensor(out=dst, in0=dst, scalar=st[:, 8 + b:9 + b], in1=add,
                                              op0=ALU.mult, op1=ALU.add)

            def streamed(m):
                dve.wait_ge(fold_mm, m + 1)
                fac = ps[:, 4:6, :].rearrange("p a b -> p (a b)")
                add = ps[:, 6:8, :].rearrange("p a b -> p (a b)")
                for b in range(NB):
                    if m == 3:
                        dve.wait_ge(ht_mm, NB * 3)
                    if m == 0:
                        link(d.tensor_tensor(h[:, b, :], xres[:, b, :], fac, ALU.mult))
                        d.tensor_tensor(h[:, b, :], h[:, b, :], add, ALU.add).then_inc(h_ready, 1)
                    else:
                        affine((None, 0, 1, 1, 2)[m], b, h[:, b, :], fac, add).then_inc(h_ready, 1)

            def turned(m):
                for b in range(NB):
                    dve.wait_ge(ht_mm, NB * m + b + 1)
                    d.tensor_copy(hT[:, 4:8, b * P:(b + 1) * P],
                                  ps[:, turn_bank(m) + 2 * b + 1, :].rearrange("p (k s) -> p k s", k=4)).then_inc(ht_ready[1], 1)

            def unit_out(u, dst, kind):
                if u % 2 == 0:
                    return
                unit_filled(dve, u)
                if kind == "k":
                    cc = dst
                    link(d.tensor_copy(kT[0:64, 2 * cc, :], ps[0:64, u % 4, 0:S]))
                    d.tensor_copy(kT[64:P, 2 * cc + 1, :], ps[64:P, u % 4, 0:S]).then_inc(pj_ev[1], 1)
                elif kind == "q":
                    d.tensor_scalar(dst, ps[:, u % 4, 0:S], QSCALE, None, ALU.mult).then_inc(pj_ev[1], 1)
                else:
                    d.tensor_copy(dst, ps[:, u % 4, :]).then_inc(pj_ev[1], 1)

            def forget_gate():
                dve.wait_ge(f_act, 1)
                link(d.tensor_scalar(fz[:, 0, :], ps[0:HF, 0, 0:S], bf[:, 0:1], 0.0, ALU.add, ALU.min))
                link(d.tensor_tensor(fz[:, 1, :], fz[:, 2, :], fz[:, 0, :], ALU.subtract))
                link(d.memset(fz[:, 3, :], 1.0))
                link(d.tensor_tensor_scan(ncum[0:HF, P:3 * P], fz[:, 3, :], fz[:, 1, :], 0.0, ALU.mult, ALU.add))
                d.tensor_copy(ncum[0:HF, 0:P], ncum[0:HF, P:2 * P]).then_inc(f_steps, 1)

            def soft(H, bias, factor):
                t = H % 4
                dve.wait_ge(s_mm, H + 1)
                link(d.scalar_tensor_tensor(out=lg[:, t, :], in0=bias[:, :], scalar=factor, in1=ps[:, H % 2, 0:3 * P],
                                            op0=ALU.mult, op1=ALU.add))
                d.tensor_reduce(negm[:, t, 0:1], lg[:, t, 0:P], AX.X, ALU.max, negate=True).then_inc(mx, 1)
                d.tensor_reduce(negm[:, t, 1:2], lg[:, t, P:3 * P], AX.X, ALU.max, negate=True).then_inc(mx, 1)

            def fox_norm(H):
                t = H % 4
                dve.wait_ge(ex, 2 * (H + 1))
                link(d.reciprocal(rr[:, t, :], rs[:, t, :]))
                d.tensor_scalar(lg[:, t, 0:P], lg[:, t, 0:P], rr[:, t, 0:1], None, ALU.mult).then_inc(pn, 1)
                d.tensor_scalar(lg[:, t, P:3 * P], lg[:, t, P:3 * P], rr[:, t, 1:2], None, ALU.mult).then_inc(pn, 1)

            def diff_norm(hd):
                dve.wait_ge(ex, 2 * (HF + 2 * hd + 2))
                t = 2 * (hd % 2)
                link(d.reciprocal(rr[:, t + 1, :], rs[:, t + 1, :]))
                link(d.scalar_tensor_tensor(out=rr[:, t, :], in0=rr[:, t + 1, :], scalar=lam2[:, 0:1], in1=rs[:, t, :],
                                            op0=ALU.mult, op1=ALU.mult))
                for q, (lo, hi) in enumerate(((0, P), (P, 3 * P))):
                    d.scalar_tensor_tensor(out=lg[:, t, lo:hi], in0=lg[:, t + 1, lo:hi], scalar=rr[:, t, q:q + 1],
                                           in1=lg[:, t, lo:hi], op0=ALU.mult, op1=ALU.add).then_inc(pn, 1)
                d.reciprocal(ss[:, hd, 3, :], rs[:, t, :]).then_inc(sum1_inv, 1)

            def norm_sums(norm, b):
                yb = ps[:, 2 * b:2 * b + 2, :].rearrange("p a b -> p (a b)")
                link(d.tensor_tensor(h[:, b, :], gbc[:, :], yb, ALU.mult))
                link(d.scalar_tensor_tensor(out=xres[:, b, :], in0=xres[:, b, :], scalar=ALPHA, in1=h[:, b, :],
                                            op0=ALU.mult, op1=ALU.add, accum_out=st[:, b:b + 1]))
                d.tensor_scalar(st[:, 2 + b:3 + b], st[:, b:b + 1], -1.0 / D, None, ALU.mult).then_inc(r_sum, 1)

            def y_ready(norm, b):
                if norm % 2 == 0 and b == 0:
                    dve.wait_ge(y_mm, norm // 2 + 1)
                elif norm % 2 == 0:
                    for n in N_WO[norm // 2]:
                        spent(dve, n)
                else:
                    dve.wait_ge(sc_mm, 10 * (norm // 2) + 9 + b)

            def post_norm(norm):
                dve.wait_ge(g_ev, 2 * (norm + 1))
                if norm:
                    dve.wait_ge(x_ready, NB * norm)
                for b in range(NB):
                    y_ready(norm, b)
                    norm_sums(norm, b)

            def gained(norm):
                dve.wait_ge(lnx_mm, norm + 1)
                lg_ = ps[:, 4:6, :].rearrange("p a b -> p (a b)")
                lb_ = ps[:, 6:8, :].rearrange("p a b -> p (a b)")
                for b in range(NB):
                    dst = h if norm == 3 else xres
                    affine(norm, b, dst[:, b, :], lg_, lb_).then_inc(x_ready, 1)

            def rank4(src, n, cmp, eq, dst):
                a4 = src.unsqueeze(2).broadcast_to([P, n, 4, 4])
                b4 = src.unsqueeze(3).broadcast_to([P, n, 4, 4])
                tri = tri4[:, :, :].unsqueeze(1).broadcast_to([P, n, 4, 4])
                link(d.tensor_tensor(cmp, a4, b4, ALU.is_gt))
                link(d.tensor_tensor(eq, a4, b4, ALU.is_equal))
                link(d.tensor_tensor(eq, eq, tri, ALU.mult))
                link(d.tensor_tensor(cmp, cmp, eq, ALU.add))
                link(d.tensor_reduce(dst, cmp, AX.X, ALU.add))

            def pick_pair(i):
                for b in range(NB):
                    for j in range(2):
                        d.tensor_scalar(pick[:, b, j * CAP:(j + 1) * CAP], lane[:, :],
                                        pos[:, b, bass.ds(i * 2 + j, 1)], None, ALU.is_equal).then_inc(picked, 1)

            def nothing_added():
                link(d.memset(putT[:, :], 0.0))
                link(d.memset(y[:, :], 0.0))

            def route(l):
                def t3(k):
                    return rt[:, k, :].rearrange("p (b e) -> p b e", b=NB)

                def t4(k):
                    return rt[:, k, :].rearrange("p (g e) -> p g e", e=EG)
                dve.wait_ge(rt_mm, 2 * l + 1)
                lgt = ps[:, 0, 0:NB * NE]
                mxr = st[:, 10:12]
                link(d.tensor_copy(rt[:, 2, :], lgt))
                link(d.tensor_reduce(mxr, t3(2), AX.X, ALU.max))
                d.tensor_tensor(t3(0), t3(2), mxr.unsqueeze(2).broadcast_to([P, NB, NE]), ALU.subtract).then_inc(rt_dve, 1)
                dve.wait_ge(rt_act, l + 1)
                link(d.tensor_reduce(st[:, 12:14], t3(1), AX.X, ALU.add))
                link(d.reciprocal(st[:, 12:14], st[:, 12:14]))
                link(d.tensor_tensor(t3(3), t3(1), st[:, 12:14].unsqueeze(2).broadcast_to([P, NB, NE]), ALU.mult))
                link(d.tensor_tensor(t3(4), t3(3), rb[:, :].unsqueeze(1).broadcast_to([P, NB, NE]), ALU.add))
                A, B = t4(4)[:, :, 0:4:2], t4(4)[:, :, 1:4:2]
                hi = rg[:, 0, 0:16].rearrange("p (g e) -> p g e", e=2)
                lo = rg[:, 1, 0:16].rearrange("p (g e) -> p g e", e=2)
                link(d.tensor_tensor(hi, A, B, ALU.max))
                link(d.tensor_tensor(lo, A, B, ALU.min))
                m1, x1, x2 = rg[:, 2, 0:8], rg[:, 3, 0:8], rg[:, 4, 0:8]
                link(d.tensor_tensor(m1, hi[:, :, 0], hi[:, :, 1], ALU.max))
                link(d.tensor_tensor(x1, hi[:, :, 0], hi[:, :, 1], ALU.min))
                link(d.tensor_tensor(x2, lo[:, :, 0], lo[:, :, 1], ALU.max))
                link(d.tensor_tensor(x1, x1, x2, ALU.max))
                link(d.tensor_tensor(m1, m1, x1, ALU.add))
                gsum = m1.rearrange("p (b g) -> p b g", b=NB)
                c2 = [rc[:, k, 0:NB * 16].rearrange("p (n i j) -> p n i j", i=4, j=4) for k in range(2)]
                rank4(gsum, NB, c2[0], c2[1], rg[:, 5, 0:8].rearrange("p (b g) -> p b g", b=NB))
                link(d.tensor_scalar(rg[:, 5, 0:8], rg[:, 5, 0:8], 0.5, None, ALU.is_lt))
                c8 = [rc[:, k, :].rearrange("p (n i j) -> p n i j", i=4, j=4) for k in range(2)]
                rank4(t4(4), NB * NG, c8[0], c8[1], t4(5))
                link(d.tensor_scalar(rt[:, 5, :], rt[:, 5, :], 1.5, None, ALU.is_lt))
                link(d.tensor_tensor(t4(6), t4(5), rg[:, 5, 0:8].unsqueeze(2).broadcast_to([P, NB * NG, EG]), ALU.mult))
                d.tensor_copy(rt[:, 7, :], rt[:, 6, :]).then_inc(rt_mask, 1)
                link(d.tensor_tensor(rt[:, 8, :], rt[:, 3, :], rt[:, 6, :], ALU.mult))
                link(d.tensor_reduce(st[:, 14:16], t3(8), AX.X, ALU.add))
                link(d.reciprocal(st[:, 14:16], st[:, 14:16]))
                link(d.memset(gate[:, :, :], 0.0))
                link(d.memset(pos[:, :, :], -1.0))
                link(d.tensor_tensor(gate[:, :, 0:NE], t3(8), st[:, 14:16].unsqueeze(2).broadcast_to([P, NB, NE]), ALU.mult))
                dve.wait_ge(rt_mm, 2 * l + 2)
                link(d.scalar_tensor_tensor(out=rt[:, 9, :], in0=ps[:, 0, NB * NE:2 * NB * NE], scalar=1.0, in1=rt[:, 6, :],
                                            op0=ALU.add, op1=ALU.mult))
                link(d.tensor_scalar(pos[:, :, 0:NE], t3(9), -1.0, None, ALU.add))
                pick_pair(0)
                tot = ps[0:1, 0, 2 * NB * NE:2 * NB * NE + NE]
                link(d.tensor_scalar(cnt[:, 0, :], tot, float(CAP) + 0.5, None, ALU.is_gt))
                for r in range(2, ROUNDS + 1):
                    link(d.tensor_scalar(cnt[:, 1, :], tot, r * float(CAP) + 0.5, None, ALU.is_gt))
                    link(d.tensor_tensor(cnt[:, 0, :], cnt[:, 0, :], cnt[:, 1, :], ALU.add))
                link(d.memset(cnt[:, 2, :], 1.0))
                start = 0.0 if l == 0 else cnt[:, 5, 0:1]
                link(d.tensor_tensor_scan(cnt[:, 3, :], cnt[:, 2, :], cnt[:, 0, :], start, ALU.mult, ALU.add))
                link(d.tensor_tensor(cnt[:, 4, :], cnt[:, 3, :], cnt[:, 0, :], ALU.subtract))
                link(d.tensor_copy(cnt[:, 5, 0:1], cnt[:, 3, NE - 1:NE]))
                link(d.tensor_copy(tabn[:, :], cnt[:, 0, :]))
                d.tensor_copy(tabb[:, :], cnt[:, 4, :]).then_inc(tab, 1)
                dve.wait_ge(tab, l + 1)

            def experts(l):
                n0 = N_MOE[l]

                def put_pair(i):
                    for b in range(NB):
                        for j in range(2):
                            d.tensor_scalar(put[:, b, j * CAP:(j + 1) * CAP], lane[:, :],
                                            pos[:, b, bass.ds(i * 2 + j, 1)], gate[:, b, bass.ds(i * 2 + j, 1)],
                                            ALU.is_equal, ALU.mult).then_inc(putted, 1)

                def tokens_out(G):
                    dve.wait_ge(ga_mm, G + 1)
                    d.tensor_copy(xg[:, 0:512], ps[:, 6, :]).then_inc(xg_ev, 1)

                def turned_out(G):
                    dve.wait_ge(tx_mm, G + 1)
                    d.tensor_copy(xT[:, 0:4, :].rearrange("p a b -> p (a b)"), ps[:, 6, :]).then_inc(xt_ev, 1)

                def glu(j, q):
                    gt = ps[:, 4 + j, :].rearrange("p (c s) -> p c s", c=4)
                    dve.wait_ge(sg_r[j], q + 1)
                    d.tensor_tensor(tg[:, j, :, :], sg[:, j, :, :], gt[:, :, 0:CAP], ALU.mult).then_inc(tg_r[j], 1)
                    dve.wait_ge(tg_r[j], q + 1)
                    d.tensor_tensor(aT[:, j, :].rearrange("p (c s) -> p c s", c=4), tg[:, j, :, :],
                                    gt[:, :, CAP:2 * CAP], ALU.mult).then_inc(at_r[j], 1)

                def overflow_pick(e):
                    for b in range(NB):
                        d.tensor_scalar(opick[:, b, :], lane[:, :], opos[:, b:b + 1], None,
                                        ALU.is_equal).then_inc(o_pick, 1)
                        d.tensor_scalar(oput[:, b, :], lane[:, :], opos[:, b:b + 1],
                                        gate[:, b, bass.ds(e, 1)], ALU.is_equal, ALU.mult).then_inc(o_pick, 1)

                def overflow_first(i, j):
                    e = i * 2 + j
                    if j or not isinstance(i, int):
                        dve.wait_ge(o_pick, i * 8 + 4 * ((NE + 1) * l + j))
                    elif l:
                        dve.wait_ge(o_pick, 4 * (NE + 1))
                    d.tensor_scalar(opos[:, :].unsqueeze(2), pos[:, :, bass.ds(e, 1)], -float(CAP), None,
                                    ALU.add).then_inc(o_pos, 1)
                    dve.wait_ge(o_pos, i * 2 + ((NE + 1) * l + j + 1))
                    overflow_pick(e)

                def overflow(i, j):
                    e = i * 2 + j
                    n = dve.value_load(tabn[0:1, bass.ds(e, 1)], min_val=0, max_val=ROUNDS)
                    b0 = dve.value_load(tabb[0:1, bass.ds(e, 1)], min_val=0, max_val=2 * NE * ROUNDS)
                    with dve.If(n > 0):
                        with dve.Fori(b0, b0 + n) as g:
                            k = g * 13
                            dve.wait_ge(o_pe, g * 7 + 2)
                            d.tensor_copy(oxT[:, :, :].rearrange("p a b -> p (a b)"), ps[:, 7, :]).then_inc(o_dve, 1)
                            dve.wait_ge(o_act, g * 4 + 3)
                            gt = ps[:, 7, :].rearrange("p (c s) -> p c s", c=4)
                            d.tensor_tensor(osg[:, :, :], osg[:, :, :], gt[:, :, 0:CAP], ALU.mult).then_inc(o_dve, 1)
                            dve.wait_ge(o_dve, k + 3)
                            d.tensor_tensor(oaT.rearrange("p (c s) -> p c s", c=4), osg[:, :, :],
                                            gt[:, :, CAP:2 * CAP], ALU.mult).then_inc(o_dve, 1)
                            dve.wait_ge(o_pe, g * 7 + 5)
                            dve.wait_ge(x_ready, NB * (2 * l + 1))
                            d.tensor_copy(oy[0:CAP, 512:D], ps[CAP:P, 6, :]).then_inc(o_dve, 1)
                            dve.wait_ge(o_pe, g * 7 + 6)
                            d.tensor_copy(oputT[0:CAP, :], ps[0:CAP, 7, 0:S]).then_inc(o_dve, 1)
                            d.tensor_scalar(opos[:, :], opos[:, :], -float(CAP), None, ALU.add).then_inc(o_dve, 1)
                            dve.wait_ge(o_dve, k + 7)
                            for b in range(NB):
                                d.tensor_scalar(opick[:, b, :], lane[:, :], opos[:, b:b + 1], None,
                                                ALU.is_equal).then_inc(o_dve, 1)
                                d.tensor_scalar(oput[:, b, :], lane[:, :], opos[:, b:b + 1],
                                                gate[:, b, bass.ds(e, 1)], ALU.is_equal, ALU.mult).then_inc(o_dve, 1)
                            dve.wait_ge(o_pe, g * 7 + 7)
                            dve.sem_inc(o_dve, 3)
                            dve.wait_ge(o_dve, k + 14)

                tokens_out(9 * l)
                turned_out(9 * l)
                overflow_first(0, 0)
                with dve.Fori(0, PAIRS) as i:
                    q = i + 8 * l
                    G = i + 9 * l
                    overflow(i, 0)
                    overflow_first(i, 1)
                    dve.wait_ge(ga_mm, G + 1)
                    pick_pair(i + 1)
                    put_pair(i)
                    overflow(i, 1)
                    tokens_out(G + 1)
                    overflow_first(i, 2)
                    glu(0, q)
                    turned_out(G + 1)
                    glu(1, q)
                    dve.wait_ge(sc_mm, i + (10 * l + 1))
                    dve.wait_ge(tp_mm, q + 1)
                    d.tensor_copy(putT[:, :], ps[:, 6, 0:S]).then_inc(tp_ev, 1)
                    spent(dve, n0 + 4, i)
                    d.tensor_copy(y[0:CAP, 512:D], ps[CAP:P, 4, :]).then_inc(y_ev[0], 1)
                    spent(dve, n0 + 5, i)
                    d.tensor_copy(y[CAP:P, 512:D], ps[CAP:P, 5, :]).then_inc(y_ev[1], 1)

            for j in (1, 3):
                spent(dve, N_ADA[0][j])
                d.tensor_copy(parts[:, j, :], ps[:, j, :]).then_inc(part_ev[1], 1)
            dve.wait_ge(x_in, 16 * NB)
            streamed(0)
            turned(0)
            dve.wait_ge(small_in, 16 * SMALL)
            for g0 in (0, 4):
                if g0:
                    link(d.tensor_scalar(rows[64:P, g0, :], rows[64:P, g0, :], 1.0, None, ALU.add))
                link(d.tensor_scalar(rows[0:64, g0 + 1, :], rows[0:64, g0 + 1, :], 1.0, None, ALU.add))
                link(d.tensor_scalar(rows[:, g0 + 2, :], rows[:, g0 + 2, :], 1.0, None, ALU.add))
            link(d.tensor_scalar(rows[64:P, 3, :], rows[64:P, 3, :], 1.0, None, ALU.add))
            d.tensor_scalar(normg[:, :], normg[:, :], 1.0 - LAM_INIT, None, ALU.mult).then_inc(normg_r, 1)
            for t in range(2):
                link(d.tensor_tensor(lamt[:, :], lamin[:, 2 * t, :], lamin[:, 2 * t + 1, :], ALU.mult))
                ins = d.tensor_reduce(lam2[:, t:t + 1], lamt[:, :], AX.X, ALU.add)
                if t == 0:
                    link(ins)
                else:
                    ins.then_inc(lam_r, 1)
            for (u, kind, dst) in proj_units(0):
                if u == GATE_UNIT:
                    forget_gate()
                    share(2, 3)
                else:
                    unit_out(u, dst, kind)
                if u in (1, 3, 7):
                    share(1, {1: 0, 3: 2, 7: 3}[u])
                if u == 13:
                    mod_rows(1)
                if u in (13, 15):
                    share(2, {13: 0, 15: 2}[u])
            mod_rows(2)
            for t in range(HF + 5):
                if t < HF:
                    if t >= 4:
                        dve.wait_ge(pt_mm, t - 3)
                    soft(t, maskf, 1.0)
                if 1 <= t <= HF:
                    fox_norm(t - 1)
                if t >= 5 and t % 2:
                    pair = (t - 5) // 2
                    dve.wait_ge(pv_mm, 2 * pair + 2)
                    d.tensor_copy(oT[:, pair, :], ps[:, 4 + pair % 2, 0:S]).then_inc(o_ev, 1)
                if t == 8:
                    dve.wait_ge(mod_mm, SUMS[3] - 1)
                if 2 <= t < 6 or 8 <= t < 12:
                    k = 2 * (t - 2) if t < 6 else 2 * (t - 8)
                    weigh(dve, d, heap, 3, 0 if t < 6 else 2, part3(0), ks=(k, k + 1))
                if t == 18:
                    mod_rows(3)
                if t == 14:
                    mod_rows(4)
            nothing_added()
            dve.wait_ge(gate_mm, 1)
            for m in (1, 2, 3):
                fold_rows(m)
            post_norm(0)
            streamed(1)
            turned(1)
            route(0)
            experts(0)
            post_norm(1)
            streamed(2)
            turned(2)
            us = proj_units(1)
            link(d.memset(kT[:, :, :], 0.0))
            d.memset(ncum[:, 0:1], 0.0).then_inc(f_steps, 1)
            streamed(3)
            for (u, kind, dst) in us[:8]:
                unit_out(u, dst, kind)
                if u - UNITS0 in (1, 3):
                    share(5, {1: 0, 3: 2}[u - UNITS0])
            gained(1)
            share(5, 3)
            for (u, kind, dst) in us[8:12]:
                unit_out(u, dst, kind)
            mod_rows(5)
            turned(3)
            share(6, 0)
            for (u, kind, dst) in us[12:]:
                unit_out(u, dst, kind)
                if u - UNITS0 in (13, 15):
                    share(6, {13: 2, 15: 3}[u - UNITS0])
            mod_rows(6)
            dve.wait_ge(lam_r, 2)
            link(d.scalar_tensor_tensor(out=lam2[:, 0:1], in0=lam2[:, 2:3], scalar=-1.0, in1=lam2[:, 3:4],
                                        op0=ALU.mult, op1=ALU.add))
            link(d.tensor_scalar(lam2[:, 0:1], lam2[:, 0:1], -LAM_INIT, None, ALU.add))
            for t in range(HD + 4):
                if t < HD:
                    slope = -(2.0 ** (-8.0 * (t + 1) / HD))
                    if t >= 2:
                        dve.wait_ge(pt_mm, HF + t - 1)
                    soft(HF + 2 * t, dist, slope)
                    soft(HF + 2 * t + 1, dist, slope)
                if 1 <= t <= HD:
                    diff_norm(t - 1)
                if t >= 4:
                    hd = t - 4
                    dve.wait_ge(o_pow, hd + 1)
                    d.tensor_tensor(h[:, :, hd * P:(hd + 1) * P],
                                    ps[:, 4 + hd % 3, 0:S].rearrange("p (b n) -> p b n", b=NB),
                                    ss[:, hd, 2, :].unsqueeze(2).broadcast_to([P, NB, P]), ALU.mult).then_inc(o_ev, 1)
            for q in range(2):
                dve.wait_ge(ot_mm, 2 * q + 2)
                d.tensor_scalar(oT[:, 4 * q + 2:4 * q + 4, :].rearrange("p a b -> p (a b)"), ps[:, 2 * q + 1, :],
                                normg[:, 0:1], None, ALU.mult).then_inc(ot_ev, 1)
            nothing_added()
            dve.wait_ge(gate_mm, 3)
            fold_rows(4)
            post_norm(2)
            streamed(4)
            turned(4)
            route(1)
            experts(1)
            post_norm(3)
            gained(3)

        @block.tensor
        def _(pe):
            t = nc.tensor

            def mod_product(gi):
                ns = N_ADA[gi]
                for n in ns:
                    landed(pe, n)
                for k in range(KC):
                    for j, n in enumerate(ns):
                        mm = t.matmul(ps[32 * j:32 * j + 32, mod_bank(gi), :], crep[:, k, :], wcols(n)[:, k, :],
                                      start=(k == 0), stop=(k == KC - 1))
                        if k == KC - 1:
                            mm.then_inc(used[slot(n)], 1)

            def mod_sum(gi, quarters=range(4)):
                for j in quarters:
                    spent(pe, N_ADA[gi][j])
                if gi == 1:
                    pe.wait_ge(h_ready, 2)
                elif gi in (2, 3):
                    pe.wait_ge(mod_row, gi - 1)
                elif gi == 6:
                    stream_turned(3)
                for j in quarters:
                    src = part3(j) if gi == 3 else acc[:, j, :]
                    mm = t.matmul(ps[32 * j:32 * j + 32, mod_bank(gi), :], ones[:, 0:32], src, start=True, stop=True)
                mm.then_inc(mod_mm, 1)

            def first_modulation():
                pe.wait_ge(consts, 9)
                pe.wait_ge(bias0, 2)
                (cg, cj), (sg_, sj) = MODS[0]
                bank = {}
                for first, j0 in ((4, cj), (6, sj)):
                    for q in range(2):
                        bank[j0 + q] = first + q
                        t.matmul(ps[:, first + q, :], sel(32 * (j0 + q)), rows[:, 0, :], start=True, stop=False)
                pe.wait_ge(csil, 2)
                for j in range(4):
                    n = N_ADA[0][j]
                    landed(pe, n)
                    for k in range(2):
                        for strip in range(4):
                            mm = t.matmul(ps[32 * strip:32 * strip + 32, j, :], crep[:, 2 * strip + k, :],
                                          wcols(n)[:, 2 * strip + k, :], start=(k == 0), stop=(k == 1))
                    mm.then_inc(used[slot(n)], 1)
                    for q in {0: (), 3: (2, 3)}.get(j, (j - 1,)):
                        pe.wait_ge(part_ev[q % 2], q // 2 + 1)
                        mm = t.matmul(ps[:, bank[q], :], strips[:, :].broadcast_to([P, P]), parts[:, q, :],
                                      start=False, stop=True)
                mm.then_inc(fold_mm, 1)

            def spread(row, bank):
                gi, j = row
                for q in range(2):
                    mm = t.matmul(ps[:, bank + q, :], sel(32 * (j + q)), rows[:, gi, :], start=True, stop=True)
                return mm

            def spread_gate(norm):
                pe.wait_ge(mod_row, ROW["g_" + "af"[norm % 2], norm // 2][0])
                spread(ROW["g_" + "af"[norm % 2], norm // 2], 4).then_inc(gate_mm, 1)

            def spread_fold(m):
                pe.wait_ge(folded, m)
                spread(MODS[m][0], 4)
                spread(MODS[m][1], 6).then_inc(fold_mm, 1)

            def spread_norm(norm):
                name, l = "af"[norm % 2], norm // 2
                spread(ROW["ln_" + name + "_g", l], 4)
                spread(ROW["ln_" + name + "_b", l], 6).then_inc(lnx_mm, 1)

            def turn_stream(m):
                for b in range(NB):
                    pe.wait_ge(h_ready, 2 * m + b + 1)
                    for k in range(KC):
                        o = (k % 4) * P
                        mm = t.transpose(ps[:, turn_bank(m) + 2 * b + k // 4, o:o + P], h[:, b, k * P:(k + 1) * P], ident[:, :])
                    mm.then_inc(ht_mm, 1)

            def stream_turned(m, b=NB - 1):
                for s_ in range(2):
                    pe.wait_ge(ht_ready[s_], NB * m + b + 1)

            def unit_free(u):
                if u >= 4 and u - UNITS0 not in (0, 1, 2, 3):
                    if u - 4 == GATE_UNIT:
                        pe.wait_ge(f_steps, 1)
                    else:
                        pe.wait_ge(pj_ev[u % 2], pj_even(u - 3) if u % 2 == 0 else pj_odd(u - 3))

            def turned_units(u, ns, after={}):
                for piece in ns:
                    landed(pe, piece)
                    for cc in range(4):
                        unit_free(u)
                        for k in range(KC):
                            mm = t.matmul(ps[:, u % 4, 0:S], wcols(piece)[:, k, cc * P:(cc + 1) * P], hT[:, k, :],
                                          start=(k == 0), stop=(k == KC - 1))
                        mm.then_inc(used[slot(piece)] if cc == 3 else pj_mm, 1)
                        if u in after:
                            mod_sum(after[u])
                        u += 1
                return u

            def natural_units(u, ns):
                for piece in ns:
                    landed(pe, piece)
                    for b in range(NB):
                        unit_free(u)
                        for k in range(KC):
                            mm = t.matmul(ps[:, u % 4, :], hT[:, k, b * P:(b + 1) * P], wcols(piece)[:, k, :],
                                          start=(k == 0), stop=(k == KC - 1))
                        mm.then_inc(used[slot(piece)] if b == 1 else pj_mm, 1)
                        u += 1
                return u

            def scores(H, chunk, half, head):
                bank = H % 2
                if H >= 2:
                    pe.wait_ge(mx, 2 * (H - 1))
                if head is not None:
                    t.matmul(ps[:, bank, 0:3 * P], sel(head), ncum[:, :], start=True, stop=True)
                first = head is None
                kk = kT[:, 2 * chunk + half, :]
                t.matmul(ps[:, bank, 0:P], qT[:, chunk, 0:P], kk[:, 0:P], start=first, stop=True,
                         skip_group_check=True)
                t.matmul(ps[:, bank, P:3 * P], qT[:, chunk, P:2 * P], kk, start=first, stop=True,
                         skip_group_check=True).then_inc(s_mm, 1)

            def turn_probs(T, buf, pn_count):
                pe.wait_ge(pn, pn_count)
                if T >= 2:
                    pe.wait_ge(pt_ev, T - 1)
                for q in range(3):
                    mm = t.transpose(ps[:, 2 + T % 2, q * P:(q + 1) * P], lg[:, buf, q * P:(q + 1) * P], ident[:, :])
                mm.then_inc(pt_mm, 1)

            def fox_values(hh):
                pair = hh // 2
                lo = 64 * (hh % 2)
                bank = 4 + pair % 2
                pe.wait_ge(pt_ev, hh + 1)
                if hh % 2 == 0 and pair >= 2:
                    pe.wait_ge(o_ev, pair - 1)
                t.matmul(ps[lo:lo + 64, bank, 0:S], v[:, 0, 64 * hh:64 * hh + 64], pT[:, hh % 2, 0:S],
                         start=True, stop=True)
                t.matmul(ps[lo:lo + 64, bank, P:S], v[:, 1, 64 * hh:64 * hh + 64], pT[:, hh % 2, S:S + P],
                         start=False, stop=True, skip_group_check=True).then_inc(pv_mm, 1)

            def diff_values(hd):
                T = HF + hd
                bank = 4 + hd % 3
                pe.wait_ge(pt_ev, T + 1)
                if hd >= 3:
                    pe.wait_ge(o_ev, HD + hd - 2)
                vv = [v[:, b, hd * P:(hd + 1) * P] for b in range(NB)]
                t.matmul(ps[:, bank, 0:P], pT[:, T % 2, 0:P], vv[0], start=True, stop=True)
                t.matmul(ps[:, bank, P:S], pT[:, T % 2, P:S], vv[0], start=True, stop=False)
                t.matmul(ps[:, bank, P:S], pT[:, T % 2, S:S + P], vv[1], start=False, stop=True).then_inc(pv_mm, 1)

            def out_product(l):
                ns = N_WO[l]
                norm = 2 * l
                spread_gate(norm)
                for n in ns:
                    landed(pe, n)
                for b in range(NB):
                    for s_ in range(2):
                        for k in range(KC):
                            mm = t.matmul(ps[:, 2 * b + s_, :], oT[:, k, b * P:(b + 1) * P], wcols(ns[s_])[:, k, :],
                                          start=(k == 0), stop=(k == KC - 1))
                        if b == 0 and s_ == 1:
                            mm.then_inc(y_mm, 1)
                            pe.wait_ge(g_ev, 2 * (norm + 1))
                            spread_fold((1, None, 4)[norm])
                        if b == 1 and s_ == 0:
                            mm.then_inc(used[slot(ns[0])], 1)
                mm.then_inc(used[slot(ns[1])], 1)

            def route(l):
                m = (1, 4)[l]
                for b in range(NB):
                    stream_turned(m, b)
                    for k in range(KC):
                        mm = t.matmul(ps[:, 0, b * NE:(b + 1) * NE], hT[:, k, b * P:(b + 1) * P], rw[:, k, :],
                                      start=(k == 0), stop=(k == KC - 1))
                mm.then_inc(rt_mm, 1)
                spread_norm(2 * l)
                pe.wait_ge(rt_mask, l + 1)
                m0, m1 = rt[:, 7, 0:NE], rt[:, 7, NE:2 * NE]
                ra, rb_, tt = (ps[:, 0, o:o + NE] for o in (NB * NE, (NB + 1) * NE, 2 * NB * NE))
                t.matmul(ra, before[:, :], m0, start=True, stop=True)
                t.matmul(rb_, ones[:, :], m0, start=True, stop=False)
                t.matmul(rb_, before[:, :], m1, start=False, stop=True)
                t.matmul(tt, ones[:, :], m0, start=True, stop=False)
                t.matmul(tt, ones[:, :], m1, start=False, stop=True).then_inc(rt_mm, 1)
                pe.wait_ge(ln_ev, 4 * (l + 1))
                spread_gate(2 * l + 1)

            def experts(l):
                n0 = N_MOE[l]

                def gather(G):
                    pe.wait_ge(picked, (G + 1) * 4)
                    for q in range(2):
                        for b in range(NB):
                            mm = t.matmul(ps[:, 6 + q, :], pick[:, b, :], h[:, b, q * 512:q * 512 + 512],
                                          start=(b == 0), stop=(b == NB - 1))
                    mm.then_inc(ga_mm, 1)

                def turn_tokens(G):
                    pe.wait_ge(xg_ev, (G + 1) * 2)
                    for k in range(KC):
                        mm = t.transpose(ps[:, 6 + k // 4, (k % 4) * P:(k % 4 + 1) * P], xg[:, k * P:(k + 1) * P], ident[:, :])
                    mm.then_inc(tx_mm, 1)

                def gate_up(j, i, lhs, bank, ks, last):
                    ng, nu = n0 + 2 * j, n0 + 2 * j + 1
                    for k in ks:
                        mg = t.matmul(ps[0:CAP, bank, :], lhs(k), wcols(ng)[:, k, :], start=(k == 0), stop=(k == KC - 1))
                        mu = t.matmul(ps[CAP:P, bank, :], lhs(k), wcols(nu)[:, k, :], start=(k == 0), stop=(k == KC - 1))
                    if last:
                        mg.then_inc(used[slot(ng)], 1)
                        mu.then_inc(used[slot(nu)], 1)
                    return mu

                def down(j, lhs, bank):
                    n = n0 + 4 + j
                    for f in range(4):
                        t.matmul(ps[0:CAP, bank, :], lhs(f), wdown(n)[:, f, 0:512], start=(f == 0), stop=(f == 3))
                        mm = t.matmul(ps[CAP:P, bank, :], lhs(f), wdown(n)[:, f, 512:D], start=(f == 0), stop=(f == 3))
                    return mm

                def add_back(lhs, yy, blocks=range(NB)):
                    for b in blocks:
                        for q in range(2):
                            mm = t.matmul(ps[:, 2 * b + q, :], lhs(b), yy(q), start=False, stop=True,
                                          skip_group_check=True)
                    return mm

                def overflow(i, j):
                    n = pe.value_load(tabn[0:1, bass.ds(i * 2 + j, 1)], min_val=0, max_val=ROUNDS)
                    b = pe.value_load(tabb[0:1, bass.ds(i * 2 + j, 1)], min_val=0, max_val=2 * NE * ROUNDS)
                    with pe.If(n > 0):
                        with pe.Fori(b, b + n) as g:
                            k = g * 13
                            pe.wait_ge(o_pick, i * 8 + 4 * ((NE + 1) * l + j + 1))
                            pe.wait_ge(o_dve, k + 1)
                            for bb in range(NB):
                                for q in range(2):
                                    mm = t.matmul(ps[q * CAP:(q + 1) * CAP, 6, :], opick[:, bb, :],
                                                  h[:, bb, q * 512:q * 512 + 512], start=(bb == 0), stop=(bb == 1))
                            mm.then_inc(o_pe, 1)
                            pe.wait_ge(o_act, g * 4 + 1)
                            for q in range(4):
                                mm = t.transpose(ps[:, 7, q * P:(q + 1) * P], ox[:, q * P:(q + 1) * P], ident[:, :])
                            mm.then_inc(o_pe, 1)
                            pe.wait_ge(o_dve, k + 2)
                            landed(pe, n0 + 2 * j, i)
                            landed(pe, n0 + 2 * j + 1, i)
                            gate_up(j, i, lambda kk: oxT[:, kk % 4, (kk // 4) * CAP:(kk // 4 + 1) * CAP],
                                    6, range(KC), False).then_inc(o_pe, 1)
                            pe.wait_ge(o_act, g * 4 + 2)
                            for q in range(4):
                                mm = t.transpose(ps[:, 7, q * P:(q + 1) * P], ox[:, q * P:(q + 1) * P], ident[:, :])
                            mm.then_inc(o_pe, 1)
                            pe.wait_ge(o_dve, k + 4)
                            landed(pe, n0 + 4 + j, i)
                            down(j, lambda f: oaT[:, f * CAP:(f + 1) * CAP], 6).then_inc(o_pe, 1)
                            for bb in range(NB):
                                mm = t.transpose(ps[0:CAP, 7, bb * P:(bb + 1) * P], oput[:, bb, :], ident[:, :])
                            mm.then_inc(o_pe, 1)
                            pe.wait_ge(o_act, g * 4 + 4)
                            pe.wait_ge(o_dve, k + 6)
                            add_back(lambda bb: oputT[0:CAP, bb * P:(bb + 1) * P],
                                     lambda q: oy[0:CAP, q * 512:q * 512 + 512]).then_inc(o_pe, 1)

                gather(9 * l)
                turn_tokens(9 * l)
                pe.wait_ge(tab, l + 1)
                for bank in range(4):
                    t.matmul(ps[:, bank, :], ones[:, :], y[:, 0:512], start=True, stop=True)
                pe.wait_ge(g_ev, 2 * (2 * l + 2))
                with pe.Fori(0, PAIRS) as i:
                    q = i + 8 * l
                    G = i + 9 * l
                    pe.wait_ge(xt_ev, (G + 1) * 2)
                    pe.wait_ge(tp_ev, q + 1)
                    overflow(i, 0)
                    pe.wait_ge(y_ev[0], (q + 1) * 2)
                    landed(pe, n0, i)
                    landed(pe, n0 + 1, i)
                    gate_up(0, i, lambda k: xT[:, k, 0:CAP], 4, range(KC), True)
                    pe.wait_ge(y_ev[1], (q + 1) * 2)
                    overflow(i, 1)
                    gather(G + 1)
                    landed(pe, n0 + 2, i)
                    landed(pe, n0 + 3, i)
                    gate_up(1, i, lambda k: xT[:, k, CAP:P], 5, range(4), False)
                    pe.wait_ge(gu_ev[0], q + 1)
                    for f in range(4):
                        mm = t.transpose(ps[:, 4, f * P:(f + 1) * P], gu[:, 0, f * P:(f + 1) * P], ident[:, :])
                    mm.then_inc(tg_mm[0], 1)
                    gate_up(1, i, lambda k: xT[:, k, CAP:P], 5, range(4, KC), True)
                    turn_tokens(G + 1)
                    add_back(lambda b: putT[:, b * P:(b + 1) * P],
                             lambda qq: y[:, qq * 512:qq * 512 + 512]).then_inc(sc_mm, 1)
                    pe.wait_ge(gu_ev[1], q + 1)
                    for f in range(4):
                        mm = t.transpose(ps[:, 5, f * P:(f + 1) * P], gu[:, 1, f * P:(f + 1) * P], ident[:, :])
                    mm.then_inc(tg_mm[1], 1)
                    pe.wait_ge(at_r[0], q + 1)
                    landed(pe, n0 + 4, i)
                    down(0, lambda f: aT[:, 0, f * CAP:(f + 1) * CAP], 4).then_inc(used[slot(n0 + 4)], 1)
                    pe.wait_ge(xt_ev, (G + 2) * 2)
                    pe.wait_ge(putted, (q + 1) * 4)
                    for b in range(NB):
                        mm = t.transpose(ps[:, 6, b * P:(b + 1) * P], put[:, b, :], ident[:, :])
                    mm.then_inc(tp_mm, 1)
                    pe.wait_ge(at_r[1], q + 1)
                    landed(pe, n0 + 5, i)
                    down(1, lambda f: aT[:, 1, f * CAP:(f + 1) * CAP], 5).then_inc(used[slot(n0 + 5)], 1)
                pe.wait_ge(tp_ev, 8 * (l + 1) + 1)
                pe.wait_ge(y_ev[0], (8 * (l + 1) + 1) * 2)
                pe.wait_ge(y_ev[1], (8 * (l + 1) + 1) * 2)
                for b in range(NB):
                    add_back(lambda b: putT[:, b * P:(b + 1) * P],
                             lambda qq: y[:, qq * 512:qq * 512 + 512], (b,)).then_inc(sc_mm, 1)

            first_modulation()
            turn_stream(0)
            stream_turned(0)
            u = turned_units(0, N_FOXQK, {12: 1})
            unit_free(u)
            for k in range(KC):
                mm = t.matmul(ps[0:HF, 0, 0:S], wf[:, k, :], hT[:, k, :], start=(k == 0), stop=(k == KC - 1))
            mm.then_inc(pj_mm, 1)
            natural_units(u + 1, N_FOXV)
            mod_sum(2)
            pe.wait_ge(pj_ev[0], pj_even(UNITS0))
            pe.wait_ge(pj_ev[1], pj_odd(UNITS0))
            pe.wait_ge(f_steps, 1)
            for hh in range(HF + 3):
                if hh < HF:
                    scores(hh, hh // 2, hh % 2, hh)
                if 2 <= hh < HF + 2:
                    turn_probs(hh - 2, (hh - 2) % 4, 2 * (hh - 1))
                if hh >= 3:
                    fox_values(hh - 3)
                if hh == 7:
                    mod_sum(3, (0, 1))
                if hh == 11:
                    mod_product(4)
                if hh == 15:
                    mod_sum(3, (2, 3))
            pe.wait_ge(o_ev, HD)
            pe.wait_ge(pt_ev, HF)
            out_product(0)
            turn_stream(1)
            route(0)
            experts(0)
            spread_fold(2)
            turn_stream(2)
            spread_fold(3)
            stream_turned(2)
            pe.wait_ge(f_steps, 2)
            u = turned_units(UNITS0, N_KVK)
            pe.wait_ge(h_ready, 2 * 4)
            spread_norm(1)
            u = natural_units(u, N_KVV)
            pe.wait_ge(x_ready, NB * 2)
            mod_sum(5)
            pe.wait_ge(mod_row, 5)
            turn_stream(3)
            stream_turned(3)
            turned_units(u, N_WQ)
            mod_sum(6)
            pe.wait_ge(pj_ev[0], pj_even(UNITS0 + 20))
            pe.wait_ge(pj_ev[1], pj_odd(UNITS0 + 20))
            for hd in range(HD + 3):
                if hd < HD:
                    scores(HF + 2 * hd, hd, 0, None)
                    scores(HF + 2 * hd + 1, hd, 1, None)
                if 2 <= hd < HD + 2:
                    turn_probs(HF + hd - 2, 2 * (hd % 2), 2 * HF + 2 * (hd - 1))
                if hd >= 3:
                    diff_values(hd - 3)
            pe.wait_ge(o_ev, HD + HD)
            pe.wait_ge(pt_ev, HF + HD)
            for k in range(KC):
                for b in range(NB):
                    o = (k % 2) * S + b * P
                    mm = t.transpose(ps[:, k // 2, o:o + P], h[:, b, k * P:(k + 1) * P], ident[:, :])
                if k % 2:
                    mm.then_inc(ot_mm, 1)
            pe.wait_ge(ot_ev, 4)
            out_product(1)
            turn_stream(4)
            route(1)
            experts(1)
            spread_norm(3)


_INS = ["x", "c", "ada_w", "ada_b", "ln_attn_g", "ln_attn_b", "ln_ffn_g", "ln_ffn_b", "fox_w_in", "fox_b_f", "fox_w_o",
        "kv_ada_w", "kv_ada_b", "kv_w", "diff_w_q", "diff_lambda", "diff_norm_g", "diff_w_o",
        "router_w", "router_b", "moe_w_gate", "moe_w_up", "moe_w_down"]
_OUTS = [((1, 256, 1024), "float32")]


def kernel(**inputs):
    import numpy as _np
    import concourse.bacc as _bacc
    from concourse import mybir as _mybir
    from concourse.bass_utils import run_bass_kernel_spmd as _run

    nc = _bacc.Bacc("TRN2", target_bir_lowering=False, num_devices=1)
    arrays, args = {}, []
    for name in _INS:
        a = _np.ascontiguousarray(inputs[name])
        arrays[f"in_{name}_dram"] = a
        args.append(nc.dram_tensor(f"in_{name}_dram", a.shape, _mybir.dt.from_np(a.dtype), kind="ExternalInput").ap())
    for i, (shape, dtype) in enumerate(_OUTS):
        dt = _mybir.dt.from_np(_np.dtype(dtype))
        args.append(nc.dram_tensor(f"out_{i}_dram", shape, dt, kind="ExternalOutput").ap())
    build(nc, *args)
    r = _run(nc, [arrays], core_ids=[0])
    return r.results[0]["out_0_dram"]
```
